# Optimizing a Trainium2 kernel written in Bass

```python
import math
import jax
import jax.numpy as jnp
from jax import lax
import numpy as np

D_MODEL = 1024
BATCH = 1
SEQ = 256
DEPTH = 2
DEC_BATCH = 8
DEC_SEQ = 1
PAST_LEN = 1024
PAGE_SIZE = 128

N_A_LAYERS = DEPTH // 2
N_B_LAYERS = DEPTH - N_A_LAYERS
N_DENSE = (DEPTH + 1) // 2
N_MOE = DEPTH // 2
SSM_GROUP = 16
SSM_GROUPS = D_MODEL // SSM_GROUP
SSM_STATE = 64
N_HEADS = 16
N_KV_HEADS = 4
HEAD_DIM = 64
Q_PER_KV = N_HEADS // N_KV_HEADS
KV_WIDTH = N_KV_HEADS * HEAD_DIM
WINDOW = 128
NUM_BUCKETS = 32
MAX_DISTANCE = 128
ATTN_SCALE = 1.0 / math.sqrt(HEAD_DIM)
NEG_INF = -1e30
D_FF = 2816
N_EXPERTS = 8
TOP_K = 2
D_FF_EXPERT = 3584
EPS = 1e-6

kernel_name = 'yoco_s5_swa_sink_step'

def rmsnorm(x, g):
    xf = x.astype(jnp.float32)
    y = xf * lax.rsqrt(jnp.mean(xf * xf, axis=-1, keepdims=True) + EPS)
    return (y * g.astype(jnp.float32)).astype(x.dtype)

def swiglu(h, w_gu, w_down):
    a, b = jnp.split(h @ w_gu, 2, axis=-1)
    return (jax.nn.silu(a) * b) @ w_down

def moe_swiglu(h, w_router, w_gu, w_down):
    logits = jnp.einsum('btd,de->bte', h, w_router, preferred_element_type=jnp.float32)
    top_v, top_i = lax.top_k(logits, TOP_K)
    gates = jax.nn.softmax(top_v, axis=-1)
    comb = jnp.einsum('btk,btke->bte', gates, jax.nn.one_hot(top_i, N_EXPERTS, dtype=jnp.float32))
    out = jnp.zeros(h.shape, jnp.float32)
    for e in range(N_EXPERTS):
        out = out + comb[..., e:e + 1] * swiglu(h, w_gu[e], w_down[e]).astype(jnp.float32)
    return out.astype(h.dtype)

def _ssm_combine(left, right):
    a_l, b_l = left
    a_r, b_r = right
    return a_r * a_l, a_r * b_l + b_r

def s5_mixer(u, h0, a_re, a_im, log_dt, b_re, b_im, c_re, c_im, d_skip, w_glu):
    bsz, t_len, _ = u.shape
    lam = lax.complex(a_re.astype(jnp.float32), a_im.astype(jnp.float32))
    dt = jnp.exp(log_dt.astype(jnp.float32))[:, None]
    lam_bar = jnp.exp(lam * dt)
    b_mat = lax.complex(b_re.astype(jnp.float32), b_im.astype(jnp.float32))
    b_bar = ((lam_bar - 1.0) / lam)[..., None] * b_mat
    uf = u.astype(jnp.float32).reshape(bsz, t_len, SSM_GROUPS, SSM_GROUP)
    bu = lax.complex(jnp.einsum('btgh,gph->btgp', uf, jnp.real(b_bar)),
                     jnp.einsum('btgh,gph->btgp', uf, jnp.imag(b_bar)))
    if h0 is not None:
        bu = bu.at[:, 0].add(lam_bar * h0)
    a = jnp.broadcast_to(lam_bar, (1, t_len, SSM_GROUPS, SSM_STATE))
    _, h = lax.associative_scan(_ssm_combine, (a, bu), axis=1)
    y = (jnp.einsum('btgp,ghp->btgh', jnp.real(h), c_re.astype(jnp.float32))
         - jnp.einsum('btgp,ghp->btgh', jnp.imag(h), c_im.astype(jnp.float32)))
    y = y.reshape(bsz, t_len, D_MODEL) + d_skip.astype(jnp.float32) * u.astype(jnp.float32)
    z = jax.nn.gelu(y).astype(u.dtype)
    gl = z @ w_glu
    out = gl[..., :D_MODEL] * jax.nn.sigmoid(gl[..., D_MODEL:])
    return out, h[:, -1]

def t5_bucket(dist):
    max_exact = NUM_BUCKETS // 2
    d = jnp.maximum(dist, 0)
    large = max_exact + (jnp.log(jnp.maximum(d, 1).astype(jnp.float32) / max_exact)
                         / math.log(MAX_DISTANCE / max_exact) * (NUM_BUCKETS - max_exact)).astype(jnp.int32)
    large = jnp.minimum(large, NUM_BUCKETS - 1)
    return jnp.where(d < max_exact, d, large)

def sink_attention(q, k, v, dist, valid, sinks, rel_bias):
    n_q, n_k = dist.shape
    bias = rel_bias.astype(jnp.float32)[t5_bucket(dist)]
    bias = jnp.transpose(bias, (2, 0, 1)).reshape(N_KV_HEADS, Q_PER_KV, n_q, n_k)
    s = jnp.einsum('nqgrd,nkgd->ngrqk', q, k, preferred_element_type=jnp.float32) * ATTN_SCALE + bias
    s = jnp.where(valid, s, NEG_INF)
    sink = sinks.astype(jnp.float32).reshape(N_KV_HEADS, Q_PER_KV)[None, :, :, None, None]
    m = jnp.maximum(jnp.max(s, axis=-1, keepdims=True), sink)
    p = jnp.exp(s - m)
    probs = p / (jnp.sum(p, axis=-1, keepdims=True) + jnp.exp(sink - m))
    return jnp.einsum('ngrqk,nkgd->nqgrd', probs.astype(v.dtype), v)

def window_attn_prompt(q, k, v, sinks, rel_bias):
    bsz, t_len = q.shape[:2]
    nb = t_len // WINDOW
    qb = q.reshape(bsz * nb, WINDOW, N_KV_HEADS, Q_PER_KV, HEAD_DIM)

    def band(z):
        zb = z.reshape(bsz, nb, WINDOW, N_KV_HEADS, HEAD_DIM)
        zprev = jnp.concatenate([jnp.zeros_like(zb[:, :1]), zb[:, :-1]], axis=1)
        return jnp.concatenate([zprev, zb], axis=2).reshape(bsz * nb, 2 * WINDOW, N_KV_HEADS, HEAD_DIM)

    qi = jnp.arange(WINDOW)[:, None]
    kj = jnp.arange(2 * WINDOW)[None, :]
    dist = qi + WINDOW - kj
    in_band = (dist >= 0) & (dist < WINDOW)
    key_ok = (jnp.arange(nb)[:, None] > 0) | (jnp.arange(2 * WINDOW)[None, :] >= WINDOW)
    valid = in_band[None] & key_ok[:, None, :]
    valid = jnp.broadcast_to(valid[None], (bsz, nb, WINDOW, 2 * WINDOW)).reshape(bsz * nb, 1, 1, WINDOW, 2 * WINDOW)
    o = sink_attention(qb, band(k), band(v), dist, valid, sinks, rel_bias)
    return o.reshape(bsz, t_len, N_HEADS * HEAD_DIM)

def window_attn_sample(q, k_all, v_all, sinks, rel_bias):
    bsz, s_len = q.shape[:2]
    qi = jnp.arange(s_len)[:, None]
    kj = jnp.arange(WINDOW + s_len)[None, :]
    dist = qi + WINDOW - kj
    valid = ((dist >= 0) & (dist < WINDOW))[None, None, None]
    o = sink_attention(q, k_all, v_all, dist, valid, sinks, rel_bias)
    return o.reshape(bsz, s_len, N_HEADS * HEAD_DIM)

def run_trunk(x, ssm_h0, k_win, v_win, g_mix, g_ffn, g_kv, g_final,
              ssm_a_re, ssm_a_im, ssm_log_dt, ssm_b_re, ssm_b_im, ssm_c_re, ssm_c_im, ssm_d, w_glu,
              w_kv, w_q, w_o, attn_sinks, rel_bias,
              w_ffn_gate_up, w_ffn_down, w_router, w_exp_gate_up, w_exp_down):
    bsz, t_len, _ = x.shape
    ssm_states = []
    k_all = v_all = new_k_win = new_v_win = None
    for l in range(DEPTH):
        if l < N_A_LAYERS:
            h0 = None if ssm_h0 is None else ssm_h0[l]
            y, h_last = s5_mixer(rmsnorm(x, g_mix[l]), h0, ssm_a_re[l], ssm_a_im[l], ssm_log_dt[l],
                                 ssm_b_re[l], ssm_b_im[l], ssm_c_re[l], ssm_c_im[l], ssm_d[l], w_glu[l])
            ssm_states.append(h_last)
            x = x + y
        else:
            if k_all is None:
                kv = rmsnorm(x, g_kv) @ w_kv
                k_new = kv[..., :KV_WIDTH].reshape(bsz, t_len, N_KV_HEADS, HEAD_DIM)
                v_new = kv[..., KV_WIDTH:].reshape(bsz, t_len, N_KV_HEADS, HEAD_DIM)
                if k_win is None:
                    k_all, v_all = k_new, v_new
                else:
                    k_all = jnp.concatenate([k_win, k_new], axis=1)
                    v_all = jnp.concatenate([v_win, v_new], axis=1)
                new_k_win = k_all[:, -WINDOW:]
                new_v_win = v_all[:, -WINDOW:]
            j = l - N_A_LAYERS
            q = (rmsnorm(x, g_mix[l]) @ w_q[j]).reshape(bsz, t_len, N_KV_HEADS, Q_PER_KV, HEAD_DIM)
            if k_win is None:
                o = window_attn_prompt(q, k_all, v_all, attn_sinks[j], rel_bias)
            else:
                o = window_attn_sample(q, k_all, v_all, attn_sinks[j], rel_bias)
            x = x + o @ w_o[j]
        h = rmsnorm(x, g_ffn[l])
        if l % 2 == 0:
            x = x + swiglu(h, w_ffn_gate_up[l // 2], w_ffn_down[l // 2])
        else:
            x = x + moe_swiglu(h, w_router[l // 2], w_exp_gate_up[l // 2], w_exp_down[l // 2])
    return rmsnorm(x, g_final), jnp.stack(ssm_states, axis=0), new_k_win, new_v_win

def setup_inputs(seed: int = 0) -> dict:
    key = jax.random.key(seed)
    ks = iter(jax.random.split(key, 40))

    def nrm(shape, scale):
        return jax.random.normal(next(ks), shape, jnp.float32) * scale

    d = D_MODEL
    a_im_base = jnp.pi * jnp.arange(SSM_STATE, dtype=jnp.float32)[None, None, :]
    return {
        'x_prompt': nrm((BATCH, SEQ, d), 1.0),
        'x_sample': nrm((DEC_BATCH, DEC_SEQ, d), 1.0),
        'state_ssm_re': nrm((N_A_LAYERS, DEC_BATCH, SSM_GROUPS, SSM_STATE), 0.1),
        'state_ssm_im': nrm((N_A_LAYERS, DEC_BATCH, SSM_GROUPS, SSM_STATE), 0.1),
        'cache_k_win': nrm((DEC_BATCH, WINDOW, N_KV_HEADS, HEAD_DIM), 1.0),
        'cache_v_win': nrm((DEC_BATCH, WINDOW, N_KV_HEADS, HEAD_DIM), 1.0),
        'g_mix': 1.0 + nrm((DEPTH, d), 0.05),
        'g_ffn': 1.0 + nrm((DEPTH, d), 0.05),
        'g_kv': 1.0 + nrm((d,), 0.05),
        'g_final': 1.0 + nrm((d,), 0.05),
        'ssm_a_re': -0.5 + nrm((N_A_LAYERS, SSM_GROUPS, SSM_STATE), 0.01),
        'ssm_a_im': a_im_base + nrm((N_A_LAYERS, SSM_GROUPS, SSM_STATE), 0.01),
        'ssm_log_dt': jax.random.uniform(next(ks), (N_A_LAYERS, SSM_GROUPS), jnp.float32,
                                         minval=math.log(1e-3), maxval=math.log(1e-1)),
        'ssm_b_re': nrm((N_A_LAYERS, SSM_GROUPS, SSM_STATE, SSM_GROUP), (2 * SSM_GROUP) ** -0.5),
        'ssm_b_im': nrm((N_A_LAYERS, SSM_GROUPS, SSM_STATE, SSM_GROUP), (2 * SSM_GROUP) ** -0.5),
        'ssm_c_re': nrm((N_A_LAYERS, SSM_GROUPS, SSM_GROUP, SSM_STATE), 0.3),
        'ssm_c_im': nrm((N_A_LAYERS, SSM_GROUPS, SSM_GROUP, SSM_STATE), 0.3),
        'ssm_d': 1.0 + nrm((N_A_LAYERS, d), 0.1),
        'w_glu': nrm((N_A_LAYERS, d, 2 * d), d ** -0.5),
        'w_kv': nrm((d, 2 * KV_WIDTH), d ** -0.5),
        'w_q': nrm((N_B_LAYERS, d, N_HEADS * HEAD_DIM), d ** -0.5),
        'w_o': nrm((N_B_LAYERS, N_HEADS * HEAD_DIM, d), (N_HEADS * HEAD_DIM) ** -0.5),
        'attn_sinks': nrm((N_B_LAYERS, N_HEADS), 1.0),
        'rel_bias': nrm((NUM_BUCKETS, N_HEADS), 0.5),
        'w_ffn_gate_up': nrm((N_DENSE, d, 2 * D_FF), d ** -0.5),
        'w_ffn_down': nrm((N_DENSE, D_FF, d), D_FF ** -0.5),
        'w_router': nrm((N_MOE, d, N_EXPERTS), d ** -0.5),
        'w_exp_gate_up': nrm((N_MOE, N_EXPERTS, d, 2 * D_FF_EXPERT), d ** -0.5),
        'w_exp_down': nrm((N_MOE, N_EXPERTS, D_FF_EXPERT, d), D_FF_EXPERT ** -0.5),
    }

def reference(x_prompt, x_sample, state_ssm_re, state_ssm_im, cache_k_win, cache_v_win,
              g_mix, g_ffn, g_kv, g_final,
              ssm_a_re, ssm_a_im, ssm_log_dt, ssm_b_re, ssm_b_im, ssm_c_re, ssm_c_im, ssm_d, w_glu,
              w_kv, w_q, w_o, attn_sinks, rel_bias,
              w_ffn_gate_up, w_ffn_down, w_router, w_exp_gate_up, w_exp_down):
    weights = (g_mix, g_ffn, g_kv, g_final,
               ssm_a_re, ssm_a_im, ssm_log_dt, ssm_b_re, ssm_b_im, ssm_c_re, ssm_c_im, ssm_d, w_glu,
               w_kv, w_q, w_o, attn_sinks, rel_bias,
               w_ffn_gate_up, w_ffn_down, w_router, w_exp_gate_up, w_exp_down)
    y_prompt, h_p, k_win_p, v_win_p = run_trunk(x_prompt, None, None, None, *weights)
    h0 = lax.complex(state_ssm_re.astype(jnp.float32), state_ssm_im.astype(jnp.float32))
    y_sample, h_s, k_win_s, v_win_s = run_trunk(x_sample, h0, cache_k_win, cache_v_win, *weights)
    return (y_prompt, y_sample, jnp.real(h_p), jnp.imag(h_p), k_win_p, v_win_p,
            jnp.real(h_s), jnp.imag(h_s), k_win_s, v_win_s)


_drawn_inputs = setup_inputs


def setup_inputs(seed=0):
    import zlib

    import numpy as np

    out = dict(_drawn_inputs(seed))
    spreads = {}
    factors = {}
    for name, (base, spread) in spreads.items():
        noise = np.random.default_rng([zlib.crc32(name.encode()), seed]).standard_normal(out[name].shape)
        drawn = base * np.exp(spread * noise) if base else spread * noise
        out[name] = jnp.asarray(drawn.astype(out[name].dtype))
    for name, factor in factors.items():
        out[name] = (out[name] * factor).astype(out[name].dtype)
    return out
```

```python
from contextlib import ExitStack
import math

import numpy as np
import concourse.bass as bass
from concourse import mybir

F32 = mybir.dt.float32
I32 = mybir.dt.int32
ALU = mybir.AluOpType
ACT = mybir.ActivationFunctionType
AX_X = mybir.AxisListType.X

P = 128
D = 1024
KC = D // P
TP, TS = 256, 8
NT = TP + TS
G, H, S = 64, 16, 64
L = 8
NB = TP // L
UC = NB + TS
SMID = 4
GH = G // 2
CH = KC // 2
G8 = P // H
NH, NKV, HD, R = 16, 4, 64, 4
W = 128
NBUCK = 32
SCALE = 1.0 / math.sqrt(HD)
NEG = -1e30
DFF = 2816
E, DFE = 8, 3584
EPS = 1e-6
TILE = 2048
NF = DFF // P
GLU0, GU0, DN0, KV0, Q0, O0, NDENSE = 0, 8, 30, 41, 43, 47, 51
JE, NGU, NDE = DFE // 512, 28, 14
NE = NGU + NDE
RING = 6
EARLY = 3
BANK = 512
TWO_PI_HI = 6.28125
TWO_PI_LO = 2 * math.pi - TWO_PI_HI
MAGIC = 1.5 * 2.0 ** 23
PI_IN = 3.1415925
HEADS = [(2 * gp + b) * R + r for gp in range(2) for r in range(R) for b in range(2)]
G_MIX0, G_MIX1, G_FFN0, G_FFN1, G_KV, G_FIN, SSM_D = range(7)


def build(nc, xT, vecs, wd, we, wr, a_re, a_im, log_dt, bq, bx, cq, cx, h0q, h0x,
          kcT, vc, sinks, relb, onehot,
          yT, hp_out, hs_out, kp_out, vp_out, ks_out, vs_out):
    with ExitStack() as ctx:
        cur = [ctx]

        def sb(name, shape, dt=F32):
            return cur[0].enter_context(nc.sbuf_tensor(name, shape, dt))

        sems = {}

        def sem(name):
            if name not in sems:
                sems[name] = ctx.enter_context(nc.semaphore(name))
            return sems[name]

        ps = ctx.enter_context(nc.psum_tensor("ps", [P, 8, BANK], F32))
        bias_dram = nc.dram_tensor("bias_rows", (NH, P, 384), F32).ap()

        X = sb("X", [P, KC, NT])
        XN = sb("XN", [P, KC, NT])
        TMP = sb("TMP", [P, KC, NT])
        rstd = sb("rstd", [P, NT])
        root = sb("root", [P, NT])
        vec = sb("vec", [P, 7, KC])
        ones = sb("ones", [P, P])
        ident = sb("ident", [P, P])
        epsb = sb("epsb", [P, 1])
        halfpi = sb("halfpi", [P, 1])
        raw = [sb(f"raw{i}", [P, TILE]) for i in range(EARLY)]

        ssm = ExitStack()
        cur[0] = ssm
        swp = sb("swp", [P, P])
        sel = sb("sel", [P, 8, 240])
        tmask = sb("tmask", [P, P])
        sgn = sb("sgn", [P, 1])
        nsgn = sb("nsgn", [P, 1])
        kramp = sb("kramp", [P, 9])
        jramp = sb("jramp", [P, NB])
        are, aim, dtt = sb("are", [P, G]), sb("aim", [P, G]), sb("dtt", [P, G])
        BQ, BX, CQ, CX = (sb(n, [P, GH, H]) for n in ("BQ", "BX", "CQ", "CX"))
        H0Q, H0X = sb("H0Q", [P, G, TS]), sb("H0X", [P, G, TS])
        q = [sb(f"q{i}", [P, G]) for i in range(14)]
        MT = sb("MT", [P, 9, G])
        T9 = [sb(f"t9{i}", [P, 9, G]) for i in range(2)]
        ER, EI = sb("ER", [P, 9, G]), sb("EI", [P, 9, G])
        TA, TB, TC = (sb(n, [P, GH, NB]) for n in ("TA", "TB", "TC"))
        COS, SS = sb("COS", [P, GH, NB]), sb("SS", [P, GH, NB])
        AM, CM, TM = sb("AM", [P, GH, P]), sb("CM", [P, GH, P]), sb("TM", [P, GH, P])
        PT = sb("PT", [P, GH, H])
        CT = sb("CT", [P, GH, H])
        AT = sb("AT", [P, 8, 192])
        U = sb("U", [P, GH, UC])
        WV = sb("WV", [P, 1 + GH * NB])
        R8 = sb("R8", [P, GH, NB])
        SV = sb("SV", [P, GH, NB])
        VS = sb("VS", [P, GH, TS])
        HM = sb("HM", [P, GH, UC])
        GL = sb("GL", [P, GH])
        HP = sb("HP", [P, G])
        HS = sb("HS", [P, G, TS])
        Y = sb("Y", [P, G, UC])
        ssm.close()

        cur[0] = ctx
        raw += [sb(f"raw{i}", [P, TILE]) for i in range(EARLY, RING)]
        WR = sb("WR", [P, KC, E])
        tri = sb("tri", [P, P])
        slot = sb("slot", [P, 3, P])
        LG = sb("LG", [P, 3, E])
        dz = sb("dz", [P, 3, E])
        attn = ExitStack()
        cur[0] = attn
        FA = sb("FA", [P, NF, NT])
        SG = sb("SG", [P, 2, NT])
        KT = sb("KT", [P, 2, NT])
        QT = sb("QT", [P, KC, NT])
        OT = sb("OT", [P, KC, NT])
        VT = sb("VT", [P, 3, NKV * HD])
        BIAS = sb("BIAS", [P, NH, 2 * W])
        BSM = sb("BSM", [P, W])
        relx = sb("relx", [NBUCK + 1, NH])
        oneh = sb("oneh", [NBUCK + 1, 384])
        brow = sb("brow", [NH, 384])
        SINK = sb("SINK", [P, NH])
        SINKC = sb("SINKC", [P, 1])
        KCT = sb("KCT", [P, TS, 2, W])
        VC = sb("VC", [P, TS, NKV * HD])
        SC = sb("SC", [P, 2, 384])
        mx = sb("mx", [P, 2, 2])
        nm = sb("nm", [P, 2, 2])
        sm = sb("sm", [P, 2, 2])
        es = sb("es", [P, 2, 2])
        rd = sb("rd", [P, 2, 2])
        PTT = sb("PTT", [P, 2, 384])
        STS = sb("STS", [P, P])
        attn.close()
        cur[0] = ctx
        r1, r2, r3, r4 = (sb(f"r{i}", [P, 3, E]) for i in range(1, 5))
        top = sb("top", [P, 3, 8])
        v1 = sb("v1", [P, 3])
        SELM = sb("SELM", [P, 3, E])
        GATE = sb("GATE", [P, 3, E])
        POS = sb("POS", [P, 3, E])
        cnt = sb("cnt", [1, 2 * E])
        run = sb("run", [1, 2 * E + 1])
        plan = sb("plan", [1, 4 * E + 1], I32)
        HT = sb("HT", [P, 3, D])
        DSP = sb("DSP", [P, 2, 3, P])
        DG = sb("DG", [P, 3, P])
        XE = sb("XE", [P, 2, KC, P])
        GS = sb("GS", [P, 2, NT])
        SIL = sb("SIL", [P, 2, BANK])
        AC = sb("AC", [P, 2, BANK])
        ACT_T = sb("ACT_T", [P, 2, 4, P])
        AF = sb("AF", [P, DFE // P, P])
        YE = sb("YE", [P, D])

        block = ctx.enter_context(nc.Block())

        def slot_loads(n):
            return n // RING + 1

        loaded = [sem(f"tile_loaded_{i}") for i in range(RING)]
        used = sem("tiles_used")

        @block.sync
        def _(sp):
            sp.dma_start(X[:, :, :], xT).then_inc(sem("x_loaded"), 16)
            sp.dma_start(vec[:, :, :], vecs).then_inc(sem("vec_loaded"), 16)
            for half in range(2):
                rows = slice(64 * half, 64 * half + 64)
                sp.dma_start(are[rows, :], a_re).then_inc(sem("lam_loaded"), 16)
                sp.dma_start(aim[rows, :], a_im).then_inc(sem("lam_loaded"), 16)
            sp.dma_start(dtt[:, :], log_dt.to_broadcast([P, G])).then_inc(sem("lam_loaded"), 16)
            sp.dma_start(H0Q[:, :, :], h0q).then_inc(sem("h0_loaded"), 16)
            sp.dma_start(H0X[:, :, :], h0x).then_inc(sem("h0_loaded"), 16)
            for hf in range(2):
                gs = slice(hf * GH, hf * GH + GH)
                if hf == 1:
                    sp.wait_ge(sem("a_built"), 1)
                sp.dma_start(BQ[:, :, :], bq[:, gs, :]).then_inc(sem("b_loaded"), 16)
                sp.dma_start(BX[:, :, :], bx[:, gs, :]).then_inc(sem("b_loaded"), 16)
                if hf == 1:
                    sp.wait_ge(sem("c_built"), 1)
                sp.dma_start(CQ[:, :, :], cq[:, gs, :]).then_inc(sem("c_loaded"), 16)
                sp.dma_start(CX[:, :, :], cx[:, gs, :]).then_inc(sem("c_loaded"), 16)
                if hf == 0:
                    for n in range(EARLY):
                        sp.dma_start(raw[n][:, :], wd[n]).then_inc(loaded[n], 16)
            sp.wait_ge(sem("states_done"), 2)
            sp.dma_start(hp_out, HP[:, :]).then_inc(sem("stored"), 16)
            sp.dma_start(hs_out, HS[:, :, :]).then_inc(sem("stored_ssm"), 16)
            sp.wait_ge(sem("stored"), 16)
            sp.wait_ge(sem("stored_ssm"), 16)
            sp.wait_ge(sem("y_mixed"), 8)
            for n in range(EARLY, RING):
                sp.dma_start(raw[n][:, :], wd[n]).then_inc(loaded[n], 16)
            for n in range(RING, NDENSE):
                sp.wait_ge(used, n - RING + 1)
                sp.dma_start(raw[n % RING][:, :], wd[n]).then_inc(loaded[n % RING], 16)

            def expert_tiles(e, r):
                for m in range(NE):
                    n = NDENSE + m
                    free = sp.snap(r * NE + (n - RING + 1))
                    src = we[bass.ds(e * NE + m, 1)].rearrange("a p n -> (a p) n")
                    sp.wait_ge(used, free)
                    sp.dma_start(raw[n % RING][:, :], src).then_inc(loaded[n % RING], 16)

            with sp.Fori(0, E) as e:
                expert_tiles(e, e)
            sp.wait_ge(sem("plan_ready"), 1)
            with sp.Fori(0, E) as e:
                for k in range(2):
                    i = sp.snap(e * 2 + k)
                    more = sp.value_load(plan[0:1, bass.ds(i, 1)], min_val=0, max_val=1)
                    with sp.If(more > 0):
                        r = sp.value_load(plan[0:1, bass.ds(i + 2 * E, 1)], min_val=E, max_val=E + 4)
                        expert_tiles(e, r)
            sp.wait_ge(sem("out_ready"), 1)
            sp.dma_start(yT, XN[:, :, :]).then_inc(sem("stored"), 16)
            sp.wait_ge(sem("stored"), 32)

        @block.gpsimd
        def _(pool):
            g = nc.gpsimd
            g.memset(ones[:, :], 1.0).then_inc(sem("pool_step"), 1)
            g.memset(epsb[:, :], EPS).then_inc(sem("pool_step"), 1)
            g.memset(halfpi[:, :], math.pi / 2).then_inc(sem("pool_step"), 1)
            g.memset(sel[:, :, :], 0.0).then_inc(sem("pool_step"), 1)
            g.iota(kramp[:, :], pattern=[[1, 9]], base=-4, channel_multiplier=0,
                   allow_small_or_imprecise_dtypes=True).then_inc(sem("pool_step"), 1)
            g.iota(jramp[:, :], pattern=[[1, NB]], base=0, channel_multiplier=0,
                   allow_small_or_imprecise_dtypes=True).then_inc(sem("pool_step"), 1)
            pool.wait_ge(sem("pool_step"), 6)
            g.affine_select(out=ident[:, :], in_=ones[:, :], compare_op=ALU.is_equal, fill=0.0, base=0,
                            pattern=[[-1, P]], channel_multiplier=1).then_inc(sem("consts"), 1)
            g.affine_select(out=swp[:, 0:64], in_=ones[:, 0:64], compare_op=ALU.is_equal, fill=0.0, base=-64,
                            pattern=[[-1, 64]], channel_multiplier=1).then_inc(sem("consts"), 1)
            g.affine_select(out=swp[:, 64:128], in_=ones[:, 0:64], compare_op=ALU.is_equal, fill=0.0, base=0,
                            pattern=[[-1, 64]], channel_multiplier=1).then_inc(sem("consts"), 1)
            g.affine_select(out=sel[:, :, 112:128], in_=ones[:, :].rearrange("p (m x) -> p m x", m=8),
                            compare_op=ALU.is_equal, fill=0.0, base=0, pattern=[[-16, 8], [-1, 16]],
                            channel_multiplier=1).then_inc(sem("consts"), 1)
            g.affine_select(out=tmask[:, :], in_=ones[:, :], compare_op=ALU.is_ge, fill=0.0, base=15,
                            pattern=[[16, 8], [0, 16]], channel_multiplier=-1).then_inc(sem("consts"), 1)
            pool.wait_ge(sem("consts"), 5)
            pool.wait_ge(sem("pow_ready"), 1)
            n = 0
            for hf in range(2):
                gs = slice(hf * GH, hf * GH + GH)
                pool.wait_ge(sem("c_loaded"), 32 * (hf + 1))
                if hf == 1:
                    pool.wait_ge(sem("half_used"), 1)
                for s in range(L):
                    fr = T9[0][:, s, gs].unsqueeze(2).to_broadcast([P, GH, H])
                    fs = T9[1][:, s, gs].unsqueeze(2).to_broadcast([P, GH, H])
                    out = CM[:, :, s * H:(s + 1) * H]
                    if n:
                        pool.wait_ge(sem("c_step"), n)
                    g.tensor_tensor(out, CQ[:, :, :], fr, ALU.mult).then_inc(sem("c_step"), 1)
                    g.tensor_tensor(CT[:, :, :], CX[:, :, :], fs, ALU.mult).then_inc(sem("c_step"), 1)
                    n += 2
                    pool.wait_ge(sem("c_step"), n)
                    ins = g.tensor_tensor(out, out, CT[:, :, :], ALU.add)
                    if s < L - 1:
                        ins.then_inc(sem("c_step"), 1)
                        n += 1
                    else:
                        ins.then_inc(sem("c_built"), 1)
                        pool.wait_ge(sem("c_built"), hf + 1)
            pool.wait_ge(sem("y_mixed"), 8)
            g.affine_select(out=tri[:, :], in_=ones[:, :], compare_op=ALU.is_gt, fill=0.0, base=0,
                            pattern=[[1, P]], channel_multiplier=-1).then_inc(sem("route_consts"), 1)
            g.iota(slot[:, :, :], pattern=[[P, 3], [1, P]], base=0, channel_multiplier=0,
                   allow_small_or_imprecise_dtypes=True).then_inc(sem("route_consts"), 1)
            g.memset(LG[:, :, :], 0.0).then_inc(sem("route_consts"), 1)
            g.memset(dz[:, :, :], 1.0).then_inc(sem("route_consts"), 1)
            pool.wait_ge(sem("route_consts"), 4)
            g.memset(dz[:, :, 0:1], 0.0).then_inc(sem("route_consts"), 1)
            pool.dma_start(relx[0:NBUCK, :], relb).then_inc(sem("rel_loaded"), 16)
            pool.dma_start(oneh[:, :], onehot).then_inc(sem("rel_loaded"), 16)
            pool.dma_start(SINK[:, :], sinks.to_broadcast([P, NH])).then_inc(sem("sink_loaded"), 16)
            for b in range(TS):
                pool.dma_start(SINKC[b * NH:(b + 1) * NH, :], sinks.rearrange("a h -> h a"))\
                    .then_inc(sem("sink_loaded"), 16)
            for b in range(TS):
                pool.dma_start(KCT[:, b, :, 0:W - 1], kcT[b][:, :, 1:W]).then_inc(sem("cache_loaded"), 16)
            pool.dma_start(VC[0:W - 1, :, :], vc[1:W]).then_inc(sem("cache_loaded"), 16)
            pool.dma_start(WR[:, :, :], wr).then_inc(sem("router_loaded"), 16)
            pool.wait_ge(sem("bias_rows_ready"), 1)
            pool.dma_start(bias_dram, brow[:, :].unsqueeze(1).to_broadcast([NH, P, 384]))\
                .then_inc(sem("bias_stored"), 16)
            pool.wait_ge(sem("bias_stored"), 16)
            for h in range(NH):
                src = bias_dram[h, :, 127:127 + 2 * W]
                src = bass.AP(src.tensor, src.offset, [[384 - 1, P], [1, 2 * W]])
                pool.dma_start(BIAS[:, h, :], src).then_inc(sem("bias_loaded"), 16)
            for b in range(TS):
                pool.dma_start(BSM[b * NH:(b + 1) * NH, :], bias_dram[:, 0, W:2 * W]).then_inc(sem("bias_loaded"), 16)

            pool.wait_ge(sem("v_ready"), 3)
            pool.dma_start(VC[W - 1:W, :, :], VT[0:TS, 2, :]).then_inc(sem("cache_loaded"), 16)
            pool.wait_ge(sem("cache_loaded"), 16 * (TS + 2))
            pool.wait_ge(sem("kc_ready"), 1)
            pool.dma_start(kp_out, KT[:, :, TP - W:TP]).then_inc(sem("kv_stored"), 16)
            pool.dma_start(vp_out, VT[:, 1, :]).then_inc(sem("kv_stored"), 16)
            pool.dma_start(ks_out, KCT[:, :, :, :]).then_inc(sem("kv_stored"), 16)
            pool.dma_start(vs_out, VC[:, :, :]).then_inc(sem("kv_stored"), 16)
            pool.wait_ge(sem("kv_stored"), 64)

        @block.scalar
        def _(act):
            a = nc.scalar

            def norm(i, ready, n_ready):
                act.wait_ge(ready, n_ready)
                if i:
                    act.wait_ge(sem("norm_summed"), i)
                a.activation(TMP[:, :, :], X[:, :, :], ACT.Square).then_inc(sem("squared"), 1)
                act.wait_ge(sem("norm_summed"), i + 1)
                if i:
                    act.wait_ge(sem("rstd_ready"), i)
                else:
                    act.wait_ge(sem("consts"), 5)
                a.activation(root[:, :], ps[:, 0, 0:NT], ACT.Sqrt, bias=epsb[:, :], scale=1.0 / D)\
                    .then_inc(sem("root_ready"), 1)

            act.wait_ge(sem("lam_loaded"), 80)
            a.activation(q[0][:, :], dtt[:, :], ACT.Tanh, scale=1.0 / 32).then_inc(sem("tanh_ready"), 1)
            norm(0, sem("x_loaded"), 16)
            act.wait_ge(sem("decay_ready"), 1)
            a.activation(q[3][:, :], q[1][:, :], ACT.Tanh, scale=0.5).then_inc(sem("tanh_ready"), 1)
            act.wait_ge(sem("phase9_ready"), 1)
            a.activation(EI[:, :, :], T9[0][:, :, :], ACT.Sin).then_inc(sem("sin9_ready"), 1)
            a.activation(ER[:, :, :], T9[0][:, :, :], ACT.Abs).then_inc(sem("sin9_ready"), 1)
            a.activation(q[6][:, :], q[4][:, :], ACT.Sin, scale=0.5).then_inc(sem("sin9_ready"), 1)
            act.wait_ge(sem("sin9_ready"), 3)
            a.activation(ER[:, :, :], ER[:, :, :], ACT.Sin, scale=-1.0, bias=halfpi[:, :])\
                .then_inc(sem("sin9_ready"), 1)
            for hf in range(2):
                act.wait_ge(sem("phase_ready"), hf + 1)
                if hf:
                    act.wait_ge(sem("states_done"), 1)
                a.activation(SS[:, :, :], TA[:, :, :], ACT.Sin, scale=sgn[:, :]).then_inc(sem("turn_ready"), 1)
                a.activation(COS[:, :, :], TA[:, :, :], ACT.Abs).then_inc(sem("turn_ready"), 1)
                act.wait_ge(sem("turn_ready"), 3 * hf + 2)
                a.activation(COS[:, :, :], COS[:, :, :], ACT.Sin, scale=-1.0, bias=halfpi[:, :])\
                    .then_inc(sem("turn_ready"), 1)
                if hf:
                    act.wait_ge(sem("y_made"), 4)
                for k in range(G8):
                    act.wait_ge(sem("u_moved"), 8 * hf + k + 1)
                    a.copy(U[:, :, :].rearrange("p (c k) n -> p k c n", k=G8)[:, k],
                           ps[:, k % 2, 0:CH * UC].rearrange("p (c n) -> p c n", c=CH)).then_inc(sem("u_ready"), 1)
                for b in range(GH // 4):
                    act.wait_ge(sem("a_turned"), 8 * hf + b + 1)
                    if 8 * hf + b >= 2:
                        act.wait_ge(sem("v_made"), (8 * hf + b) // 2)
                    dst = AT[:, 4 * (b % 2):4 * (b % 2) + 4, :]
                    src = ps[:, 4 + b % 2, :].rearrange("p (g n) -> p g n", g=4)
                    a.copy(dst[:, :, 0:128], src).then_inc(sem("at_ready"), 1)
                    a.copy(dst[:, :, 128:192], src[:, :, 0:64]).then_inc(sem("at_ready"), 1)
                for b in range(4):
                    act.wait_ge(sem("y_made"), 4 * hf + b + 1)
                    a.copy(Y[:, hf * GH + 8 * b:hf * GH + 8 * b + 8, :],
                           ps[:, 4 + b % 2, 0:8 * UC].rearrange("p (g n) -> p g n", g=8)).then_inc(sem("y_ready"), 1)
            act.wait_ge(sem("y_mixed"), 8)
            a.activation(XN[:, :, :], TMP[:, :, :], ACT.Gelu_apprx_tanh).then_inc(sem("z_ready"), 1)

            def gate(n, func, first, before):
                act.wait_ge(sem("pair_made"), n + 1)
                if n >= 2:
                    act.wait_ge(sem("pair_done"), n - 1)
                a.activation(SG[:, n % 2, :], ps[:, 2 * (n % 2) + first, 0:NT], func).then_inc(sem("gated"), 1)

            for n in range(8):
                gate(n, ACT.Sigmoid, 1, 0)
            act.wait_ge(sem("bias_made"), 1)
            a.copy(brow[:, :], ps[0:NH, 7, 0:384]).then_inc(sem("bias_rows_ready"), 1)
            norm(1, sem("pair_done"), 8)
            for n in range(8, 8 + NF):
                gate(n, ACT.Silu, 0, 0)
            norm(2, sem("resid_ffn"), 8)
            act.wait_ge(sem("pair_made"), 31)
            for i in range(2):
                a.copy(KT[:, i, :], ps[:, 0 + i, 0:NT]).then_inc(sem("k_ready"), 1)
            act.wait_ge(sem("v_made2"), 3)
            for t in range(3):
                rows = P if t < 2 else TS
                a.copy(VT[0:rows, t, :], ps[0:rows, 4 + t, 0:NKV * HD]).then_inc(sem("v_ready"), 1)
            act.wait_ge(sem("k_ready"), 2)
            act.wait_ge(sem("cache_loaded"), 16 * (TS + 1))
            a.copy(KCT[:, :, :, W - 1].rearrange("p b k -> p k b"), KT[:, :, TP:NT]).then_inc(sem("kc_ready"), 1)
            for n in range(31, 35):
                act.wait_ge(sem("pair_made"), n + 1)
                for i in range(2):
                    a.copy(QT[:, 2 * (n - 31) + i, :], ps[:, 2 * (n % 2) + i, 0:NT]).then_inc(sem("q_ready"), 1)
            for h in range(NH + 1):
                b = h % 2
                act.wait_ge(sem("shift_ready"), h + 1)
                if h >= 2:
                    act.wait_ge(sem("p_turned"), h - 1)
                if h < NH:
                    a.activation(SC[:, b, 0:128], SC[:, b, 0:128], ACT.Exp, bias=nm[:, b, 0:1],
                                 accum_out=sm[:, b, 0:1]).then_inc(sem("exp_ready"), 1)
                    a.activation(SC[:, b, 128:384], SC[:, b, 128:384], ACT.Exp, bias=nm[:, b, 1:2],
                                 accum_out=sm[:, b, 1:2]).then_inc(sem("exp_ready"), 1)
                    a.activation(es[:, b, :], nm[:, b, :], ACT.Exp, bias=SINK[:, HEADS[h]:HEADS[h] + 1]).then_inc(sem("exp_ready"), 1)
                else:
                    a.activation(SC[:, b, 0:128], SC[:, b, 0:128], ACT.Exp, bias=nm[:, b, 0:1],
                                 accum_out=sm[:, b, 0:1]).then_inc(sem("exp_ready"), 1)
                    a.activation(es[:, b, 0:1], nm[:, b, 0:1], ACT.Exp, bias=SINKC[:, :]).then_inc(sem("exp_ready"), 1)
                act.wait_ge(sem("p_turned"), h + 1)
                if h >= 2:
                    act.wait_ge(sem("pv_made"), h - 1)
                n = 384 if h < NH else 128
                a.copy(PTT[:, b, 0:n], ps[:, 2 + b, 0:n]).then_inc(sem("pt_ready"), 1)
            norm(3, sem("resid_o"), 8)
            act.wait_ge(sem("kv_stored"), 64)
            for t in range(3):
                rows = P if t < 2 else TS
                for hf in range(2):
                    act.wait_ge(sem("h_turned"), 2 * t + hf + 1)
                    a.copy(HT[0:rows, t, hf * 512:hf * 512 + 512], ps[0:rows, 1 + hf, :]).then_inc(sem("ht_ready"), 1)
            act.wait_ge(sem("gap_ready"), 1)
            a.activation(r4[:, :, :], r3[:, :, :], ACT.Exp).then_inc(sem("gexp_ready"), 1)

            def expert(r):
                for i in range(2):
                    act.wait_ge(sem("gathered"), act.snap(2 * r + (i + 1)))
                    a.copy(XE[:, 0, 4 * i:4 * i + 4, :], ps[:, 6 + i, :].rearrange("p (c n) -> p c n", c=4))\
                        .then_inc(sem("xe_ready"), 1)
                for j in range(JE):
                    act.wait_ge(sem("gu_made"), act.snap(JE * r + (j + 1)))
                    if j >= 2:
                        act.wait_ge(sem("act_ready"), act.snap(JE * r + (j - 1)))
                    a.activation(SIL[:, j % 2, :], ps[:, 2 * (j % 2), :], ACT.Silu).then_inc(sem("silu_ready"), 1)
                    if j:
                        turned(r, j - 1)
                turned(r, JE - 1)
                for i in range(2):
                    act.wait_ge(sem("down_made"), act.snap(r + 1))
                    a.copy(YE[:, 512 * i:512 * i + 512], ps[:, 4 + i, :]).then_inc(sem("ye_ready"), 1)

            def turned(r, j):
                act.wait_ge(sem("act_turned"), act.snap(JE * r + (j + 1)))
                a.copy(AF[:, 4 * j:4 * j + 4, :], ps[:, 6 + j % 2, :].rearrange("p (c n) -> p c n", c=4))\
                    .then_inc(sem("af_ready"), 1)

            with act.Fori(0, E) as e:
                expert(e)
            act.wait_ge(sem("plan_ready"), 1)
            with act.Fori(0, 2 * E) as i:
                more = act.value_load(plan[0:1, bass.ds(i, 1)], min_val=0, max_val=1)
                with act.If(more > 0):
                    r = act.value_load(plan[0:1, bass.ds(i + 2 * E, 1)], min_val=E, max_val=E + 4)
                    expert(r)
            norm(4, sem("moe_done"), 1)

        @block.vector
        def _(dve):
            v = nc.vector
            steps = [0]

            def link(ins):
                steps[0] += 1
                ins.then_inc(sem("dve_step"), 1)
                dve.wait_ge(sem("dve_step"), steps[0])

            def reduce_phase(x, t, last=None):
                link(v.tensor_scalar(t, x, 1.0 / (2 * math.pi), MAGIC, ALU.mult, ALU.add))
                link(v.tensor_scalar(t, t, MAGIC, None, ALU.subtract))
                link(v.scalar_tensor_tensor(out=x, in0=t, scalar=-TWO_PI_HI, in1=x, op0=ALU.mult, op1=ALU.add))
                link(v.scalar_tensor_tensor(out=x, in0=t, scalar=-TWO_PI_LO, in1=x, op0=ALU.mult, op1=ALU.add))
                ins = v.tensor_scalar(x, x, PI_IN, -PI_IN, ALU.min, ALU.max)
                if last is None:
                    link(ins)
                else:
                    ins.then_inc(last, 1)

            def norm(i, gidx, done):
                dve.wait_ge(sem("root_ready"), i + 1)
                v.reciprocal(rstd[:, :], root[:, :]).then_inc(sem("rstd_ready"), 1)
                dve.wait_ge(sem("rstd_ready"), i + 1)
                scale(XN, gidx, done)

            def scale(out, gidx, done):
                for c in range(KC):
                    v.scalar_tensor_tensor(out=out[:, c, :], in0=X[:, c, :], scalar=vec[:, gidx, c:c + 1],
                                           in1=rstd[:, :], op0=ALU.mult, op1=ALU.mult).then_inc(done, 1)

            for rows, x in ((slice(0, 64), 1.0), (slice(64, 128), -1.0)):
                link(v.memset(sgn[rows, :], x))
                link(v.memset(nsgn[rows, :], -x))
            dve.wait_ge(sem("lam_loaded"), 80)
            dve.wait_ge(sem("tanh_ready"), 1)
            link(v.tensor_scalar(q[1][:, :], q[0][:, :], -1.0, 1.0, ALU.mult, ALU.add))
            link(v.reciprocal(q[1][:, :], q[1][:, :]))
            link(v.scalar_tensor_tensor(out=dtt[:, :], in0=q[0][:, :], scalar=1.0, in1=q[1][:, :],
                                        op0=ALU.add, op1=ALU.mult))
            for _ in range(4):
                link(v.tensor_tensor(dtt[:, :], dtt[:, :], dtt[:, :], ALU.mult))
            v.tensor_tensor(q[1][:, :], are[:, :], dtt[:, :], ALU.mult).then_inc(sem("decay_ready"), 1)
            link(v.tensor_tensor(q[4][:, :], aim[:, :], dtt[:, :], ALU.mult))
            reduce_phase(q[4][:, :], q[5][:, :])
            dve.wait_ge(sem("consts"), 5)
            dve.wait_ge(sem("vec_loaded"), 16)
            link(v.tensor_tensor(T9[0][:, :, :], q[4][:, :].unsqueeze(1).to_broadcast([P, 9, G]),
                                 kramp[:, :].unsqueeze(2).to_broadcast([P, 9, G]), ALU.mult))
            reduce_phase(T9[0][:, :, :], T9[1][:, :, :], sem("phase9_ready"))
            link(v.tensor_scalar(q[7][:, :], q[4][:, :], float(L), None, ALU.mult))
            reduce_phase(q[7][:, :], q[5][:, :])
            dve.wait_ge(sem("tanh_ready"), 2)
            t2 = q[3][:, :]
            link(v.tensor_scalar(q[8][:, :], t2, 1.0, None, ALU.add))
            link(v.tensor_scalar(q[9][:, :], t2, -1.0, 1.0, ALU.mult, ALU.add))
            link(v.reciprocal(q[10][:, :], q[8][:, :]))
            link(v.reciprocal(q[11][:, :], q[9][:, :]))
            link(v.memset(MT[:, 4, :], 1.0))
            link(v.tensor_tensor(MT[:, 5, :], q[8][:, :], q[11][:, :], ALU.mult))
            link(v.tensor_tensor(MT[:, 3, :], q[9][:, :], q[10][:, :], ALU.mult))
            for sgn_, one in ((1, 5), (-1, 3)):
                for k in range(2, 5):
                    link(v.tensor_tensor(MT[:, 4 + sgn_ * k, :], MT[:, 4 + sgn_ * (k - 1), :], MT[:, one, :], ALU.mult))
            norm(0, G_MIX0, sem("xn_ready"))
            dve.wait_ge(sem("sin9_ready"), 4)
            link(v.tensor_tensor(q[8][:, :], are[:, :], are[:, :], ALU.mult))
            link(v.tensor_tensor(q[9][:, :], aim[:, :], aim[:, :], ALU.mult))
            link(v.tensor_tensor(q[8][:, :], q[8][:, :], q[9][:, :], ALU.add))
            link(v.reciprocal(q[8][:, :], q[8][:, :]))
            link(v.scalar_tensor_tensor(out=q[9][:, :], in0=t2, scalar=2.0, in1=q[11][:, :],
                                        op0=ALU.mult, op1=ALU.mult))
            link(v.tensor_tensor(q[9][:, :], q[9][:, :], ER[:, 5, :], ALU.mult))
            link(v.tensor_tensor(q[6][:, :], q[6][:, :], q[6][:, :], ALU.mult))
            link(v.scalar_tensor_tensor(out=q[9][:, :], in0=q[6][:, :], scalar=-2.0, in1=q[9][:, :],
                                        op0=ALU.mult, op1=ALU.add))
            link(v.tensor_tensor(q[10][:, :], MT[:, 5, :], EI[:, 5, :], ALU.mult))
            link(v.tensor_tensor(q[12][:, :], q[9][:, :], are[:, :], ALU.mult))
            link(v.tensor_tensor(q[11][:, :], q[10][:, :], aim[:, :], ALU.mult))
            link(v.tensor_tensor(q[12][:, :], q[12][:, :], q[11][:, :], ALU.add))
            link(v.tensor_tensor(q[12][:, :], q[12][:, :], q[8][:, :], ALU.mult))
            link(v.tensor_tensor(q[13][:, :], q[10][:, :], are[:, :], ALU.mult))
            link(v.tensor_tensor(q[11][:, :], q[9][:, :], aim[:, :], ALU.mult))
            link(v.tensor_tensor(q[13][:, :], q[13][:, :], q[11][:, :], ALU.subtract))
            link(v.tensor_tensor(q[13][:, :], q[13][:, :], q[8][:, :], ALU.mult))
            link(v.tensor_tensor(ER[:, :, :], ER[:, :, :], MT[:, :, :], ALU.mult))
            link(v.tensor_tensor(EI[:, :, :], EI[:, :, :], MT[:, :, :], ALU.mult))
            link(v.tensor_scalar(T9[0][:, :, :], ER[:, :, :], sgn[:, :], None, ALU.mult))
            v.tensor_scalar(T9[1][:, :, :], EI[:, :, :], -1.0, None, ALU.mult).then_inc(sem("pow_ready"), 1)
            link(v.tensor_copy(q[0][:, :], ER[:, 5, :]))
            link(v.tensor_scalar(q[1][:, :], EI[:, 5, :], nsgn[:, :], None, ALU.mult))
            link(v.tensor_copy(q[2][:, :], ER[:, 7, :]))
            link(v.tensor_copy(q[3][:, :], EI[:, 7, :]))
            link(v.tensor_tensor(q[4][:, :], MT[:, 8, :], MT[:, 8, :], ALU.mult))
            cr = q[12][:, :].unsqueeze(1).to_broadcast([P, 9, G])
            ci = q[13][:, :].unsqueeze(1).to_broadcast([P, 9, G])
            link(v.tensor_tensor(MT[:, :, :], EI[:, :, :], ci, ALU.mult))
            link(v.tensor_tensor(EI[:, :, :], EI[:, :, :], cr, ALU.mult))
            X9 = TC[:, :, :].rearrange("p a b -> p (a b)")[:, 0:9 * G].rearrange("p (a b) -> p a b", a=9)
            link(v.tensor_tensor(X9, ER[:, :, :], ci, ALU.mult))
            link(v.tensor_tensor(ER[:, :, :], ER[:, :, :], cr, ALU.mult))
            link(v.tensor_tensor(ER[:, :, :], ER[:, :, :], MT[:, :, :], ALU.subtract))
            link(v.tensor_tensor(EI[:, :, :], EI[:, :, :], X9, ALU.add))
            link(v.tensor_scalar(EI[:, :, :], EI[:, :, :], nsgn[:, :], None, ALU.mult))
            dve.wait_ge(sem("h0_loaded"), 32)
            wide = lambda x: x.unsqueeze(2).to_broadcast([P, G, TS])
            link(v.tensor_tensor(H0Q[:, :, :], H0Q[:, :, :], wide(q[0][:, :]), ALU.mult))
            link(v.tensor_tensor(H0X[:, :, :], H0X[:, :, :], wide(q[1][:, :]), ALU.mult))
            link(v.tensor_tensor(H0Q[:, :, :], H0Q[:, :, :], H0X[:, :, :], ALU.add))

            for hf in range(2):
                gs = slice(hf * GH, hf * GH + GH)
                link(v.tensor_tensor(TA[:, :, :], q[7][:, gs].unsqueeze(2).to_broadcast([P, GH, NB]),
                                     jramp[:, :].unsqueeze(1).to_broadcast([P, GH, NB]), ALU.mult))
                reduce_phase(TA[:, :, :], TB[:, :, :], sem("phase_ready"))
                dve.wait_ge(sem("b_loaded"), 32 * (hf + 1))
                if hf:
                    dve.wait_ge(sem("toep_made"), 8)
                for s in range(L):
                    er = ER[:, 8 - s, gs].unsqueeze(2).to_broadcast([P, GH, H])
                    ei = EI[:, 8 - s, gs].unsqueeze(2).to_broadcast([P, GH, H])
                    out = AM[:, :, s * H:(s + 1) * H]
                    v.tensor_tensor(out, BQ[:, :, :], er, ALU.mult).then_inc(sem("dve_step"), 1)
                    steps[0] += 1
                    link(v.tensor_tensor(PT[:, :, :], BX[:, :, :], ei, ALU.mult))
                    ins = v.tensor_tensor(out, out, PT[:, :, :], ALU.add)
                    if s < L - 1:
                        link(ins)
                    else:
                        ins.then_inc(sem("a_built"), 1)
                link(v.tensor_copy(R8[:, :, :], q[4][:, gs].unsqueeze(2).to_broadcast([P, GH, NB])))
                link(v.memset(R8[:, :, 0:1], 0.0))
                link(v.memset(WV[:, 0:1], 0.0))
                dve.wait_ge(sem("turn_ready"), 3 * hf + 3)
                wv = WV[:, 1:].rearrange("p (g j) -> p g j", g=GH)

                def turn_back(b):
                    dve.wait_ge(sem("v_made"), 4 * hf + b + 1)
                    bk = 6 if b % 2 == 0 else 0
                    g8 = slice(8 * b, 8 * b + 8)
                    V = ps[:, bk, 0:8 * UC].rearrange("p (g n) -> p g n", g=8)
                    VX = ps[:, bk + 1, 0:8 * UC].rearrange("p (g n) -> p g n", g=8)
                    v.tensor_tensor(TB[:, g8, :], V[:, :, 0:NB], COS[:, g8, :], ALU.mult).then_inc(sem("dve_step"), 1)
                    v.tensor_copy(VS[:, g8, :], V[:, :, NB:UC]).then_inc(sem("dve_step"), 1)
                    steps[0] += 2
                    v.tensor_tensor(TC[:, g8, :], VX[:, :, 0:NB], SS[:, g8, :], ALU.mult).then_inc(sem("v_turned"), 1)
                    dve.wait_ge(sem("dve_step"), steps[0])
                    dve.wait_ge(sem("v_turned"), 4 * hf + b + 1)
                    link(v.tensor_tensor(wv[:, g8, :], TB[:, g8, :], TC[:, g8, :], ALU.add))

                for b in range(8):
                    dve.wait_ge(sem("toep_made"), 8 * hf + b + 1)
                    v.tensor_tensor(TM[:, 4 * b:4 * b + 4, :], ps[:, 2 + b % 2, :].rearrange("p (g n) -> p g n", g=4),
                                    tmask[:, :].unsqueeze(1).to_broadcast([P, 4, P]), ALU.mult)\
                        .then_inc(sem("toep_ready"), 1)
                    if b % 2 and b > 1:
                        turn_back(b // 2 - 1)
                turn_back(3)
                sv = SV[:, :, :].rearrange("p g j -> p (g j)")
                v.tensor_tensor_scan(sv, WV[:, 0:GH * NB], R8[:, :, :].rearrange("p g j -> p (g j)"), 0.0,
                                     ALU.add, ALU.mult).then_inc(sem("scanned"), 1)
                dve.wait_ge(sem("scanned"), hf + 1)
                v.tensor_tensor(GL[:, :], SV[:, :, NB - 1], wv[:, :, NB - 1], ALU.add).then_inc(sem("last_ready"), 1)
                link(v.tensor_tensor(TB[:, :, :], SV[:, :, :], COS[:, :, :], ALU.mult))
                for i in range(2):
                    dve.wait_ge(sem("swapped"), 3 * hf + i + 1)
                    g16 = slice(16 * i, 16 * i + 16)
                    link(v.tensor_tensor(TC[:, g16, :], ps[:, 2 + i, :].rearrange("p (g j) -> p g j", g=16),
                                         SS[:, g16, :], ALU.mult))
                if hf:
                    dve.wait_ge(sem("y_made"), 4)
                link(v.tensor_tensor(HM[:, :, 0:NB], TB[:, :, :], TC[:, :, :], ALU.subtract))
                v.tensor_copy(HM[:, :, NB:UC], H0Q[:, gs, :]).then_inc(sem("h_ready"), 1)
                c31, s31 = COS[:, :, NB - 1], SS[:, :, NB - 1]
                link(v.tensor_scalar(q[8][:, 0:GH], s31, sgn[:, :], None, ALU.mult))
                link(v.tensor_tensor(q[9][:, 0:GH], q[2][:, gs], c31, ALU.mult))
                link(v.tensor_tensor(q[10][:, 0:GH], q[3][:, gs], q[8][:, 0:GH], ALU.mult))
                link(v.tensor_tensor(q[9][:, 0:GH], q[9][:, 0:GH], q[10][:, 0:GH], ALU.subtract))
                link(v.tensor_tensor(q[8][:, 0:GH], q[8][:, 0:GH], q[2][:, gs], ALU.mult))
                link(v.tensor_tensor(q[10][:, 0:GH], q[3][:, gs], c31, ALU.mult))
                link(v.tensor_tensor(q[8][:, 0:GH], q[8][:, 0:GH], q[10][:, 0:GH], ALU.add))
                link(v.tensor_scalar(q[8][:, 0:GH], q[8][:, 0:GH], nsgn[:, :], None, ALU.mult))
                link(v.tensor_tensor(q[9][:, 0:GH], q[9][:, 0:GH], GL[:, :], ALU.mult))
                dve.wait_ge(sem("swapped"), 3 * hf + 3)
                link(v.tensor_tensor(q[8][:, 0:GH], ps[:, 7, 0:GH], q[8][:, 0:GH], ALU.mult))
                link(v.tensor_tensor(HP[:, gs], q[9][:, 0:GH], q[8][:, 0:GH], ALU.add))
                v.tensor_tensor(HS[:, gs, :], H0Q[:, gs, :], VS[:, :, :], ALU.add).then_inc(sem("states_done"), 1)
            dve.wait_ge(sem("squared"), 1)
            for c in range(KC):
                v.tensor_scalar(TMP[:, c, :], XN[:, c, :], vec[:, SSM_D, c:c + 1], None, ALU.mult)\
                    .then_inc(sem("du_ready"), 1)
            dve.wait_ge(sem("du_ready"), 8)
            for s in range(L):
                dve.wait_ge(sem("y_moved"), s + 1)
                y_t = TMP[:, :, s:TP:L]
                wide_cols = UC if s == SMID else NB
                src = ps[:, s % 2, 0:KC * wide_cols].rearrange("p (c n) -> p c n", c=KC)
                if s == SMID:
                    link(v.tensor_tensor(TMP[:, :, TP:NT], src[:, :, NB:UC], TMP[:, :, TP:NT], ALU.add))
                v.tensor_tensor(y_t, src[:, :, 0:NB], y_t, ALU.add).then_inc(sem("y_mixed"), 1)

            dve.wait_ge(sem("y_mixed"), 8)
            v.memset(relx[NBUCK:NBUCK + 1, :], NEG).then_inc(sem("outside_ready"), 1)
            for n in range(8):
                dve.wait_ge(sem("gated"), n + 1)
                link(v.tensor_tensor(SG[:, n % 2, :], ps[:, 2 * (n % 2), 0:NT], SG[:, n % 2, :], ALU.mult))
                v.tensor_tensor(X[:, n, :], X[:, n, :], SG[:, n % 2, :], ALU.add).then_inc(sem("pair_done"), 1)
            norm(1, G_FFN0, sem("xn_ready"))
            for n in range(8, 8 + NF):
                dve.wait_ge(sem("gated"), n + 1)
                v.tensor_tensor(FA[:, n - 8, :], ps[:, 2 * (n % 2) + 1, 0:NT], SG[:, n % 2, :], ALU.mult)\
                    .then_inc(sem("pair_done"), 1)
            dve.wait_ge(sem("ffn_made"), 1)
            for c in range(KC):
                v.tensor_tensor(X[:, c, :], ps[:, c, 0:NT], X[:, c, :], ALU.add).then_inc(sem("resid_ffn"), 1)
            dve.wait_ge(sem("norm_summed"), 3)
            norm(2, G_KV, sem("xn_ready"))
            scale(FA, G_MIX1, sem("xq_ready"))
            dve.wait_ge(sem("sink_loaded"), 16 * (TS + 1))
            dve.wait_ge(sem("bias_loaded"), 16 * (NH + TS))

            def scores(h):
                b = h % 2
                dve.wait_ge(sem("s_made"), h + 1)
                if h >= 2:
                    dve.wait_ge(sem("p_turned"), h - 1)
                if h < NH:
                    v.scalar_tensor_tensor(out=SC[:, b, 0:W], in0=ps[:, b, 0:W], scalar=SCALE,
                                           in1=BIAS[:, HEADS[h], W:2 * W], op0=ALU.mult, op1=ALU.add)\
                        .then_inc(sem("dve_step"), 1)
                    v.scalar_tensor_tensor(out=SC[:, b, W:3 * W], in0=ps[:, b, W:3 * W], scalar=SCALE,
                                           in1=BIAS[:, HEADS[h], :], op0=ALU.mult, op1=ALU.add).then_inc(sem("s_read"), 1)
                    steps[0] += 1
                    dve.wait_ge(sem("dve_step"), steps[0])
                    link(v.reduce_max(mx[:, b, 0:1], SC[:, b, 0:W], AX_X))
                    dve.wait_ge(sem("s_read"), h + 1)
                    link(v.reduce_max(mx[:, b, 1:2], SC[:, b, W:3 * W], AX_X))
                    v.tensor_scalar(nm[:, b, :], mx[:, b, :], SINK[:, HEADS[h]:HEADS[h] + 1], -1.0, ALU.max, ALU.mult)\
                        .then_inc(sem("shift_ready"), 1)
                else:
                    v.scalar_tensor_tensor(out=SC[:, b, 0:W], in0=ps[:, b, 0:W], scalar=SCALE,
                                           in1=BSM[:, :], op0=ALU.mult, op1=ALU.add).then_inc(sem("s_read"), 1)
                    dve.wait_ge(sem("s_read"), h + 1)
                    link(v.reduce_max(mx[:, b, 0:1], SC[:, b, 0:W], AX_X))
                    v.tensor_scalar(nm[:, b, 0:1], mx[:, b, 0:1], SINKC[:, :], -1.0, ALU.max, ALU.mult)\
                        .then_inc(sem("shift_ready"), 1)

            def probs(h):
                b = h % 2
                k = 2 if h < NH else 1
                dve.wait_ge(sem("exp_ready"), 3 * h + 3 if h < NH else 3 * NH + 2)
                link(v.tensor_tensor(rd[:, b, 0:k], sm[:, b, 0:k], es[:, b, 0:k], ALU.add))
                link(v.reciprocal(rd[:, b, 0:k], rd[:, b, 0:k]))
                if h < NH:
                    v.tensor_scalar(SC[:, b, 0:W], SC[:, b, 0:W], rd[:, b, 0:1], None, ALU.mult)\
                        .then_inc(sem("p_ready"), 1)
                    v.tensor_scalar(SC[:, b, W:3 * W], SC[:, b, W:3 * W], rd[:, b, 1:2], None, ALU.mult)\
                        .then_inc(sem("p_ready"), 1)
                else:
                    v.tensor_scalar(SC[:, b, 0:W], SC[:, b, 0:W], rd[:, b, 0:1], None, ALU.mult)\
                        .then_inc(sem("p_ready"), 1)

            def heads_out(h):
                c = h // 2
                dve.wait_ge(sem("pv_made"), h + 1)
                v.tensor_copy(OT[:, c, 0:TP], ps[:, 4 + c % 2, 0:TP]).then_inc(sem("o_ready"), 1)

            for h in range(NH):
                scores(h)
                if h:
                    probs(h - 1)
                if h >= 3 and h % 2:
                    heads_out(h - 2)
            dve.wait_ge(sem("st_made"), 1)
            sts = STS[:, :].rearrange("p (x g r) -> p x g r", g=2, r=R)
            for i in range(2):
                v.tensor_copy(sts[:, :, i], ps[:, 6 + i, 0:64].rearrange("p (x r) -> p x r", r=R))\
                    .then_inc(sem("st_ready"), 1)
            probs(NH - 1)
            scores(NH)
            heads_out(NH - 1)
            probs(NH)
            dve.wait_ge(sem("os_made"), 1)
            v.tensor_copy(OT[:, :, TP:NT], ps[:, 6, 0:KC * TS].rearrange("p (c b) -> p c b", c=KC))\
                .then_inc(sem("o_ready"), 1)
            for n in range(35, 39):
                dve.wait_ge(sem("pair_made"), n + 1)
                for i in range(2):
                    c = 2 * (n - 35) + i
                    v.tensor_tensor(X[:, c, :], ps[:, 2 * (n % 2) + i, 0:NT], X[:, c, :], ALU.add)\
                        .then_inc(sem("resid_o"), 1)
            norm(3, G_FFN1, sem("xn_ready"))

            dve.wait_ge(sem("kv_stored"), 64)
            dve.wait_ge(sem("logits_made"), 1)
            dve.wait_ge(sem("route_consts"), 5)
            link(v.tensor_copy(LG[:, 0:2, :], ps[:, 3, 0:2 * E].rearrange("p (t e) -> p t e", t=2)))
            link(v.tensor_copy(LG[0:TS, 2, :], ps[0:TS, 3, 2 * E:3 * E]))
            for t in range(3):
                link(v.max(top[:, t, :], LG[:, t, :]))
            first = top[:, :, 0:1].to_broadcast([P, 3, E])
            second = top[:, :, 1:2].to_broadcast([P, 3, E])
            link(v.tensor_tensor(r1[:, :, :], LG[:, :, :], second, ALU.is_gt))
            link(v.tensor_tensor(r2[:, :, :], LG[:, :, :], second, ALU.is_equal))
            flat = lambda x: x[:, :, :].rearrange("p t e -> p (t e)")
            link(v.tensor_tensor_scan(flat(r3), flat(dz), flat(r2), 0.0, ALU.mult, ALU.add))
            link(v.tensor_reduce(v1[:, :], r1[:, :, :], AX_X, ALU.add))
            link(v.tensor_tensor(r3[:, :, :], r3[:, :, :], v1[:, :].unsqueeze(2).to_broadcast([P, 3, E]), ALU.add))
            link(v.tensor_scalar(r3[:, :, :], r3[:, :, :], 2.0, None, ALU.is_le))
            link(v.tensor_tensor(r2[:, :, :], r2[:, :, :], r3[:, :, :], ALU.mult))
            v.tensor_tensor(SELM[:, :, :], r1[:, :, :], r2[:, :, :], ALU.add).then_inc(sem("sel_ready"), 1)
            dve.wait_ge(sem("sel_ready"), 1)
            v.tensor_tensor(r3[:, :, :], LG[:, :, :], first, ALU.subtract).then_inc(sem("gap_ready"), 1)
            dve.wait_ge(sem("gexp_ready"), 1)
            link(v.tensor_tensor(GATE[:, :, :], r4[:, :, :], SELM[:, :, :], ALU.mult))
            link(v.tensor_reduce(v1[:, :], GATE[:, :, :], AX_X, ALU.add))
            link(v.reciprocal(v1[:, :], v1[:, :]))
            link(v.tensor_tensor(GATE[:, :, :], GATE[:, :, :], v1[:, :].unsqueeze(2).to_broadcast([P, 3, E]), ALU.mult))
            dve.wait_ge(sem("pos_made"), 1)
            link(v.memset(POS[:, :, :], 0.0))
            link(v.tensor_copy(POS[:, 0:2, :], ps[:, 4, 0:2 * E].rearrange("p (t e) -> p t e", t=2)))
            link(v.tensor_copy(POS[0:TS, 2, :], ps[0:TS, 4, 2 * E:3 * E]))
            link(v.scalar_tensor_tensor(out=POS[:, :, :], in0=POS[:, :, :], scalar=1.0, in1=SELM[:, :, :],
                                        op0=ALU.add, op1=ALU.mult))
            link(v.tensor_scalar(POS[:, :, :], POS[:, :, :], -1.0, None, ALU.add))
            need = cnt[:, :].rearrange("p (e k) -> p e k", k=2)
            total = ps[0:1, 4, 3 * E:4 * E]
            link(v.tensor_scalar(need[:, :, 0], total, float(P) + 0.5, None, ALU.is_gt))
            link(v.tensor_scalar(need[:, :, 1], total, 2.0 * P + 0.5, None, ALU.is_gt))
            link(v.memset(run[:, :], 1.0))
            link(v.memset(run[:, 0:1], float(E)))
            link(v.tensor_tensor_scan(run[:, 1:2 * E + 1], run[:, 1:2 * E + 1], cnt[:, :], float(E), ALU.mult, ALU.add))
            link(v.tensor_copy(plan[:, 0:2 * E], cnt[:, :]))
            v.tensor_copy(plan[:, 2 * E:4 * E + 1], run[:, :]).then_inc(sem("plan_ready"), 1)

            def dispatch(e, k, r, which):
                pc = [POS[0:(P if t < 2 else TS), t, bass.ds(e, 1)] for t in range(3)]
                gc = [GATE[0:(P if t < 2 else TS), t, bass.ds(e, 1)] for t in range(3)]
                if which == "later":
                    dve.wait_ge(sem("gate_turned"), r)
                    dve.wait_ge(sem("gathered"), dve.snap(r * 2))
                for t in range(3):
                    rows = P if t < 2 else TS
                    v.tensor_scalar(DSP[0:rows, 0, t, :], slot[0:rows, k, :], pc[t], None, ALU.is_equal)\
                        .then_inc(sem("dispatched"), 1)
                dve.wait_ge(sem("dispatched"), dve.snap(r * 3 + 3))
                for t in range(3):
                    rows = P if t < 2 else TS
                    v.tensor_scalar(DG[0:rows, t, :], DSP[0:rows, 0, t, :], gc[t], None, ALU.mult)\
                        .then_inc(sem("gate_spread"), 1)

            def expert(r):
                def act_mul(j):
                    dve.wait_ge(sem("silu_ready"), dve.snap(r * JE + (j + 1)))
                    if j >= 2:
                        dve.wait_ge(sem("act_turned"), dve.snap(r * JE + (j - 1)))
                    v.tensor_tensor(AC[:, j % 2, :], ps[:, 2 * (j % 2) + 1, :], SIL[:, j % 2, :], ALU.mult)\
                        .then_inc(sem("act_ready"), 1)
                dve.wait_ge(sem("gate_turned"), r + 1)
                v.tensor_copy(GS[:, 0, :], ps[:, 5, 0:NT]).then_inc(sem("gs_ready"), 1)
                for j in range(JE):
                    act_mul(j)
                for c in range(KC):
                    dve.wait_ge(sem("scattered"), dve.snap(r * KC + (c + 1)))
                    v.tensor_tensor(X[:, c, :], ps[:, 6 + c % 2, 0:NT], X[:, c, :], ALU.add)\
                        .then_inc(sem("x_added"), 1)

            dispatch(0, 0, 0, "first")
            expert(0)
            with dve.Fori(1, E) as e:
                dispatch(e, 0, e, "later")
                expert(e)
            with dve.Fori(0, E) as e:
                for k in range(2):
                    i = dve.snap(e * 2 + k)
                    more = dve.value_load(plan[0:1, bass.ds(i, 1)], min_val=0, max_val=1)
                    with dve.If(more > 0):
                        r = dve.value_load(plan[0:1, bass.ds(i + 2 * E, 1)], min_val=E, max_val=E + 4)
                        dispatch(e, k + 1, r, "later")
                        expert(r)
            dve.drain()
            v.memset(cnt[:, 0:1], 0.0).then_inc(sem("moe_done"), 1)
            norm(4, G_FIN, sem("xn_ready"))
            dve.wait_ge(sem("xn_ready"), 5 * KC - 0)
            v.memset(cnt[:, 0:1], 0.0).then_inc(sem("out_ready"), 1)

        @block.tensor
        def _(pe):
            t_ = nc.tensor

            def norm(i):
                pe.wait_ge(sem("squared"), i + 1)
                for c in range(KC):
                    mm = t_.matmul(ps[:, 0, 0:NT], ones[:, :], TMP[:, c, :], start=(c == 0), stop=(c == KC - 1))
                mm.then_inc(sem("norm_summed"), 1)

            pe.wait_ge(sem("consts"), 5)
            norm(0)
            for hf in range(2):
                cs = slice(hf * CH, hf * CH + CH)
                pe.wait_ge(sem("xn_ready"), 8)
                pe.wait_ge(sem("root_ready"), 1)
                for k in range(G8):
                    if k >= 2:
                        pe.wait_ge(sem("u_ready"), 8 * hf + k - 1)
                    elif hf:
                        pe.wait_ge(sem("v_turned"), 4)
                    out = ps[:, k % 2, 0:CH * UC].rearrange("p (c n) -> p c n", c=CH)
                    for s in range(L):
                        w0 = 112 - 16 * s
                        mm = t_.matmul(out[:, :, 0:NB], sel[:, k, w0:w0 + P], XN[:, cs, s:TP:L],
                                       start=(s == 0), stop=(s == L - 1), skip_group_check=True)
                        if s == SMID:
                            mm = t_.matmul(out[:, :, NB:UC], sel[:, k, w0:w0 + P], XN[:, cs, TP:NT],
                                           start=False, stop=True, skip_group_check=True)
                    mm.then_inc(sem("u_moved"), 1)
                pe.wait_ge(sem("a_built"), hf + 1)

                def project(b):
                    bk = 6 if b % 2 == 0 else 0
                    if b == 0:
                        pe.wait_ge(sem("u_ready"), 8 * hf + 8)
                        if hf:
                            pe.wait_ge(sem("states_done"), 1)
                    elif b >= 2:
                        pe.wait_ge(sem("v_turned"), 4 * hf + b - 1)
                    pe.wait_ge(sem("at_ready"), 16 * hf + 4 * b + 4)
                    for g in range(8):
                        t_.matmul(ps[:, bk, g * UC:(g + 1) * UC], AT[:, g, 0:128], U[:, 8 * b + g, :],
                                  start=True, stop=True)
                        mm = t_.matmul(ps[:, bk + 1, g * UC:(g + 1) * UC], AT[:, g, 64:192], U[:, 8 * b + g, :],
                                       start=True, stop=True)
                    mm.then_inc(sem("v_made"), 1)

                for b in range(8):
                    if b >= 2:
                        pe.wait_ge(sem("at_ready"), 16 * hf + 2 * (b - 1))
                    elif hf:
                        pe.wait_ge(sem("y_ready"), 4)
                    for g in range(4):
                        mm = t_.transpose(ps[:, 4 + b % 2, g * P:(g + 1) * P], AM[:, 4 * b + g, :], ident[:, :])
                    mm.then_inc(sem("a_turned"), 1)
                    if b == 0:
                        pe.wait_ge(sem("c_built"), hf + 1)
                    if b >= 2:
                        pe.wait_ge(sem("toep_ready"), 8 * hf + b - 1)
                    elif hf:
                        pe.wait_ge(sem("h_ready"), 1)
                    for g in range(4):
                        mm = t_.matmul(ps[:, 2 + b % 2, g * P:(g + 1) * P], AM[:, 4 * b + g, :], CM[:, 4 * b + g, :],
                                       start=True, stop=True)
                    mm.then_inc(sem("toep_made"), 1)
                    if b % 2:
                        project(b // 2)
                pe.wait_ge(sem("scanned"), hf + 1)
                pe.wait_ge(sem("toep_ready"), 8 * hf + 8)
                for i in range(2):
                    t_.matmul(ps[:, 2 + i, :], swp[:, :], SV[:, 16 * i:16 * i + 16, :].rearrange("p g j -> p (g j)"),
                              start=True, stop=True).then_inc(sem("swapped"), 1)
                pe.wait_ge(sem("last_ready"), hf + 1)
                pe.wait_ge(sem("v_turned"), 4 * hf + 4)
                t_.matmul(ps[:, 7, 0:GH], swp[:, :], GL[:, :], start=True, stop=True).then_inc(sem("swapped"), 1)
                pe.wait_ge(sem("h_ready"), hf + 1)
                pe.wait_ge(sem("at_ready"), 16 * hf + 16)
                for b in range(4):
                    if b >= 2:
                        pe.wait_ge(sem("y_ready"), 4 * hf + b - 1)
                    for g in range(8):
                        out = ps[:, 4 + b % 2, g * UC:(g + 1) * UC]
                        t_.matmul(out, TM[:, 8 * b + g, :], U[:, 8 * b + g, :], start=True, stop=False)
                        mm = t_.matmul(out, CM[:, 8 * b + g, :], HM[:, 8 * b + g, :], start=False, stop=True)
                    mm.then_inc(sem("y_made"), 1)
                    if b == 3:
                        pe.wait_ge(sem("y_made"), 4 * hf + 4)
                        pe.sem_inc(sem("half_used"), 1)
            pe.wait_ge(sem("y_ready"), 8)
            yv = Y[:, :, :].rearrange("p (c k) n -> p k c n", k=G8)
            for s in range(L):
                if s >= 2:
                    pe.wait_ge(sem("y_mixed"), s - 1)
                cols = UC if s == SMID else NB
                out = ps[:, s % 2, 0:KC * cols].rearrange("p (c n) -> p c n", c=KC)
                for k in range(G8):
                    w0 = 112 - 16 * k
                    mm = t_.matmul(out, sel[:, s, w0:w0 + P], yv[:, k, :, 0:cols], start=(k == 0), stop=(k == G8 - 1))
                mm.then_inc(sem("y_moved"), 1)

            def pair(n, tile, rhs, wait, slot_n=None):
                pe.wait_ge(loaded[tile % RING], 16 * slot_loads(tile))
                if wait:
                    pe.wait_ge(*wait)
                w = raw[tile % RING]
                for i in range(2):
                    for k in range(KC):
                        mm = t_.matmul(ps[:, 2 * (n % 2) + i, 0:NT], w[:, (2 * k + i) * P:(2 * k + i + 1) * P],
                                       rhs[:, k, :], start=(k == 0), stop=(k == KC - 1))
                    if i == 0:
                        pass
                mm.then_inc(sem("pair_made"), 1)
                pe.wait_ge(sem("pair_made"), n + 1)
                pe.sem_inc(used, 1)

            pe.wait_ge(sem("z_ready"), 1)
            pe.wait_ge(sem("y_mixed"), 8)
            for n in range(8):
                pair(n, GLU0 + n, XN, (sem("pair_done"), n - 1) if n >= 2 else None)
            pe.wait_ge(sem("rel_loaded"), 32)
            pe.wait_ge(sem("outside_ready"), 1)
            t_.matmul(ps[0:NH, 7, 0:384], relx[:, :], oneh[:, :], start=True, stop=True).then_inc(sem("bias_made"), 1)
            norm(1)
            pe.wait_ge(sem("xn_ready"), 16)
            pe.wait_ge(sem("root_ready"), 2)
            for n in range(8, 8 + NF):
                pair(n, GU0 + n - 8, XN, (sem("pair_done"), n - 1))
            pe.wait_ge(sem("pair_done"), 30)
            for j in range(NF // 2):
                tile = DN0 + j
                pe.wait_ge(loaded[tile % RING], 16 * slot_loads(tile))
                w = raw[tile % RING]
                for k in range(2):
                    for c in range(KC):
                        mm = t_.matmul(ps[:, c, 0:NT], w[:, (k * KC + c) * P:(k * KC + c + 1) * P], FA[:, 2 * j + k, :],
                                       start=(j == 0 and k == 0), stop=(j == NF // 2 - 1 and k == 1))
                mm.then_inc(used, 1)
            pe.wait_ge(used, KV0)
            pe.sem_inc(sem("ffn_made"), 1)
            pe.wait_ge(sem("resid_ffn"), 8)
            norm(2)
            pe.wait_ge(sem("xn_ready"), 24)
            pe.wait_ge(sem("root_ready"), 3)
            pair(30, KV0, XN, None)
            tile = KV0 + 1
            pe.wait_ge(loaded[tile % RING], 16 * slot_loads(tile))
            for t in range(3):
                rows = P if t < 2 else TS
                for k in range(KC):
                    mm = t_.matmul(ps[0:rows, 4 + t, 0:256], XN[:, k, t * P:t * P + rows],
                                   raw[tile % RING][:, k * 256:(k + 1) * 256], start=(k == 0), stop=(k == KC - 1))
                mm.then_inc(sem("v_made2"), 1)
            pe.wait_ge(sem("v_made2"), 3)
            pe.sem_inc(used, 1)
            pe.wait_ge(sem("xq_ready"), 8)
            for n in range(31, 35):
                pair(n, Q0 + n - 31, FA, (sem("k_ready"), 2) if n < 33 else (sem("q_ready"), 2 * (n - 32)))
            pe.wait_ge(sem("q_ready"), 8)
            pe.wait_ge(sem("v_ready"), 3)

            def score(h):
                c, b = h // 2, h % 2
                rows = slice(64 * b, 64 * b + 64)
                if h >= 2:
                    pe.wait_ge(sem("s_read"), h - 1)
                kv = KT[rows, c // 4, :]
                t_.matmul(ps[:, b, 0:W], QT[rows, c, 0:W], kv[:, 0:W], start=True, stop=True)
                t_.matmul(ps[:, b, W:3 * W], QT[rows, c, W:TP], kv[:, 0:2 * W], start=True, stop=True)\
                    .then_inc(sem("s_made"), 1)

            def turn(h):
                b = h % 2
                pe.wait_ge(sem("p_ready"), 2 * h + 2 if h < NH else 2 * NH + 1)
                if h >= 2:
                    pe.wait_ge(sem("pt_ready"), h - 1)
                for i in range(3 if h < NH else 1):
                    mm = t_.transpose(ps[:, 2 + b, i * P:(i + 1) * P], SC[:, b, i * P:(i + 1) * P], ident[:, :])
                mm.then_inc(sem("p_turned"), 1)

            def mix(h):
                c, b = h // 2, h % 2
                rows = slice(64 * b, 64 * b + 64)
                g = 2 * (c // 4) + b
                pe.wait_ge(sem("pt_ready"), h + 1)
                if c >= 2 and b == 0:
                    pe.wait_ge(sem("o_ready"), c - 1)
                out = ps[rows, 4 + c % 2, :]
                vg = lambda t: VT[:, t, g * HD:(g + 1) * HD]
                t_.matmul(out[:, 0:W], vg(0), PTT[:, b, 0:W], start=True, stop=True)
                t_.matmul(out[:, W:TP], vg(0), PTT[:, b, W:2 * W], start=True, stop=False)
                t_.matmul(out[:, W:TP], vg(1), PTT[:, b, 2 * W:3 * W], start=False, stop=True)\
                    .then_inc(sem("pv_made"), 1)

            for h in range(NH):
                score(h)
                if h:
                    turn(h - 1)
                if h >= 2:
                    mix(h - 2)
            pe.wait_ge(sem("kc_ready"), 1)
            pe.wait_ge(sem("cache_loaded"), 16 * (TS + 2))
            for b in range(TS):
                for g in range(NKV):
                    rows = slice(64 * (g % 2), 64 * (g % 2) + 64)
                    c0 = (2 * b + g // 2) * R
                    mm = t_.matmul(ps[:, 6 + g % 2, c0:c0 + R], KCT[rows, b, g // 2, :],
                                   QT[rows, 4 * (g // 2):4 * (g // 2) + 4, TP + b], start=True, stop=True)
            mm.then_inc(sem("st_made"), 1)
            turn(NH - 1)
            mix(NH - 2)
            pe.wait_ge(sem("st_ready"), 2)
            pe.wait_ge(sem("s_read"), NH - 1)
            t_.transpose(ps[:, 0, 0:P], STS[:, :], ident[:, :]).then_inc(sem("s_made"), 1)
            mix(NH - 1)
            turn(NH)
            pe.wait_ge(sem("pt_ready"), NH + 1)
            for b in range(TS):
                for g in range(NKV):
                    rows = slice(64 * (g % 2), 64 * (g % 2) + 64)
                    out = ps[rows, 6, 0:KC * TS].rearrange("p (c b) -> p c b", c=KC)
                    mm = t_.matmul(out[:, 4 * (g // 2):4 * (g // 2) + 4, b], VC[:, b, g * HD:(g + 1) * HD],
                                   PTT[:, 0, b * NH + g * R:b * NH + g * R + R], start=True, stop=True)
            mm.then_inc(sem("os_made"), 1)
            pe.wait_ge(sem("o_ready"), KC + 1)
            for n in range(35, 39):
                pair(n, O0 + n - 35, OT,
                     (sem("pt_ready"), NH + 1) if n < 37 else (sem("resid_o"), 2 * (n - 36)))
            norm(3)
            pe.wait_ge(sem("xn_ready"), 32)
            pe.wait_ge(sem("root_ready"), 4)
            pe.wait_ge(sem("router_loaded"), 16)
            for t in range(3):
                rows = P if t < 2 else TS
                for k in range(KC):
                    mm = t_.matmul(ps[0:rows, 3, t * E:(t + 1) * E], XN[:, k, t * P:t * P + rows], WR[:, k, :],
                                   start=(k == 0), stop=(k == KC - 1))
            mm.then_inc(sem("logits_made"), 1)
            for t in range(3):
                rows = P if t < 2 else TS
                for hf in range(2):
                    if t:
                        pe.wait_ge(sem("ht_ready"), 2 * t + hf - 1)
                    for k in range(4):
                        mm = t_.transpose(ps[0:rows, 1 + hf, k * P:(k + 1) * P],
                                          XN[:, 4 * hf + k, t * P:t * P + rows], ident[:, :])
                    mm.then_inc(sem("h_turned"), 1)
            pe.wait_ge(sem("sel_ready"), 1)
            for t in range(3):
                rows = P if t < 2 else TS
                out = ps[0:rows, 4, t * E:(t + 1) * E]
                for u in range(t):
                    t_.matmul(out, ones[:, 0:rows], SELM[:, u, :], start=(u == 0), stop=False)
                t_.matmul(out, tri[0:rows, 0:rows], SELM[0:rows, t, :], start=(t == 0), stop=True)
            for t in range(3):
                rows = P if t < 2 else TS
                mm = t_.matmul(ps[0:1, 4, 3 * E:4 * E], ones[0:rows, 0:1], SELM[0:rows, t, :],
                               start=(t == 0), stop=(t == 2))
            mm.then_inc(sem("pos_made"), 1)
            pe.wait_ge(sem("ht_ready"), 6)
            pe.wait_ge(sem("plan_ready"), 1)

            def expert(r, first):
                pe.wait_ge(sem("gate_spread"), pe.snap(r * 3 + 3))
                if not first:
                    pe.wait_ge(sem("ye_ready"), pe.snap(r * 2))
                for t in range(3):
                    rows = P if t < 2 else TS
                    mm = t_.transpose(ps[:, 5, t * P:t * P + rows], DG[0:rows, t, :], ident[0:rows, 0:rows])
                mm.then_inc(sem("gate_turned"), 1)
                if not first:
                    pe.wait_ge(sem("x_added"), pe.snap(r * KC))
                for i in range(2):
                    for c in range(4):
                        for t in range(3):
                            rows = P if t < 2 else TS
                            mm = t_.matmul(ps[:, 6 + i, c * P:(c + 1) * P],
                                           HT[0:rows, t, (4 * i + c) * P:(4 * i + c + 1) * P],
                                           DSP[0:rows, 0, t, :], start=(t == 0), stop=(t == 2))
                    mm.then_inc(sem("gathered"), 1)
                pe.wait_ge(sem("xe_ready"), pe.snap(r * 2 + 2))

                def turn(j):
                    pe.wait_ge(sem("act_ready"), pe.snap(r * JE + (j + 1)))
                    if j >= 2:
                        pe.wait_ge(sem("af_ready"), pe.snap(r * JE + (j - 1)))
                    for i in range(4):
                        mm = t_.transpose(ps[:, 6 + j % 2, i * P:(i + 1) * P], AC[:, j % 2, i * P:(i + 1) * P],
                                          ident[:, :])
                    mm.then_inc(sem("act_turned"), 1)

                def arrived(m):
                    n = NDENSE + m
                    pe.wait_ge(loaded[n % RING], pe.snap(r * (16 * NE // RING) + 16 * slot_loads(n)))
                    return raw[n % RING]

                for j in range(JE):
                    if j >= 2:
                        pe.wait_ge(sem("act_ready"), pe.snap(r * JE + (j - 1)))
                    for kq in range(4):
                        w = arrived(4 * j + kq)
                        for k in range(2):
                            for i in range(2):
                                mm = t_.matmul(ps[:, 2 * (j % 2) + i, :], XE[:, 0, 2 * kq + k, :],
                                               w[:, (2 * k + i) * 512:(2 * k + i + 1) * 512],
                                               start=(kq == 0 and k == 0), stop=(kq == 3 and k == 1))
                        mm.then_inc(used, 1)
                    pe.wait_ge(used, pe.snap(r * NE + (NDENSE + 4 * j + 4)))
                    pe.sem_inc(sem("gu_made"), 1)
                    if j:
                        turn(j - 1)
                turn(JE - 1)
                pe.wait_ge(sem("gs_ready"), r + 1)
                for m in range(NDE):
                    w = arrived(NGU + m)
                    pe.wait_ge(sem("af_ready"), pe.snap(r * JE + (m // 2 + 1)))
                    for k in range(2):
                        for i in range(2):
                            mm = t_.matmul(ps[:, 4 + i, :], AF[:, 2 * m + k, :],
                                           w[:, (2 * k + i) * 512:(2 * k + i + 1) * 512],
                                           start=(m == 0 and k == 0), stop=(m == NDE - 1 and k == 1))
                    mm.then_inc(used, 1)
                pe.wait_ge(used, pe.snap(r * NE + (NDENSE + NE)))
                pe.sem_inc(sem("down_made"), 1)
                pe.wait_ge(sem("ye_ready"), pe.snap(r * 2 + 2))
                for c in range(KC):
                    if c >= 2:
                        pe.wait_ge(sem("x_added"), pe.snap(r * KC + (c - 1)))
                    t_.matmul(ps[:, 6 + c % 2, 0:NT], YE[:, c * P:(c + 1) * P], GS[:, 0, :], start=True, stop=True)\
                        .then_inc(sem("scattered"), 1)

            expert(0, True)
            with pe.Fori(1, E) as e:
                expert(e, False)
            with pe.Fori(0, 2 * E) as i:
                more = pe.value_load(plan[0:1, bass.ds(i, 1)], min_val=0, max_val=1)
                with pe.If(more > 0):
                    r = pe.value_load(plan[0:1, bass.ds(i + 2 * E, 1)], min_val=E, max_val=E + 4)
                    expert(r, False)
            norm(4)
            pe.wait_ge(sem("root_ready"), 5)


def _tiles(w, outs, pair):
    v = w.reshape(KC, P, -1)
    return [np.stack([v[:, :, a:a + P], v[:, :, b:b + P]], 2).transpose(1, 0, 2, 3).reshape(P, TILE)
            for a, b in pair]


def kernel(**inp):
    import concourse.bacc as bacc
    from concourse.bass_utils import run_bass_kernel_spmd

    a = {k: np.asarray(v) for k, v in inp.items()}
    c8 = lambda v: v.reshape(KC, P).T
    x = np.concatenate([a["x_prompt"].reshape(TP, D), a["x_sample"].reshape(TS, D)], 0)
    xT = x.T.reshape(KC, P, NT).transpose(1, 0, 2)
    vecs = np.stack([c8(v) for v in (a["g_mix"][0], a["g_mix"][1], a["g_ffn"][0], a["g_ffn"][1],
                                     a["g_kv"], a["g_final"], a["ssm_d"][0])], 1)
    cols = np.concatenate([np.arange(h * HD, (h + 1) * HD) for h in HEADS])
    wq, wo = a["w_q"][0][:, cols], a["w_o"][0][cols, :]
    wdn = a["w_ffn_down"][0].reshape(NF // 2, 2, P, D).transpose(0, 2, 1, 3).reshape(NF // 2, P, TILE)
    wkv = a["w_kv"]
    wv = wkv[:, 256:].reshape(KC, P, 256).transpose(1, 0, 2).reshape(P, TILE)
    wd = np.stack(
        _tiles(a["w_glu"][0], None, [(j * P, D + j * P) for j in range(KC)])
        + _tiles(a["w_ffn_gate_up"][0], None, [(j * P, DFF + j * P) for j in range(NF)])
        + list(wdn)
        + _tiles(wkv, None, [(0, P)]) + [wv]
        + _tiles(wq, None, [(2 * j * P, (2 * j + 1) * P) for j in range(4)])
        + _tiles(wo, None, [(2 * j * P, (2 * j + 1) * P) for j in range(4)]), 0)
    gu = a["w_exp_gate_up"][0].reshape(E, 4, 2, P, 2, JE, 512).transpose(0, 5, 1, 3, 2, 4, 6)
    dn = a["w_exp_down"][0].reshape(E, NDE, 2, P, D).transpose(0, 1, 3, 2, 4)
    we = np.concatenate([gu.reshape(E, NGU, P, TILE), dn.reshape(E, NDE, P, TILE)], 1).reshape(E * NE, P, TILE)
    wr = a["w_router"][0].reshape(KC, P, E).transpose(1, 0, 2)
    br, bi = (a[k][0].transpose(1, 0, 2) for k in ("ssm_b_re", "ssm_b_im"))
    cr, ci = (a[k][0].transpose(2, 0, 1) for k in ("ssm_c_re", "ssm_c_im"))
    hr, hi = (a[k][0].transpose(2, 1, 0) for k in ("state_ssm_re", "state_ssm_im"))
    dist = 255 - np.arange(384)
    large = 16 + (np.log(np.maximum(dist, 1).astype(np.float32) / 16) / math.log(8) * 16).astype(np.int32)
    bucket = np.where(dist < 16, dist, np.minimum(large, NBUCK - 1))
    bucket = np.where((dist >= 0) & (dist < W), bucket, NBUCK)
    onehot = (np.arange(NBUCK + 1)[:, None] == bucket[None]).astype(np.float32)
    ins = {
        "xT": xT, "vecs": vecs, "wd": wd, "we": we, "wr": wr,
        "a_re": a["ssm_a_re"][0].T, "a_im": a["ssm_a_im"][0].T, "log_dt": a["ssm_log_dt"],
        "bq": np.concatenate([br, bi], 0), "bx": np.concatenate([bi, br], 0),
        "cq": np.concatenate([cr, ci], 0), "cx": np.concatenate([ci, cr], 0),
        "h0q": np.concatenate([hr, hi], 0), "h0x": np.concatenate([hi, hr], 0),
        "kcT": a["cache_k_win"].reshape(TS, W, 2, P).transpose(0, 3, 2, 1),
        "vc": a["cache_v_win"].reshape(TS, W, 256).transpose(1, 0, 2),
        "sinks": a["attn_sinks"], "relb": a["rel_bias"], "onehot": onehot,
    }
    outs = {"yT": (P, KC, NT), "hp": (P, G), "hs": (P, G, TS), "kp": (P, 2, W), "vp": (P, 256),
            "ks": (P, TS, 2, W), "vs": (P, TS, 256)}
    nc = bacc.Bacc("TRN2", target_bir_lowering=False, num_devices=1)
    arrays, args = {}, []
    for name, v in ins.items():
        arrays["in_" + name] = np.ascontiguousarray(v)
        args.append(nc.dram_tensor("in_" + name, v.shape, F32, kind="ExternalInput").ap())
    for name, shape in outs.items():
        args.append(nc.dram_tensor("out_" + name, shape, F32, kind="ExternalOutput").ap())
    build(nc, *args)
    o = run_bass_kernel_spmd(nc, [arrays], core_ids=[0]).results[0]
    y = o["out_yT"].transpose(1, 0, 2).reshape(D, NT).T
    hp, hs = o["out_hp"], o["out_hs"]
    st = lambda v: v.transpose(2, 1, 0)[None]
    return (y[:TP].reshape(1, TP, D), y[TP:].reshape(TS, 1, D),
            hp[:S].T.reshape(1, 1, G, S), hp[S:].T.reshape(1, 1, G, S),
            o["out_kp"].transpose(2, 1, 0).reshape(1, W, NKV, HD), o["out_vp"].reshape(1, W, NKV, HD),
            st(hs[:S]), st(hs[S:]),
            o["out_ks"].transpose(1, 3, 2, 0).reshape(TS, W, NKV, HD),
            o["out_vs"].transpose(1, 0, 2).reshape(TS, W, NKV, HD))
```

```python
from contextlib import ExitStack
import math

import numpy as np
import concourse.bass as bass
from concourse import mybir

F32 = mybir.dt.float32
F32R = mybir.dt.float32r
I32 = mybir.dt.int32
ALU = mybir.AluOpType
ACT = mybir.ActivationFunctionType
AX_X = mybir.AxisListType.X

P = 128
D = 1024
KC = D // P
TP, TS = 256, 8
NT = TP + TS
G, H, S = 64, 16, 64
L = 8
NB = TP // L
UC = NB + TS
SMID = 4
GH = G // 2
CH = KC // 2
G8 = P // H
NH, NKV, HD, R = 16, 4, 64, 4
W = 128
NBUCK = 32
SCALE = 1.0 / math.sqrt(HD)
NEG = -1e30
DFF = 2816
E, DFE = 8, 3584
EPS = 1e-6
TILE = 2048
NF = DFF // P
GLU0, GU0, DN0, KV0, Q0, O0, NDENSE = 0, 8, 30, 41, 43, 47, 51
JE, NGU, NDE = DFE // 512, 28, 14
NE = NGU + NDE
RING = 6
SPLIT = 3
EARLY = 3
BANK = 512
TWO_PI_HI = 6.28125
TWO_PI_LO = 2 * math.pi - TWO_PI_HI
MAGIC = 1.5 * 2.0 ** 23
PI_IN = 3.1415925
HEADS = [(2 * gp + b) * R + r for gp in range(2) for r in range(R) for b in range(2)]
G_MIX0, G_MIX1, G_FFN0, G_FFN1, G_KV, G_FIN, SSM_D = range(7)


def build(nc, xT, vecs, wd, we, wr, a_re, a_im, log_dt, bq, bx, cq, cx, h0q, h0x,
          kcT, vc, sinks, relb, onehot,
          yT, hp_out, hs_out, kp_out, vp_out, ks_out, vs_out):
    with ExitStack() as ctx:
        cur = [ctx]

        def sb(name, shape, dt=F32):
            return cur[0].enter_context(nc.sbuf_tensor(name, shape, dt))

        sems = {}

        def sem(name):
            if name not in sems:
                sems[name] = ctx.enter_context(nc.semaphore(name))
            return sems[name]

        ps = ctx.enter_context(nc.psum_tensor("ps", [P, 8, BANK], F32))
        bias_dram = nc.dram_tensor("bias_rows", (NH, P, 384), F32).ap()

        X = sb("X", [P, KC, NT])

        def in_one_place(*tensors):
            for t in tensors:
                with ExitStack() as own:
                    cur[0] = own if t is not tensors[-1] else ctx
                    made = [sb(*a) for a in t]
                yield made if len(made) > 1 else made[0]
            cur[0] = ctx

        XN, (XEH, XEL), XNL = in_one_place(
            [("XN", [P, KC, NT])], [("XEH", [P, KC, P], F32R), ("XEL", [P, KC, P], F32R)],
            [("XNL", [P, KC, NT], F32R)])
        TMP, (YEH, YEL), XNH = in_one_place(
            [("TMP", [P, KC, NT])], [("YEH", [P, D], F32R), ("YEL", [P, D], F32R)],
            [("XNH", [P, KC, NT], F32R)])
        rstd = sb("rstd", [P, NT])
        root = sb("root", [P, NT])
        vec = sb("vec", [P, 7, KC])
        ones = sb("ones", [P, P])
        ident = sb("ident", [P, P])
        epsb = sb("epsb", [P, 1])
        halfpi = sb("halfpi", [P, 1])
        raw = [sb(f"raw{i}", [P, TILE]) for i in range(EARLY)]

        ssm = ExitStack()
        cur[0] = ssm
        swp = sb("swp", [P, P])
        sel = sb("sel", [P, 8, 240])
        tmask = sb("tmask", [P, P])
        sgn = sb("sgn", [P, 1])
        nsgn = sb("nsgn", [P, 1])
        kramp = sb("kramp", [P, 9])
        jramp = sb("jramp", [P, NB])
        are, aim, dtt = sb("are", [P, G]), sb("aim", [P, G]), sb("dtt", [P, G])
        BQ, BX, CQ, CX = (sb(n, [P, GH, H]) for n in ("BQ", "BX", "CQ", "CX"))
        H0Q, H0X = sb("H0Q", [P, G, TS]), sb("H0X", [P, G, TS])
        q = [sb(f"q{i}", [P, G]) for i in range(14)]
        MT = sb("MT", [P, 9, G])
        T9 = [sb(f"t9{i}", [P, 9, G]) for i in range(2)]
        ER, EI = sb("ER", [P, 9, G]), sb("EI", [P, 9, G])
        TA, TB, TC = (sb(n, [P, GH, NB]) for n in ("TA", "TB", "TC"))
        COS, SS = sb("COS", [P, GH, NB]), sb("SS", [P, GH, NB])
        AM, CM, TM = sb("AM", [P, GH, P]), sb("CM", [P, GH, P]), sb("TM", [P, GH, P])
        PT = sb("PT", [P, GH, H])
        CT = sb("CT", [P, GH, H])
        AT = sb("AT", [P, 8, 192])
        U = sb("U", [P, GH, UC])
        WV = sb("WV", [P, 1 + GH * NB])
        R8 = sb("R8", [P, GH, NB])
        SV = sb("SV", [P, GH, NB])
        VS = sb("VS", [P, GH, TS])
        HM = sb("HM", [P, GH, UC])
        GL = sb("GL", [P, GH])
        HP = sb("HP", [P, G])
        HS = sb("HS", [P, G, TS])
        Y = sb("Y", [P, G, UC])
        ssm.close()

        cur[0] = ctx
        raw += [sb(f"raw{i}", [P, TILE]) for i in range(EARLY, RING)]
        WH = [sb(f"WH{i}", [P, TILE], F32R) for i in range(SPLIT)]
        WL = [sb(f"WL{i}", [P, TILE], F32R) for i in range(SPLIT)]
        WR = sb("WR", [P, KC, E])
        tri = sb("tri", [P, P])
        slot = sb("slot", [P, 3, P])
        LG = sb("LG", [P, 3, E])
        dz = sb("dz", [P, 3, E])
        attn = ExitStack()
        inner = ExitStack()
        cur[0] = inner
        QT = sb("QT", [P, KC, NT])
        KCT = sb("KCT", [P, TS, 2, W])
        VC = sb("VC", [P, TS, NKV * HD])
        with ExitStack() as a1:
            cur[0] = a1
            XQ, XQH = sb("XQ", [P, KC, NT]), sb("XQH", [P, KC, NT], F32R)
        with ExitStack() as a1:
            cur[0] = a1
            XQL = sb("XQL", [P, KC, NT], F32R)
        cur[0] = inner
        OTH, OTL = sb("OTH", [P, KC, NT], F32R), sb("OTL", [P, KC, NT], F32R)
        inner.close()
        cur[0] = attn
        FAH = sb("FAH", [P, NF, NT], F32R)
        FAL = sb("FAL", [P, NF, NT], F32R)
        SG = sb("SG", [P, 2, NT])
        KT = sb("KT", [P, 2, NT])
        VT = sb("VT", [P, 3, NKV * HD])
        BIAS = sb("BIAS", [P, NH, 2 * W])
        BSM = sb("BSM", [P, W])
        relx = sb("relx", [NBUCK + 1, NH])
        oneh = sb("oneh", [NBUCK + 1, 384])
        brow = sb("brow", [NH, 384])
        SINK = sb("SINK", [P, NH])
        SINKC = sb("SINKC", [P, 1])
        SC = sb("SC", [P, 2, 384])
        mx = sb("mx", [P, 2, 2])
        nm = sb("nm", [P, 2, 2])
        sm = sb("sm", [P, 2, 2])
        es = sb("es", [P, 2, 2])
        rd = sb("rd", [P, 2, 2])
        PTT = sb("PTT", [P, 2, 384])
        STS = sb("STS", [P, P])
        attn.close()
        cur[0] = ctx
        r1, r2, r3, r4 = (sb(f"r{i}", [P, 3, E]) for i in range(1, 5))
        top = sb("top", [P, 3, 8])
        v1 = sb("v1", [P, 3])
        SELM = sb("SELM", [P, 3, E])
        GATE = sb("GATE", [P, 3, E])
        POS = sb("POS", [P, 3, E])
        cnt = sb("cnt", [1, 2 * E])
        run = sb("run", [1, 2 * E + 1])
        plan = sb("plan", [1, 4 * E + 1], I32)
        HTH, HTL = sb("HTH", [P, 3, D], F32R), sb("HTL", [P, 3, D], F32R)
        DSP = sb("DSP", [P, 3, P], F32R)
        DG = sb("DG", [P, 3, P])
        GSH, GSL = sb("GSH", [P, NT], F32R), sb("GSL", [P, NT], F32R)
        SIL = sb("SIL", [P, 2, BANK])
        AC = sb("AC", [P, 2, BANK])
        AFH, AFL = sb("AFH", [P, DFE // P, P], F32R), sb("AFL", [P, DFE // P, P], F32R)

        block = ctx.enter_context(nc.Block())

        def at(eng, tile, step=0, per=1):
            r, stride, c = tile
            value = c + step
            return per * value if r is None else eng.snap(r * (stride * per) + per * value)

        def loads(eng, tile):
            r, stride, c = tile
            value = 16 * (c // RING + 1)
            return value if r is None else eng.snap(r * (16 * stride // RING) + value)

        def dense(n):
            return (None, 0, n)

        def expert_tile(r, m):
            return (r, NE, NDENSE + m)

        def after(tile, k):
            r, stride, c = tile
            return (r, stride, c + k)

        def tokens(t):
            return P if t < 2 else TS

        loaded = [sem(f"tile_loaded_{i}") for i in range(RING)]
        split = sem("tiles_split")
        used = sem("tiles_used")
        PAIRS = 6
        TURNS = NF // PAIRS

        @block.sync
        def _(sp):
            sp.dma_start(X[:, :, :], xT).then_inc(sem("x_loaded"), 16)
            sp.dma_start(vec[:, :, :], vecs).then_inc(sem("vec_loaded"), 16)
            for half in range(2):
                rows = slice(64 * half, 64 * half + 64)
                sp.dma_start(are[rows, :], a_re).then_inc(sem("lam_loaded"), 16)
                sp.dma_start(aim[rows, :], a_im).then_inc(sem("lam_loaded"), 16)
            sp.dma_start(dtt[:, :], log_dt.to_broadcast([P, G])).then_inc(sem("lam_loaded"), 16)
            sp.dma_start(H0Q[:, :, :], h0q).then_inc(sem("h0_loaded"), 16)
            sp.dma_start(H0X[:, :, :], h0x).then_inc(sem("h0_loaded"), 16)
            for hf in range(2):
                gs = slice(hf * GH, hf * GH + GH)
                if hf == 1:
                    sp.wait_ge(sem("a_built"), 1)
                sp.dma_start(BQ[:, :, :], bq[:, gs, :]).then_inc(sem("b_loaded"), 16)
                sp.dma_start(BX[:, :, :], bx[:, gs, :]).then_inc(sem("b_loaded"), 16)
                if hf == 1:
                    sp.wait_ge(sem("c_built"), 1)
                sp.dma_start(CQ[:, :, :], cq[:, gs, :]).then_inc(sem("c_loaded"), 16)
                sp.dma_start(CX[:, :, :], cx[:, gs, :]).then_inc(sem("c_loaded"), 16)
                if hf == 0:
                    for n in range(EARLY):
                        sp.dma_start(raw[n][:, :], wd[n]).then_inc(loaded[n], 16)
            sp.wait_ge(sem("states_done"), 2)
            sp.dma_start(hp_out, HP[:, :]).then_inc(sem("stored"), 16)
            sp.dma_start(hs_out, HS[:, :, :]).then_inc(sem("stored_ssm"), 16)
            sp.wait_ge(sem("stored"), 16)
            sp.wait_ge(sem("stored_ssm"), 16)
            sp.wait_ge(sem("y_mixed"), 8)
            for n in range(EARLY, RING):
                sp.dma_start(raw[n][:, :], wd[n]).then_inc(loaded[n], 16)

            def load(tile, src):
                free = at(sp, tile, 1 - RING)
                sp.wait_ge(split, free)
                sp.dma_start(raw[tile[2] % RING][:, :], src).then_inc(loaded[tile[2] % RING], 16)

            turns = NDENSE // RING - 1
            with sp.Fori(0, turns) as r:
                for i in range(RING):
                    load((r, RING, RING + i), wd[bass.ds(r * RING + (RING + i), 1)].rearrange("a p n -> (a p) n"))
            for n in range((turns + 1) * RING, NDENSE):
                load(dense(n), wd[n])

            def expert_tiles(e, r):
                for m in range(NE):
                    load(expert_tile(r, m), we[bass.ds(e * NE + m, 1)].rearrange("a p n -> (a p) n"))

            with sp.Fori(0, E) as e:
                expert_tiles(e, e)
            sp.wait_ge(sem("plan_ready"), 1)
            with sp.Fori(0, E) as e:
                for k in range(2):
                    i = sp.snap(e * 2 + k)
                    more = sp.value_load(plan[0:1, bass.ds(i, 1)], min_val=0, max_val=1)
                    with sp.If(more > 0):
                        r = sp.value_load(plan[0:1, bass.ds(i + 2 * E, 1)], min_val=E, max_val=E + 4)
                        expert_tiles(e, r)
            sp.wait_ge(sem("out_ready"), 1)
            sp.dma_start(yT, XN[:, :, :]).then_inc(sem("stored"), 16)
            sp.wait_ge(sem("stored"), 32)

        @block.gpsimd
        def _(pool):
            g = nc.gpsimd
            g.memset(ones[:, :], 1.0).then_inc(sem("pool_step"), 1)
            g.memset(epsb[:, :], EPS).then_inc(sem("pool_step"), 1)
            g.memset(halfpi[:, :], math.pi / 2).then_inc(sem("pool_step"), 1)
            g.memset(sel[:, :, :], 0.0).then_inc(sem("pool_step"), 1)
            g.iota(kramp[:, :], pattern=[[1, 9]], base=-4, channel_multiplier=0,
                   allow_small_or_imprecise_dtypes=True).then_inc(sem("pool_step"), 1)
            g.iota(jramp[:, :], pattern=[[1, NB]], base=0, channel_multiplier=0,
                   allow_small_or_imprecise_dtypes=True).then_inc(sem("pool_step"), 1)
            pool.wait_ge(sem("pool_step"), 6)
            g.affine_select(out=ident[:, :], in_=ones[:, :], compare_op=ALU.is_equal, fill=0.0, base=0,
                            pattern=[[-1, P]], channel_multiplier=1).then_inc(sem("consts"), 1)
            g.affine_select(out=swp[:, 0:64], in_=ones[:, 0:64], compare_op=ALU.is_equal, fill=0.0, base=-64,
                            pattern=[[-1, 64]], channel_multiplier=1).then_inc(sem("consts"), 1)
            g.affine_select(out=swp[:, 64:128], in_=ones[:, 0:64], compare_op=ALU.is_equal, fill=0.0, base=0,
                            pattern=[[-1, 64]], channel_multiplier=1).then_inc(sem("consts"), 1)
            g.affine_select(out=sel[:, :, 112:128], in_=ones[:, :].rearrange("p (m x) -> p m x", m=8),
                            compare_op=ALU.is_equal, fill=0.0, base=0, pattern=[[-16, 8], [-1, 16]],
                            channel_multiplier=1).then_inc(sem("consts"), 1)
            g.affine_select(out=tmask[:, :], in_=ones[:, :], compare_op=ALU.is_ge, fill=0.0, base=15,
                            pattern=[[16, 8], [0, 16]], channel_multiplier=-1).then_inc(sem("consts"), 1)
            pool.wait_ge(sem("consts"), 5)
            pool.wait_ge(sem("pow_ready"), 1)
            n = 0
            for hf in range(2):
                gs = slice(hf * GH, hf * GH + GH)
                pool.wait_ge(sem("c_loaded"), 32 * (hf + 1))
                if hf == 1:
                    pool.wait_ge(sem("half_used"), 1)
                for s in range(L):
                    fr = T9[0][:, s, gs].unsqueeze(2).to_broadcast([P, GH, H])
                    fs = T9[1][:, s, gs].unsqueeze(2).to_broadcast([P, GH, H])
                    out = CM[:, :, s * H:(s + 1) * H]
                    if n:
                        pool.wait_ge(sem("c_step"), n)
                    g.tensor_tensor(out, CQ[:, :, :], fr, ALU.mult).then_inc(sem("c_step"), 1)
                    g.tensor_tensor(CT[:, :, :], CX[:, :, :], fs, ALU.mult).then_inc(sem("c_step"), 1)
                    n += 2
                    pool.wait_ge(sem("c_step"), n)
                    ins = g.tensor_tensor(out, out, CT[:, :, :], ALU.add)
                    if s < L - 1:
                        ins.then_inc(sem("c_step"), 1)
                        n += 1
                    else:
                        ins.then_inc(sem("c_built"), 1)
                        pool.wait_ge(sem("c_built"), hf + 1)
            pool.wait_ge(sem("y_mixed"), 8)
            g.affine_select(out=tri[:, :], in_=ones[:, :], compare_op=ALU.is_gt, fill=0.0, base=0,
                            pattern=[[1, P]], channel_multiplier=-1).then_inc(sem("route_consts"), 1)
            g.iota(slot[:, :, :], pattern=[[P, 3], [1, P]], base=0, channel_multiplier=0,
                   allow_small_or_imprecise_dtypes=True).then_inc(sem("route_consts"), 1)
            g.memset(LG[:, :, :], 0.0).then_inc(sem("route_consts"), 1)
            g.memset(dz[:, :, :], 1.0).then_inc(sem("route_consts"), 1)
            pool.wait_ge(sem("route_consts"), 4)
            g.memset(dz[:, :, 0:1], 0.0).then_inc(sem("route_consts"), 1)
            pool.dma_start(relx[0:NBUCK, :], relb).then_inc(sem("rel_loaded"), 16)
            pool.dma_start(oneh[:, :], onehot).then_inc(sem("rel_loaded"), 16)
            pool.dma_start(SINK[:, :], sinks.to_broadcast([P, NH])).then_inc(sem("sink_loaded"), 16)
            for b in range(TS):
                pool.dma_start(SINKC[b * NH:(b + 1) * NH, :], sinks.rearrange("a h -> h a"))\
                    .then_inc(sem("sink_loaded"), 16)
            pool.dma_start(WR[:, :, :], wr).then_inc(sem("router_loaded"), 16)
            pool.wait_ge(sem("bias_rows_ready"), 1)
            pool.dma_start(bias_dram, brow[:, :].unsqueeze(1).to_broadcast([NH, P, 384]))\
                .then_inc(sem("bias_stored"), 16)
            pool.wait_ge(sem("bias_stored"), 16)
            for h in range(NH):
                src = bias_dram[h, :, 127:127 + 2 * W]
                src = bass.AP(src.tensor, src.offset, [[384 - 1, P], [1, 2 * W]])
                pool.dma_start(BIAS[:, h, :], src).then_inc(sem("bias_loaded"), 16)
            for b in range(TS):
                pool.dma_start(BSM[b * NH:(b + 1) * NH, :], bias_dram[:, 0, W:2 * W]).then_inc(sem("bias_loaded"), 16)

            pool.wait_ge(used, KV0)
            for b in range(TS):
                pool.dma_start(KCT[:, b, :, 0:W - 1], kcT[b][:, :, 1:W]).then_inc(sem("cache_loaded"), 16)
            pool.dma_start(VC[0:W - 1, :, :], vc[1:W]).then_inc(sem("cache_loaded"), 16)
            pool.wait_ge(sem("v_ready"), 3)
            pool.dma_start(VC[W - 1:W, :, :], VT[P - TS:P, 2, :]).then_inc(sem("new_v_loaded"), 16)
            pool.wait_ge(sem("cache_loaded"), 16 * (TS + 1))
            pool.wait_ge(sem("new_v_loaded"), 16)
            pool.wait_ge(sem("kc_ready"), 1)
            pool.dma_start(kp_out, KT[:, :, TP - W:TP]).then_inc(sem("kv_stored"), 16)
            pool.dma_start(vp_out, VT[:, 1, :]).then_inc(sem("kv_stored"), 16)
            pool.dma_start(ks_out, KCT[:, :, :, :]).then_inc(sem("kv_stored"), 16)
            pool.dma_start(vs_out, VC[:, :, :]).then_inc(sem("kv_stored"), 16)
            pool.wait_ge(sem("kv_stored"), 64)

        @block.scalar
        def _(act):
            a = nc.scalar

            def norm(i, ready, n_ready):
                act.wait_ge(ready, n_ready)
                if i:
                    act.wait_ge(sem("norm_summed"), i)
                a.activation(TMP[:, :, :], X[:, :, :], ACT.Square).then_inc(sem("squared"), 1)
                act.wait_ge(sem("norm_summed"), i + 1)
                if i:
                    act.wait_ge(sem("rstd_ready"), i)
                else:
                    act.wait_ge(sem("consts"), 5)
                a.activation(root[:, :], ps[:, 0, 0:NT], ACT.Sqrt, bias=epsb[:, :], scale=1.0 / D)\
                    .then_inc(sem("root_ready"), 1)

            act.wait_ge(sem("lam_loaded"), 80)
            a.activation(q[0][:, :], dtt[:, :], ACT.Tanh, scale=1.0 / 32).then_inc(sem("tanh_ready"), 1)
            norm(0, sem("x_loaded"), 16)
            act.wait_ge(sem("decay_ready"), 1)
            a.activation(q[3][:, :], q[1][:, :], ACT.Tanh, scale=0.5).then_inc(sem("tanh_ready"), 1)
            act.wait_ge(sem("phase9_ready"), 1)
            a.activation(EI[:, :, :], T9[0][:, :, :], ACT.Sin).then_inc(sem("sin9_ready"), 1)
            a.activation(ER[:, :, :], T9[0][:, :, :], ACT.Abs).then_inc(sem("sin9_ready"), 1)
            a.activation(q[6][:, :], q[4][:, :], ACT.Sin, scale=0.5).then_inc(sem("sin9_ready"), 1)
            act.wait_ge(sem("sin9_ready"), 3)
            a.activation(ER[:, :, :], ER[:, :, :], ACT.Sin, scale=-1.0, bias=halfpi[:, :])\
                .then_inc(sem("sin9_ready"), 1)
            for hf in range(2):
                act.wait_ge(sem("phase_ready"), hf + 1)
                if hf:
                    act.wait_ge(sem("states_done"), 1)
                a.activation(SS[:, :, :], TA[:, :, :], ACT.Sin, scale=sgn[:, :]).then_inc(sem("turn_ready"), 1)
                a.activation(COS[:, :, :], TA[:, :, :], ACT.Abs).then_inc(sem("turn_ready"), 1)
                act.wait_ge(sem("turn_ready"), 3 * hf + 2)
                a.activation(COS[:, :, :], COS[:, :, :], ACT.Sin, scale=-1.0, bias=halfpi[:, :])\
                    .then_inc(sem("turn_ready"), 1)
                if hf:
                    act.wait_ge(sem("y_made"), 4)
                for k in range(G8):
                    act.wait_ge(sem("u_moved"), 8 * hf + k + 1)
                    a.copy(U[:, :, :].rearrange("p (c k) n -> p k c n", k=G8)[:, k],
                           ps[:, k % 2, 0:CH * UC].rearrange("p (c n) -> p c n", c=CH)).then_inc(sem("u_ready"), 1)
                for b in range(GH // 4):
                    act.wait_ge(sem("a_turned"), 8 * hf + b + 1)
                    if 8 * hf + b >= 2:
                        act.wait_ge(sem("v_made"), (8 * hf + b) // 2)
                    dst = AT[:, 4 * (b % 2):4 * (b % 2) + 4, :]
                    src = ps[:, 4 + b % 2, :].rearrange("p (g n) -> p g n", g=4)
                    a.copy(dst[:, :, 0:128], src).then_inc(sem("at_ready"), 1)
                    a.copy(dst[:, :, 128:192], src[:, :, 0:64]).then_inc(sem("at_ready"), 1)
                for b in range(4):
                    act.wait_ge(sem("y_made"), 4 * hf + b + 1)
                    a.copy(Y[:, hf * GH + 8 * b:hf * GH + 8 * b + 8, :],
                           ps[:, 4 + b % 2, 0:8 * UC].rearrange("p (g n) -> p g n", g=8)).then_inc(sem("y_ready"), 1)
            act.wait_ge(sem("y_mixed"), 8)
            def hi(tile):
                slot_ = tile[2] % RING
                act.wait_ge(loaded[slot_], loads(act, tile))
                if tile[0] is not None or tile[2] >= SPLIT:
                    act.wait_ge(used, at(act, tile, 1 - SPLIT))
                a.copy(WH[tile[2] % SPLIT][:, :], raw[slot_][:, :]).then_inc(sem("hi_made"), 1)

            def xn_hi(i, dst, src, ready, n_ready):
                for k in range(2):
                    act.wait_ge(ready, n_ready[k])
                    c4 = slice(4 * k, 4 * k + 4)
                    a.copy(dst[:, c4, :], src[:, c4, :]).then_inc(sem("xn_hi_made"), 1)

            for k in range(2):
                c4 = slice(4 * k, 4 * k + 4)
                a.activation(XN[:, c4, :], TMP[:, c4, :], ACT.Gelu_apprx_tanh).then_inc(sem("z_ready"), 1)
            xn_hi(0, XNH, XN, sem("z_ready"), (1, 2))
            for n in range(SPLIT):
                hi(dense(n))

            def gate(tile, func, first):
                b = tile[2] % 2
                act.wait_ge(used, at(act, tile, 1))
                if tile[0] is not None or tile[2] >= 2:
                    act.wait_ge(sem("pair_done"), at(act, tile, -1))
                a.activation(SG[:, b, :], ps[:, 2 * b + first, 0:NT], func).then_inc(sem("gated"), 1)
                hi(after(tile, SPLIT))

            for n in range(GU0):
                gate(dense(n), ACT.Sigmoid, 1)
            act.wait_ge(sem("bias_made"), 1)
            a.copy(brow[:, :], ps[0:NH, 7, 0:384]).then_inc(sem("bias_rows_ready"), 1)
            norm(1, sem("pair_done"), 8)
            xn_hi(1, XNH, XN, sem("xn_ready"), (2 * KC - 4, 2 * KC))
            with act.Fori(0, TURNS) as r:
                for i in range(PAIRS):
                    gate((r, PAIRS, GU0 + i), ACT.Silu, 0)
            for n in range(GU0 + TURNS * PAIRS, DN0):
                gate(dense(n), ACT.Silu, 0)
            for n in range(DN0, KV0):
                hi(dense(n + SPLIT))
            norm(2, sem("resid_ffn"), 8)
            xn_hi(2, XNH, XN, sem("xn_ready"), (3 * KC - 4, 3 * KC))
            xn_hi(3, XQH, XQ, sem("xq_ready"), (4, 8))
            act.wait_ge(used, KV0 + 1)
            for i in range(2):
                a.copy(KT[:, i, :], ps[:, 2 * (KV0 % 2) + i, 0:NT]).then_inc(sem("k_ready"), 1)
            hi(dense(KV0 + SPLIT))
            act.wait_ge(used, KV0 + 2)
            for t in range(3):
                rows = slice(0, P) if t < 2 else slice(96, P)
                a.copy(VT[rows, t, :], ps[rows, 4 + t, 0:NKV * HD]).then_inc(sem("v_ready"), 1)
            hi(dense(KV0 + 1 + SPLIT))
            for n in range(Q0, O0):
                act.wait_ge(used, n + 1)
                for i in range(2):
                    a.copy(QT[:, 2 * (n - Q0) + i, :], ps[:, 2 * (n % 2) + i, 0:NT]).then_inc(sem("q_ready"), 1)
                hi(dense(n + SPLIT))
            act.wait_ge(sem("k_ready"), 2)
            act.wait_ge(sem("cache_loaded"), 16 * (TS + 1))
            a.copy(KCT[:, :, :, W - 1].rearrange("p b k -> p k b"), KT[:, :, TP:NT]).then_inc(sem("kc_ready"), 1)
            for h in range(NH + 1):
                b = h % 2
                act.wait_ge(sem("shift_ready"), h + 1)
                if h >= 2:
                    act.wait_ge(sem("p_turned"), h - 1)
                if h < NH:
                    a.activation(SC[:, b, 0:128], SC[:, b, 0:128], ACT.Exp, bias=nm[:, b, 0:1],
                                 accum_out=sm[:, b, 0:1]).then_inc(sem("exp_ready"), 1)
                    a.activation(SC[:, b, 128:384], SC[:, b, 128:384], ACT.Exp, bias=nm[:, b, 1:2],
                                 accum_out=sm[:, b, 1:2]).then_inc(sem("exp_ready"), 1)
                    a.activation(es[:, b, :], nm[:, b, :], ACT.Exp, bias=SINK[:, HEADS[h]:HEADS[h] + 1]).then_inc(sem("exp_ready"), 1)
                else:
                    a.activation(SC[:, b, 0:128], SC[:, b, 0:128], ACT.Exp, bias=nm[:, b, 0:1],
                                 accum_out=sm[:, b, 0:1]).then_inc(sem("exp_ready"), 1)
                    a.activation(es[:, b, 0:1], nm[:, b, 0:1], ACT.Exp, bias=SINKC[:, :]).then_inc(sem("exp_ready"), 1)
                act.wait_ge(sem("p_turned"), h + 1)
                if h >= 2:
                    act.wait_ge(sem("pv_made"), h - 1)
                n = 384 if h < NH else 128
                a.copy(PTT[:, b, 0:n], ps[:, 2 + b, 0:n]).then_inc(sem("pt_ready"), 1)
            for n in range(O0, NDENSE):
                hi(dense(n + SPLIT))
            norm(3, sem("resid_o"), 8)
            act.wait_ge(sem("kv_stored"), 64)
            for t in range(3):
                rows = tokens(t)
                for hf in range(2):
                    act.wait_ge(sem("h_turned"), 2 * t + hf + 1)
                    a.copy(HTH[0:rows, t, hf * 512:hf * 512 + 512], ps[0:rows, 1 + hf, :]).then_inc(sem("hth_ready"), 1)
            act.wait_ge(sem("gap_ready"), 1)
            a.activation(r4[:, :, :], r3[:, :, :], ACT.Exp).then_inc(sem("gexp_ready"), 1)

            def expert_gate_up(r, j):
                for kq in range(4):
                    m = 4 * j + kq
                    if kq == 1 and j:
                        hidden_hi(r, j - 1)
                    if kq == 3:
                        act.wait_ge(used, at(act, expert_tile(r, m), 1))
                        if j >= 2:
                            act.wait_ge(sem("act_ready"), act.snap(JE * r + (j - 1)))
                        a.activation(SIL[:, j % 2, :], ps[:, 2 * (j % 2), :], ACT.Silu).then_inc(sem("silu_ready"), 1)
                    hi(expert_tile(r, m + SPLIT))

            def hidden_hi(r, j):
                act.wait_ge(sem("act_turned"), act.snap(JE * r + (j + 1)))
                a.copy(AFH[:, 4 * j:4 * j + 4, :], ps[:, 6 + j % 2, :].rearrange("p (c n) -> p c n", c=4))\
                    .then_inc(sem("afh_ready"), 1)

            def tokens_hi(n):
                act.wait_ge(sem("gathered"), n)
                a.copy(XEH[:, :, :].rearrange("p c n -> p (c n)"), ps[:, 0:2, :].rearrange("p b n -> p (b n)"))\
                    .then_inc(sem("xeh_ready"), 1)

            def expert_rest(r, more):
                for j in range(1, JE):
                    expert_gate_up(r, j)
                for d in range(NDE):
                    if d == 1:
                        hidden_hi(r, JE - 1)
                    if d == 3:
                        act.wait_ge(sem("gate_turned"), act.snap(r + 1))
                        a.copy(GSH[:, :], ps[:, 7, 0:NT]).then_inc(sem("gsh_ready"), 1)
                    if d == 6 and more:
                        tokens_hi(act.snap(r + 2))
                    if d == NDE - 1:
                        act.wait_ge(used, at(act, expert_tile(r, NE)))
                        a.copy(YEH[:, :], ps[:, 4:6, :].rearrange("p b n -> p (b n)")).then_inc(sem("yeh_ready"), 1)
                    if more or NGU + d + SPLIT < NE:
                        hi(expert_tile(r, NGU + d + SPLIT))
                if more:
                    expert_gate_up(act.snap(r + 1), 0)

            zero = act.snap(0)
            tokens_hi(1)
            expert_gate_up(zero, 0)
            with act.Fori(0, E - 1) as e:
                expert_rest(e, True)
            last = act.snap(zero + (E - 1))
            expert_rest(last, False)
            act.wait_ge(sem("plan_ready"), 1)
            with act.Fori(0, 2 * E) as i:
                more = act.value_load(plan[0:1, bass.ds(i, 1)], min_val=0, max_val=1)
                with act.If(more > 0):
                    r = act.value_load(plan[0:1, bass.ds(i + 2 * E, 1)], min_val=E, max_val=E + 4)
                    for m in range(SPLIT):
                        hi(expert_tile(r, m))
                    tokens_hi(act.snap(r + 1))
                    expert_gate_up(r, 0)
                    expert_rest(r, False)
            norm(4, sem("moe_done"), 1)

        @block.vector
        def _(dve):
            v = nc.vector
            steps = [0]

            def link(ins):
                steps[0] += 1
                ins.then_inc(sem("dve_step"), 1)
                dve.wait_ge(sem("dve_step"), steps[0])

            def reduce_phase(x, t, last=None):
                link(v.tensor_scalar(t, x, 1.0 / (2 * math.pi), MAGIC, ALU.mult, ALU.add))
                link(v.tensor_scalar(t, t, MAGIC, None, ALU.subtract))
                link(v.scalar_tensor_tensor(out=x, in0=t, scalar=-TWO_PI_HI, in1=x, op0=ALU.mult, op1=ALU.add))
                link(v.scalar_tensor_tensor(out=x, in0=t, scalar=-TWO_PI_LO, in1=x, op0=ALU.mult, op1=ALU.add))
                ins = v.tensor_scalar(x, x, PI_IN, -PI_IN, ALU.min, ALU.max)
                if last is None:
                    link(ins)
                else:
                    ins.then_inc(last, 1)

            def norm(i, gidx, done):
                dve.wait_ge(sem("root_ready"), i + 1)
                v.reciprocal(rstd[:, :], root[:, :]).then_inc(sem("rstd_ready"), 1)
                dve.wait_ge(sem("rstd_ready"), i + 1)
                scale(XN, gidx, done)

            def scale(out, gidx, done):
                for c in range(KC):
                    v.scalar_tensor_tensor(out=out[:, c, :], in0=X[:, c, :], scalar=vec[:, gidx, c:c + 1],
                                           in1=rstd[:, :], op0=ALU.mult, op1=ALU.mult).then_inc(done, 1)

            for rows, x in ((slice(0, 64), 1.0), (slice(64, 128), -1.0)):
                link(v.memset(sgn[rows, :], x))
                link(v.memset(nsgn[rows, :], -x))
            dve.wait_ge(sem("lam_loaded"), 80)
            dve.wait_ge(sem("tanh_ready"), 1)
            link(v.tensor_scalar(q[1][:, :], q[0][:, :], -1.0, 1.0, ALU.mult, ALU.add))
            link(v.reciprocal(q[1][:, :], q[1][:, :]))
            link(v.scalar_tensor_tensor(out=dtt[:, :], in0=q[0][:, :], scalar=1.0, in1=q[1][:, :],
                                        op0=ALU.add, op1=ALU.mult))
            for _ in range(4):
                link(v.tensor_tensor(dtt[:, :], dtt[:, :], dtt[:, :], ALU.mult))
            v.tensor_tensor(q[1][:, :], are[:, :], dtt[:, :], ALU.mult).then_inc(sem("decay_ready"), 1)
            link(v.tensor_tensor(q[4][:, :], aim[:, :], dtt[:, :], ALU.mult))
            reduce_phase(q[4][:, :], q[5][:, :])
            dve.wait_ge(sem("consts"), 5)
            dve.wait_ge(sem("vec_loaded"), 16)
            link(v.tensor_tensor(T9[0][:, :, :], q[4][:, :].unsqueeze(1).to_broadcast([P, 9, G]),
                                 kramp[:, :].unsqueeze(2).to_broadcast([P, 9, G]), ALU.mult))
            reduce_phase(T9[0][:, :, :], T9[1][:, :, :], sem("phase9_ready"))
            link(v.tensor_scalar(q[7][:, :], q[4][:, :], float(L), None, ALU.mult))
            reduce_phase(q[7][:, :], q[5][:, :])
            dve.wait_ge(sem("tanh_ready"), 2)
            t2 = q[3][:, :]
            link(v.tensor_scalar(q[8][:, :], t2, 1.0, None, ALU.add))
            link(v.tensor_scalar(q[9][:, :], t2, -1.0, 1.0, ALU.mult, ALU.add))
            link(v.reciprocal(q[10][:, :], q[8][:, :]))
            link(v.reciprocal(q[11][:, :], q[9][:, :]))
            link(v.memset(MT[:, 4, :], 1.0))
            link(v.tensor_tensor(MT[:, 5, :], q[8][:, :], q[11][:, :], ALU.mult))
            link(v.tensor_tensor(MT[:, 3, :], q[9][:, :], q[10][:, :], ALU.mult))
            for sgn_, one in ((1, 5), (-1, 3)):
                for k in range(2, 5):
                    link(v.tensor_tensor(MT[:, 4 + sgn_ * k, :], MT[:, 4 + sgn_ * (k - 1), :], MT[:, one, :], ALU.mult))
            norm(0, G_MIX0, sem("xn_ready"))
            dve.wait_ge(sem("sin9_ready"), 4)
            link(v.tensor_tensor(q[8][:, :], are[:, :], are[:, :], ALU.mult))
            link(v.tensor_tensor(q[9][:, :], aim[:, :], aim[:, :], ALU.mult))
            link(v.tensor_tensor(q[8][:, :], q[8][:, :], q[9][:, :], ALU.add))
            link(v.reciprocal(q[8][:, :], q[8][:, :]))
            link(v.scalar_tensor_tensor(out=q[9][:, :], in0=t2, scalar=2.0, in1=q[11][:, :],
                                        op0=ALU.mult, op1=ALU.mult))
            link(v.tensor_tensor(q[9][:, :], q[9][:, :], ER[:, 5, :], ALU.mult))
            link(v.tensor_tensor(q[6][:, :], q[6][:, :], q[6][:, :], ALU.mult))
            link(v.scalar_tensor_tensor(out=q[9][:, :], in0=q[6][:, :], scalar=-2.0, in1=q[9][:, :],
                                        op0=ALU.mult, op1=ALU.add))
            link(v.tensor_tensor(q[10][:, :], MT[:, 5, :], EI[:, 5, :], ALU.mult))
            link(v.tensor_tensor(q[12][:, :], q[9][:, :], are[:, :], ALU.mult))
            link(v.tensor_tensor(q[11][:, :], q[10][:, :], aim[:, :], ALU.mult))
            link(v.tensor_tensor(q[12][:, :], q[12][:, :], q[11][:, :], ALU.add))
            link(v.tensor_tensor(q[12][:, :], q[12][:, :], q[8][:, :], ALU.mult))
            link(v.tensor_tensor(q[13][:, :], q[10][:, :], are[:, :], ALU.mult))
            link(v.tensor_tensor(q[11][:, :], q[9][:, :], aim[:, :], ALU.mult))
            link(v.tensor_tensor(q[13][:, :], q[13][:, :], q[11][:, :], ALU.subtract))
            link(v.tensor_tensor(q[13][:, :], q[13][:, :], q[8][:, :], ALU.mult))
            link(v.tensor_tensor(ER[:, :, :], ER[:, :, :], MT[:, :, :], ALU.mult))
            link(v.tensor_tensor(EI[:, :, :], EI[:, :, :], MT[:, :, :], ALU.mult))
            link(v.tensor_scalar(T9[0][:, :, :], ER[:, :, :], sgn[:, :], None, ALU.mult))
            v.tensor_scalar(T9[1][:, :, :], EI[:, :, :], -1.0, None, ALU.mult).then_inc(sem("pow_ready"), 1)
            link(v.tensor_copy(q[0][:, :], ER[:, 5, :]))
            link(v.tensor_scalar(q[1][:, :], EI[:, 5, :], nsgn[:, :], None, ALU.mult))
            link(v.tensor_copy(q[2][:, :], ER[:, 7, :]))
            link(v.tensor_copy(q[3][:, :], EI[:, 7, :]))
            link(v.tensor_tensor(q[4][:, :], MT[:, 8, :], MT[:, 8, :], ALU.mult))
            cr = q[12][:, :].unsqueeze(1).to_broadcast([P, 9, G])
            ci = q[13][:, :].unsqueeze(1).to_broadcast([P, 9, G])
            link(v.tensor_tensor(MT[:, :, :], EI[:, :, :], ci, ALU.mult))
            link(v.tensor_tensor(EI[:, :, :], EI[:, :, :], cr, ALU.mult))
            X9 = TC[:, :, :].rearrange("p a b -> p (a b)")[:, 0:9 * G].rearrange("p (a b) -> p a b", a=9)
            link(v.tensor_tensor(X9, ER[:, :, :], ci, ALU.mult))
            link(v.tensor_tensor(ER[:, :, :], ER[:, :, :], cr, ALU.mult))
            link(v.tensor_tensor(ER[:, :, :], ER[:, :, :], MT[:, :, :], ALU.subtract))
            link(v.tensor_tensor(EI[:, :, :], EI[:, :, :], X9, ALU.add))
            link(v.tensor_scalar(EI[:, :, :], EI[:, :, :], nsgn[:, :], None, ALU.mult))
            dve.wait_ge(sem("h0_loaded"), 32)
            wide = lambda x: x.unsqueeze(2).to_broadcast([P, G, TS])
            link(v.tensor_tensor(H0Q[:, :, :], H0Q[:, :, :], wide(q[0][:, :]), ALU.mult))
            link(v.tensor_tensor(H0X[:, :, :], H0X[:, :, :], wide(q[1][:, :]), ALU.mult))
            link(v.tensor_tensor(H0Q[:, :, :], H0Q[:, :, :], H0X[:, :, :], ALU.add))

            for hf in range(2):
                gs = slice(hf * GH, hf * GH + GH)
                link(v.tensor_tensor(TA[:, :, :], q[7][:, gs].unsqueeze(2).to_broadcast([P, GH, NB]),
                                     jramp[:, :].unsqueeze(1).to_broadcast([P, GH, NB]), ALU.mult))
                reduce_phase(TA[:, :, :], TB[:, :, :], sem("phase_ready"))
                dve.wait_ge(sem("b_loaded"), 32 * (hf + 1))
                if hf:
                    dve.wait_ge(sem("toep_made"), 8)
                for s in range(L):
                    er = ER[:, 8 - s, gs].unsqueeze(2).to_broadcast([P, GH, H])
                    ei = EI[:, 8 - s, gs].unsqueeze(2).to_broadcast([P, GH, H])
                    out = AM[:, :, s * H:(s + 1) * H]
                    v.tensor_tensor(out, BQ[:, :, :], er, ALU.mult).then_inc(sem("dve_step"), 1)
                    steps[0] += 1
                    link(v.tensor_tensor(PT[:, :, :], BX[:, :, :], ei, ALU.mult))
                    ins = v.tensor_tensor(out, out, PT[:, :, :], ALU.add)
                    if s < L - 1:
                        link(ins)
                    else:
                        ins.then_inc(sem("a_built"), 1)
                link(v.tensor_copy(R8[:, :, :], q[4][:, gs].unsqueeze(2).to_broadcast([P, GH, NB])))
                link(v.memset(R8[:, :, 0:1], 0.0))
                link(v.memset(WV[:, 0:1], 0.0))
                dve.wait_ge(sem("turn_ready"), 3 * hf + 3)
                wv = WV[:, 1:].rearrange("p (g j) -> p g j", g=GH)

                def turn_back(b):
                    dve.wait_ge(sem("v_made"), 4 * hf + b + 1)
                    bk = 6 if b % 2 == 0 else 0
                    g8 = slice(8 * b, 8 * b + 8)
                    V = ps[:, bk, 0:8 * UC].rearrange("p (g n) -> p g n", g=8)
                    VX = ps[:, bk + 1, 0:8 * UC].rearrange("p (g n) -> p g n", g=8)
                    v.tensor_tensor(TB[:, g8, :], V[:, :, 0:NB], COS[:, g8, :], ALU.mult).then_inc(sem("dve_step"), 1)
                    v.tensor_copy(VS[:, g8, :], V[:, :, NB:UC]).then_inc(sem("dve_step"), 1)
                    steps[0] += 2
                    v.tensor_tensor(TC[:, g8, :], VX[:, :, 0:NB], SS[:, g8, :], ALU.mult).then_inc(sem("v_turned"), 1)
                    dve.wait_ge(sem("dve_step"), steps[0])
                    dve.wait_ge(sem("v_turned"), 4 * hf + b + 1)
                    link(v.tensor_tensor(wv[:, g8, :], TB[:, g8, :], TC[:, g8, :], ALU.add))

                for b in range(8):
                    dve.wait_ge(sem("toep_made"), 8 * hf + b + 1)
                    v.tensor_tensor(TM[:, 4 * b:4 * b + 4, :], ps[:, 2 + b % 2, :].rearrange("p (g n) -> p g n", g=4),
                                    tmask[:, :].unsqueeze(1).to_broadcast([P, 4, P]), ALU.mult)\
                        .then_inc(sem("toep_ready"), 1)
                    if b % 2 and b > 1:
                        turn_back(b // 2 - 1)
                turn_back(3)
                sv = SV[:, :, :].rearrange("p g j -> p (g j)")
                v.tensor_tensor_scan(sv, WV[:, 0:GH * NB], R8[:, :, :].rearrange("p g j -> p (g j)"), 0.0,
                                     ALU.add, ALU.mult).then_inc(sem("scanned"), 1)
                dve.wait_ge(sem("scanned"), hf + 1)
                v.tensor_tensor(GL[:, :], SV[:, :, NB - 1], wv[:, :, NB - 1], ALU.add).then_inc(sem("last_ready"), 1)
                link(v.tensor_tensor(TB[:, :, :], SV[:, :, :], COS[:, :, :], ALU.mult))
                for i in range(2):
                    dve.wait_ge(sem("swapped"), 3 * hf + i + 1)
                    g16 = slice(16 * i, 16 * i + 16)
                    link(v.tensor_tensor(TC[:, g16, :], ps[:, 2 + i, :].rearrange("p (g j) -> p g j", g=16),
                                         SS[:, g16, :], ALU.mult))
                if hf:
                    dve.wait_ge(sem("y_made"), 4)
                link(v.tensor_tensor(HM[:, :, 0:NB], TB[:, :, :], TC[:, :, :], ALU.subtract))
                v.tensor_copy(HM[:, :, NB:UC], H0Q[:, gs, :]).then_inc(sem("h_ready"), 1)
                c31, s31 = COS[:, :, NB - 1], SS[:, :, NB - 1]
                link(v.tensor_scalar(q[8][:, 0:GH], s31, sgn[:, :], None, ALU.mult))
                link(v.tensor_tensor(q[9][:, 0:GH], q[2][:, gs], c31, ALU.mult))
                link(v.tensor_tensor(q[10][:, 0:GH], q[3][:, gs], q[8][:, 0:GH], ALU.mult))
                link(v.tensor_tensor(q[9][:, 0:GH], q[9][:, 0:GH], q[10][:, 0:GH], ALU.subtract))
                link(v.tensor_tensor(q[8][:, 0:GH], q[8][:, 0:GH], q[2][:, gs], ALU.mult))
                link(v.tensor_tensor(q[10][:, 0:GH], q[3][:, gs], c31, ALU.mult))
                link(v.tensor_tensor(q[8][:, 0:GH], q[8][:, 0:GH], q[10][:, 0:GH], ALU.add))
                link(v.tensor_scalar(q[8][:, 0:GH], q[8][:, 0:GH], nsgn[:, :], None, ALU.mult))
                link(v.tensor_tensor(q[9][:, 0:GH], q[9][:, 0:GH], GL[:, :], ALU.mult))
                dve.wait_ge(sem("swapped"), 3 * hf + 3)
                link(v.tensor_tensor(q[8][:, 0:GH], ps[:, 7, 0:GH], q[8][:, 0:GH], ALU.mult))
                link(v.tensor_tensor(HP[:, gs], q[9][:, 0:GH], q[8][:, 0:GH], ALU.add))
                v.tensor_tensor(HS[:, gs, :], H0Q[:, gs, :], VS[:, :, :], ALU.add).then_inc(sem("states_done"), 1)
            dve.wait_ge(sem("squared"), 1)
            for c in range(KC):
                v.tensor_scalar(TMP[:, c, :], XN[:, c, :], vec[:, SSM_D, c:c + 1], None, ALU.mult)\
                    .then_inc(sem("du_ready"), 1)
            dve.wait_ge(sem("du_ready"), 8)
            for s in range(L):
                dve.wait_ge(sem("y_moved"), s + 1)
                y_t = TMP[:, :, s:TP:L]
                wide_cols = UC if s == SMID else NB
                src = ps[:, s % 2, 0:KC * wide_cols].rearrange("p (c n) -> p c n", c=KC)
                if s == SMID:
                    link(v.tensor_tensor(TMP[:, :, TP:NT], src[:, :, NB:UC], TMP[:, :, TP:NT], ALU.add))
                v.tensor_tensor(y_t, src[:, :, 0:NB], y_t, ALU.add).then_inc(sem("y_mixed"), 1)

            dve.wait_ge(sem("y_mixed"), 8)
            v.memset(relx[NBUCK:NBUCK + 1, :], NEG).then_inc(sem("outside_ready"), 1)

            def lo(tile):
                hi_ = WH[tile[2] % SPLIT][:, :].bitcast(F32)
                dve.wait_ge(sem("hi_made"), at(dve, tile, 1))
                v.tensor_tensor(WL[tile[2] % SPLIT][:, :], raw[tile[2] % RING][:, :], hi_, ALU.subtract)\
                    .then_inc(split, 1)

            def xn_lo(i, dst, src, hi_):
                for k in range(2):
                    dve.wait_ge(sem("xn_hi_made"), 2 * i + k + 1)
                    c4 = slice(4 * k, 4 * k + 4)
                    v.tensor_tensor(dst[:, c4, :], src[:, c4, :], hi_[:, c4, :].bitcast(F32), ALU.subtract)\
                        .then_inc(sem("xn_split"), 1)

            xn_lo(0, XNL, XN, XNH)
            for n in range(SPLIT):
                lo(dense(n))
            for n in range(GU0):
                dve.wait_ge(sem("gated"), n + 1)
                link(v.tensor_tensor(SG[:, n % 2, :], ps[:, 2 * (n % 2), 0:NT], SG[:, n % 2, :], ALU.mult))
                v.tensor_tensor(X[:, n, :], X[:, n, :], SG[:, n % 2, :], ALU.add).then_inc(sem("pair_done"), 1)
                lo(dense(n + SPLIT))
            norm(1, G_FFN0, sem("xn_ready"))
            xn_lo(1, XNL, XN, XNH)

            def gate_up(tile):
                b = tile[2] % 2
                r, stride, c = tile
                out = c - GU0 if r is None else bass.ds(r * stride + (c - GU0), 1)
                fah, fal = (f[:, out, :] if r is None else f[:, out, :].rearrange("p a n -> p (a n)")
                            for f in (FAH, FAL))
                dve.wait_ge(sem("gated"), at(dve, tile, 1))
                v.tensor_tensor(SG[:, b, :], ps[:, 2 * b + 1, 0:NT], SG[:, b, :], ALU.mult).then_inc(sem("fa_made"), 1)
                dve.wait_ge(sem("fa_made"), at(dve, tile, 1 - GU0))
                v.tensor_copy(fah, SG[:, b, :]).then_inc(sem("fah_made"), 1)
                dve.wait_ge(sem("fah_made"), at(dve, tile, 1 - GU0))
                v.tensor_tensor(fal, SG[:, b, :], fah.bitcast(F32), ALU.subtract).then_inc(sem("pair_done"), 1)
                lo(after(tile, SPLIT))

            with dve.Fori(0, TURNS) as r:
                for i in range(PAIRS):
                    gate_up((r, PAIRS, GU0 + i))
            for n in range(GU0 + TURNS * PAIRS, DN0):
                gate_up(dense(n))
            for n in range(DN0, KV0):
                lo(dense(n + SPLIT))
            dve.wait_ge(used, KV0)
            for c in range(KC):
                v.tensor_tensor(X[:, c, :], ps[:, c, 0:NT], X[:, c, :], ALU.add).then_inc(sem("resid_ffn"), 1)
            dve.wait_ge(sem("norm_summed"), 3)
            norm(2, G_KV, sem("xn_ready"))
            scale(XQ, G_MIX1, sem("xq_ready"))
            xn_lo(2, XNL, XN, XNH)
            xn_lo(3, XQL, XQ, XQH)
            for n in range(KV0, O0):
                lo(dense(n + SPLIT))
            dve.wait_ge(sem("sink_loaded"), 16 * (TS + 1))
            dve.wait_ge(sem("bias_loaded"), 16 * (NH + TS))

            def scores(h):
                b = h % 2
                dve.wait_ge(sem("s_made"), h + 1)
                if h >= 2:
                    dve.wait_ge(sem("p_turned"), h - 1)
                if h < NH:
                    v.scalar_tensor_tensor(out=SC[:, b, 0:W], in0=ps[:, b, 0:W], scalar=SCALE,
                                           in1=BIAS[:, HEADS[h], W:2 * W], op0=ALU.mult, op1=ALU.add)\
                        .then_inc(sem("dve_step"), 1)
                    v.scalar_tensor_tensor(out=SC[:, b, W:3 * W], in0=ps[:, b, W:3 * W], scalar=SCALE,
                                           in1=BIAS[:, HEADS[h], :], op0=ALU.mult, op1=ALU.add).then_inc(sem("s_read"), 1)
                    steps[0] += 1
                    dve.wait_ge(sem("dve_step"), steps[0])
                    link(v.reduce_max(mx[:, b, 0:1], SC[:, b, 0:W], AX_X))
                    dve.wait_ge(sem("s_read"), h + 1)
                    link(v.reduce_max(mx[:, b, 1:2], SC[:, b, W:3 * W], AX_X))
                    v.tensor_scalar(nm[:, b, :], mx[:, b, :], SINK[:, HEADS[h]:HEADS[h] + 1], -1.0, ALU.max, ALU.mult)\
                        .then_inc(sem("shift_ready"), 1)
                else:
                    v.scalar_tensor_tensor(out=SC[:, b, 0:W], in0=ps[:, b, 0:W], scalar=SCALE,
                                           in1=BSM[:, :], op0=ALU.mult, op1=ALU.add).then_inc(sem("s_read"), 1)
                    dve.wait_ge(sem("s_read"), h + 1)
                    link(v.reduce_max(mx[:, b, 0:1], SC[:, b, 0:W], AX_X))
                    v.tensor_scalar(nm[:, b, 0:1], mx[:, b, 0:1], SINKC[:, :], -1.0, ALU.max, ALU.mult)\
                        .then_inc(sem("shift_ready"), 1)

            def probs(h):
                b = h % 2
                k = 2 if h < NH else 1
                dve.wait_ge(sem("exp_ready"), 3 * h + 3 if h < NH else 3 * NH + 2)
                link(v.tensor_tensor(rd[:, b, 0:k], sm[:, b, 0:k], es[:, b, 0:k], ALU.add))
                link(v.reciprocal(rd[:, b, 0:k], rd[:, b, 0:k]))
                if h < NH:
                    v.tensor_scalar(SC[:, b, 0:W], SC[:, b, 0:W], rd[:, b, 0:1], None, ALU.mult)\
                        .then_inc(sem("p_ready"), 1)
                    v.tensor_scalar(SC[:, b, W:3 * W], SC[:, b, W:3 * W], rd[:, b, 1:2], None, ALU.mult)\
                        .then_inc(sem("p_ready"), 1)
                else:
                    v.tensor_scalar(SC[:, b, 0:W], SC[:, b, 0:W], rd[:, b, 0:1], None, ALU.mult)\
                        .then_inc(sem("p_ready"), 1)

            def heads_out(h):
                c = h // 2
                dve.wait_ge(sem("pv_made"), h + 1)
                link(v.tensor_copy(OTH[:, c, 0:TP], ps[:, 4 + c % 2, 0:TP]))
                v.tensor_tensor(OTL[:, c, 0:TP], ps[:, 4 + c % 2, 0:TP], OTH[:, c, 0:TP].bitcast(F32), ALU.subtract)\
                    .then_inc(sem("o_ready"), 1)

            for h in range(NH):
                scores(h)
                if h:
                    probs(h - 1)
                if h >= 3 and h % 2:
                    heads_out(h - 2)
            dve.wait_ge(sem("st_made"), 1)
            sts = STS[:, :].rearrange("p (x g r) -> p x g r", g=2, r=R)
            for i in range(2):
                v.tensor_copy(sts[:, :, i], ps[:, 6 + i, 0:64].rearrange("p (x r) -> p x r", r=R))\
                    .then_inc(sem("st_ready"), 1)
            probs(NH - 1)
            scores(NH)
            heads_out(NH - 1)
            probs(NH)
            dve.wait_ge(sem("os_made"), 1)
            o_new = ps[:, 6, 0:KC * TS].rearrange("p (c b) -> p c b", c=KC)
            link(v.tensor_copy(OTH[:, :, TP:NT], o_new))
            v.tensor_tensor(OTL[:, :, TP:NT], o_new, OTH[:, :, TP:NT].bitcast(F32), ALU.subtract)\
                .then_inc(sem("o_ready"), 1)
            for n in range(O0, NDENSE):
                dve.wait_ge(used, n + 1)
                for i in range(2):
                    c = 2 * (n - O0) + i
                    v.tensor_tensor(X[:, c, :], ps[:, 2 * (n % 2) + i, 0:NT], X[:, c, :], ALU.add)\
                        .then_inc(sem("resid_o"), 1)
                lo(dense(n + SPLIT))
            norm(3, G_FFN1, sem("xn_ready"))

            dve.wait_ge(sem("kv_stored"), 64)
            for t in range(3):
                rows = tokens(t)
                for hf in range(2):
                    half_ = slice(hf * 512, hf * 512 + 512)
                    dve.wait_ge(sem("hth_ready"), 2 * t + hf + 1)
                    v.tensor_tensor(HTL[0:rows, t, half_], ps[0:rows, 1 + hf, :], HTH[0:rows, t, half_].bitcast(F32),
                                    ALU.subtract).then_inc(sem("ht_ready"), 1)
            dve.wait_ge(sem("logits_made"), 1)
            dve.wait_ge(sem("route_consts"), 5)
            link(v.tensor_copy(LG[:, 0:2, :], ps[:, 3, 0:2 * E].rearrange("p (t e) -> p t e", t=2)))
            link(v.tensor_copy(LG[0:TS, 2, :], ps[0:TS, 3, 2 * E:3 * E]))
            for t in range(3):
                link(v.max(top[:, t, :], LG[:, t, :]))
            first = top[:, :, 0:1].to_broadcast([P, 3, E])
            second = top[:, :, 1:2].to_broadcast([P, 3, E])
            link(v.tensor_tensor(r1[:, :, :], LG[:, :, :], second, ALU.is_gt))
            link(v.tensor_tensor(r2[:, :, :], LG[:, :, :], second, ALU.is_equal))
            flat = lambda x: x[:, :, :].rearrange("p t e -> p (t e)")
            link(v.tensor_tensor_scan(flat(r3), flat(dz), flat(r2), 0.0, ALU.mult, ALU.add))
            link(v.tensor_reduce(v1[:, :], r1[:, :, :], AX_X, ALU.add))
            link(v.tensor_tensor(r3[:, :, :], r3[:, :, :], v1[:, :].unsqueeze(2).to_broadcast([P, 3, E]), ALU.add))
            link(v.tensor_scalar(r3[:, :, :], r3[:, :, :], 2.0, None, ALU.is_le))
            link(v.tensor_tensor(r2[:, :, :], r2[:, :, :], r3[:, :, :], ALU.mult))
            v.tensor_tensor(SELM[:, :, :], r1[:, :, :], r2[:, :, :], ALU.add).then_inc(sem("sel_ready"), 1)
            dve.wait_ge(sem("sel_ready"), 1)
            v.tensor_tensor(r3[:, :, :], LG[:, :, :], first, ALU.subtract).then_inc(sem("gap_ready"), 1)
            dve.wait_ge(sem("gexp_ready"), 1)
            link(v.tensor_tensor(GATE[:, :, :], r4[:, :, :], SELM[:, :, :], ALU.mult))
            link(v.tensor_reduce(v1[:, :], GATE[:, :, :], AX_X, ALU.add))
            link(v.reciprocal(v1[:, :], v1[:, :]))
            link(v.tensor_tensor(GATE[:, :, :], GATE[:, :, :], v1[:, :].unsqueeze(2).to_broadcast([P, 3, E]), ALU.mult))
            dve.wait_ge(sem("pos_made"), 1)
            link(v.memset(POS[:, :, :], 0.0))
            link(v.tensor_copy(POS[:, 0:2, :], ps[:, 4, 0:2 * E].rearrange("p (t e) -> p t e", t=2)))
            link(v.tensor_copy(POS[0:TS, 2, :], ps[0:TS, 4, 2 * E:3 * E]))
            link(v.scalar_tensor_tensor(out=POS[:, :, :], in0=POS[:, :, :], scalar=1.0, in1=SELM[:, :, :],
                                        op0=ALU.add, op1=ALU.mult))
            link(v.tensor_scalar(POS[:, :, :], POS[:, :, :], -1.0, None, ALU.add))
            need = cnt[:, :].rearrange("p (e k) -> p e k", k=2)
            total = ps[0:1, 4, 3 * E:4 * E]
            link(v.tensor_scalar(need[:, :, 0], total, float(P) + 0.5, None, ALU.is_gt))
            link(v.tensor_scalar(need[:, :, 1], total, 2.0 * P + 0.5, None, ALU.is_gt))
            link(v.memset(run[:, :], 1.0))
            link(v.memset(run[:, 0:1], float(E)))
            link(v.tensor_tensor_scan(run[:, 1:2 * E + 1], run[:, 1:2 * E + 1], cnt[:, :], float(E), ALU.mult, ALU.add))
            link(v.tensor_copy(plan[:, 0:2 * E], cnt[:, :]))
            v.tensor_copy(plan[:, 2 * E:4 * E + 1], run[:, :]).then_inc(sem("plan_ready"), 1)

            def dispatch(e, k):
                for t in range(3):
                    rows = tokens(t)
                    pos, gate_ = POS[0:rows, t, bass.ds(e, 1)], GATE[0:rows, t, bass.ds(e, 1)]
                    v.tensor_scalar(DSP[0:rows, t, :], slot[0:rows, k, :], pos, None, ALU.is_equal)\
                        .then_inc(sem("dispatched"), 1)
                    v.tensor_scalar(DG[0:rows, t, :], slot[0:rows, k, :], pos, gate_, ALU.is_equal, ALU.mult)\
                        .then_inc(sem("gate_spread"), 1)

            def expert_gate_up(r, j, prev=None):
                for kq in range(4):
                    m = 4 * j + kq
                    if kq == 1 and j:
                        hidden_lo(r, j - 1)
                    if kq == 3:
                        dve.wait_ge(sem("silu_ready"), dve.snap(JE * r + (j + 1)))
                        if j >= 2:
                            dve.wait_ge(sem("act_turned"), dve.snap(JE * r + (j - 1)))
                        v.tensor_tensor(AC[:, j % 2, :], ps[:, 2 * (j % 2) + 1, :], SIL[:, j % 2, :], ALU.mult)\
                            .then_inc(sem("act_ready"), 1)
                    lo(expert_tile(r, m + SPLIT))
                    if prev is not None and kq % 2:
                        add(prev, kq // 2)

            def hidden_lo(r, j):
                dve.wait_ge(sem("afh_ready"), dve.snap(JE * r + (j + 1)))
                v.tensor_tensor(AFL[:, 4 * j:4 * j + 4, :], ps[:, 6 + j % 2, :].rearrange("p (c n) -> p c n", c=4),
                                AFH[:, 4 * j:4 * j + 4, :].bitcast(F32), ALU.subtract).then_inc(sem("af_split"), 1)

            def tokens_lo(n):
                dve.wait_ge(sem("gathered"), n)
                v.tensor_copy(XEL[:, :, :].rearrange("p c n -> p (c n)"), ps[:, 2:4, :].rearrange("p b n -> p (b n)"))\
                    .then_inc(sem("xel_ready"), 1)

            def add(r, i):
                dve.wait_ge(sem("scattered"), dve.snap(2 * r + (i + 1)))
                c4 = slice(4 * i, 4 * i + 4)
                v.tensor_tensor(X[:, c4, :], ps[:, 4:8, 0:NT], X[:, c4, :], ALU.add).then_inc(sem("x_added"), 1)

            def expert_rest(r, more):
                for j in range(1, JE):
                    expert_gate_up(r, j)
                for d in range(NDE):
                    if d == 1:
                        hidden_lo(r, JE - 1)
                    if d == 3:
                        dve.wait_ge(sem("gsh_ready"), dve.snap(r + 1))
                        v.tensor_tensor(GSL[:, :], ps[:, 7, 0:NT], GSH[:, :].bitcast(F32), ALU.subtract)\
                            .then_inc(sem("gs_split"), 1)
                        if more:
                            dispatch(dve.snap(r + 1), 0)
                    if d == 6 and more:
                        tokens_lo(dve.snap(r + 2))
                    if d == NDE - 1:
                        dve.wait_ge(sem("yeh_ready"), dve.snap(r + 1))
                        v.tensor_tensor(YEL[:, :], ps[:, 4:6, :].rearrange("p b n -> p (b n)"),
                                        YEH[:, :].bitcast(F32), ALU.subtract).then_inc(sem("ye_split"), 1)
                    if more or NGU + d + SPLIT < NE:
                        lo(expert_tile(r, NGU + d + SPLIT))
                if more:
                    expert_gate_up(dve.snap(r + 1), 0, r)
                else:
                    add(r, 0)
                    add(r, 1)

            zero = dve.snap(0)
            dispatch(zero, 0)
            tokens_lo(1)
            expert_gate_up(zero, 0)
            with dve.Fori(0, E - 1) as e:
                expert_rest(e, True)
            expert_rest(dve.snap(zero + (E - 1)), False)
            with dve.Fori(0, E) as e:
                for k in range(2):
                    i = dve.snap(e * 2 + k)
                    more = dve.value_load(plan[0:1, bass.ds(i, 1)], min_val=0, max_val=1)
                    with dve.If(more > 0):
                        r = dve.value_load(plan[0:1, bass.ds(i + 2 * E, 1)], min_val=E, max_val=E + 4)
                        for m in range(SPLIT):
                            lo(expert_tile(r, m))
                        dispatch(e, k + 1)
                        tokens_lo(dve.snap(r + 1))
                        expert_gate_up(r, 0)
                        expert_rest(r, False)
            dve.drain()
            v.memset(cnt[:, 0:1], 0.0).then_inc(sem("moe_done"), 1)
            norm(4, G_FIN, sem("xn_ready"))
            dve.wait_ge(sem("xn_ready"), 5 * KC - 0)
            v.memset(cnt[:, 0:1], 0.0).then_inc(sem("out_ready"), 1)

        @block.tensor
        def _(pe):
            t_ = nc.tensor

            def norm(i):
                pe.wait_ge(sem("squared"), i + 1)
                for c in range(KC):
                    mm = t_.matmul(ps[:, 0, 0:NT], ones[:, :], TMP[:, c, :], start=(c == 0), stop=(c == KC - 1))
                mm.then_inc(sem("norm_summed"), 1)

            pe.wait_ge(sem("consts"), 5)
            norm(0)
            for hf in range(2):
                cs = slice(hf * CH, hf * CH + CH)
                pe.wait_ge(sem("xn_ready"), 8)
                pe.wait_ge(sem("root_ready"), 1)
                for k in range(G8):
                    if k >= 2:
                        pe.wait_ge(sem("u_ready"), 8 * hf + k - 1)
                    elif hf:
                        pe.wait_ge(sem("v_turned"), 4)
                    out = ps[:, k % 2, 0:CH * UC].rearrange("p (c n) -> p c n", c=CH)
                    for s in range(L):
                        w0 = 112 - 16 * s
                        mm = t_.matmul(out[:, :, 0:NB], sel[:, k, w0:w0 + P], XN[:, cs, s:TP:L],
                                       start=(s == 0), stop=(s == L - 1), skip_group_check=True)
                        if s == SMID:
                            mm = t_.matmul(out[:, :, NB:UC], sel[:, k, w0:w0 + P], XN[:, cs, TP:NT],
                                           start=False, stop=True, skip_group_check=True)
                    mm.then_inc(sem("u_moved"), 1)
                pe.wait_ge(sem("a_built"), hf + 1)

                def project(b):
                    bk = 6 if b % 2 == 0 else 0
                    if b == 0:
                        pe.wait_ge(sem("u_ready"), 8 * hf + 8)
                        if hf:
                            pe.wait_ge(sem("states_done"), 1)
                    elif b >= 2:
                        pe.wait_ge(sem("v_turned"), 4 * hf + b - 1)
                    pe.wait_ge(sem("at_ready"), 16 * hf + 4 * b + 4)
                    for g in range(8):
                        t_.matmul(ps[:, bk, g * UC:(g + 1) * UC], AT[:, g, 0:128], U[:, 8 * b + g, :],
                                  start=True, stop=True)
                        mm = t_.matmul(ps[:, bk + 1, g * UC:(g + 1) * UC], AT[:, g, 64:192], U[:, 8 * b + g, :],
                                       start=True, stop=True)
                    mm.then_inc(sem("v_made"), 1)

                for b in range(8):
                    if b >= 2:
                        pe.wait_ge(sem("at_ready"), 16 * hf + 2 * (b - 1))
                    elif hf:
                        pe.wait_ge(sem("y_ready"), 4)
                    for g in range(4):
                        mm = t_.transpose(ps[:, 4 + b % 2, g * P:(g + 1) * P], AM[:, 4 * b + g, :], ident[:, :])
                    mm.then_inc(sem("a_turned"), 1)
                    if b == 0:
                        pe.wait_ge(sem("c_built"), hf + 1)
                    if b >= 2:
                        pe.wait_ge(sem("toep_ready"), 8 * hf + b - 1)
                    elif hf:
                        pe.wait_ge(sem("h_ready"), 1)
                    for g in range(4):
                        mm = t_.matmul(ps[:, 2 + b % 2, g * P:(g + 1) * P], AM[:, 4 * b + g, :], CM[:, 4 * b + g, :],
                                       start=True, stop=True)
                    mm.then_inc(sem("toep_made"), 1)
                    if b % 2:
                        project(b // 2)
                pe.wait_ge(sem("scanned"), hf + 1)
                pe.wait_ge(sem("toep_ready"), 8 * hf + 8)
                for i in range(2):
                    t_.matmul(ps[:, 2 + i, :], swp[:, :], SV[:, 16 * i:16 * i + 16, :].rearrange("p g j -> p (g j)"),
                              start=True, stop=True).then_inc(sem("swapped"), 1)
                pe.wait_ge(sem("last_ready"), hf + 1)
                pe.wait_ge(sem("v_turned"), 4 * hf + 4)
                t_.matmul(ps[:, 7, 0:GH], swp[:, :], GL[:, :], start=True, stop=True).then_inc(sem("swapped"), 1)
                pe.wait_ge(sem("h_ready"), hf + 1)
                pe.wait_ge(sem("at_ready"), 16 * hf + 16)
                for b in range(4):
                    if b >= 2:
                        pe.wait_ge(sem("y_ready"), 4 * hf + b - 1)
                    for g in range(8):
                        out = ps[:, 4 + b % 2, g * UC:(g + 1) * UC]
                        t_.matmul(out, TM[:, 8 * b + g, :], U[:, 8 * b + g, :], start=True, stop=False)
                        mm = t_.matmul(out, CM[:, 8 * b + g, :], HM[:, 8 * b + g, :], start=False, stop=True)
                    mm.then_inc(sem("y_made"), 1)
                    if b == 3:
                        pe.wait_ge(sem("y_made"), 4 * hf + 4)
                        pe.sem_inc(sem("half_used"), 1)
            pe.wait_ge(sem("y_ready"), 8)
            yv = Y[:, :, :].rearrange("p (c k) n -> p k c n", k=G8)
            for s in range(L):
                if s >= 2:
                    pe.wait_ge(sem("y_mixed"), s - 1)
                cols = UC if s == SMID else NB
                out = ps[:, s % 2, 0:KC * cols].rearrange("p (c n) -> p c n", c=KC)
                for k in range(G8):
                    w0 = 112 - 16 * k
                    mm = t_.matmul(out, sel[:, s, w0:w0 + P], yv[:, k, :, 0:cols], start=(k == 0), stop=(k == G8 - 1))
                mm.then_inc(sem("y_moved"), 1)

            def passes(out, stat, mov, first, last):
                (sh, sl), (mh, ml) = stat, mov
                t_.matmul(out, sh, mh, start=first, stop=False)
                t_.matmul(out, sh, ml, start=False, stop=False)
                return t_.matmul(out, sl, mh, start=False, stop=last)

            def arrived(tile):
                pe.wait_ge(split, at(pe, tile, 1))
                return WH[tile[2] % SPLIT], WL[tile[2] % SPLIT]

            def pair(tile, rhs, wait=None):
                w = arrived(tile)
                if wait:
                    pe.wait_ge(*wait)
                for i in range(2):
                    for k in range(KC):
                        cols = slice((2 * k + i) * P, (2 * k + i + 1) * P)
                        mm = passes(ps[:, 2 * (tile[2] % 2) + i, 0:NT], [x[:, cols] for x in w],
                                    [x[:, k, :] for x in rhs], k == 0, k == KC - 1)
                mm.then_inc(used, 1)

            XNS = (XNH, XNL)
            pe.wait_ge(sem("xn_split"), 2)
            for n in range(GU0):
                pair(dense(n), XNS, (sem("pair_done"), n - 1) if n >= 2 else None)
            pe.wait_ge(sem("rel_loaded"), 32)
            pe.wait_ge(sem("outside_ready"), 1)
            t_.matmul(ps[0:NH, 7, 0:384], relx[:, :], oneh[:, :], start=True, stop=True).then_inc(sem("bias_made"), 1)
            norm(1)
            pe.wait_ge(sem("xn_ready"), 16)
            pe.wait_ge(sem("root_ready"), 2)
            pe.wait_ge(sem("xn_split"), 4)
            with pe.Fori(0, TURNS) as r:
                for i in range(PAIRS):
                    tile = (r, PAIRS, GU0 + i)
                    pair(tile, XNS, (sem("pair_done"), at(pe, tile, -1)))
            for n in range(GU0 + TURNS * PAIRS, DN0):
                pair(dense(n), XNS, (sem("pair_done"), n - 1))
            pe.wait_ge(sem("pair_done"), DN0)
            for j in range(NF // 2):
                w = arrived(dense(DN0 + j))
                for k in range(2):
                    for c in range(KC):
                        cols = slice((k * KC + c) * P, (k * KC + c + 1) * P)
                        mm = passes(ps[:, c, 0:NT], [x[:, cols] for x in w], [f[:, 2 * j + k, :] for f in (FAH, FAL)],
                                    j == 0 and k == 0, j == NF // 2 - 1 and k == 1)
                mm.then_inc(used, 1)
            pe.wait_ge(sem("resid_ffn"), 8)
            norm(2)
            pe.wait_ge(sem("root_ready"), 3)
            pe.wait_ge(sem("xn_split"), 6)
            pair(dense(KV0), XNS)
            w = arrived(dense(KV0 + 1))
            for t in range(3):
                tok = slice(t * P, (t + 1) * P) if t < 2 else slice(NT - P, NT)
                for k in range(KC):
                    mm = passes(ps[:, 4 + t, 0:256], [x[:, k, tok] for x in XNS],
                                [x[:, k * 256:(k + 1) * 256] for x in w], k == 0, k == KC - 1)
            mm.then_inc(used, 1)
            pe.wait_ge(sem("xn_split"), 8)
            for n in range(Q0, O0):
                pair(dense(n), (XQH, XQL), (sem("k_ready"), 2) if n < Q0 + 2 else (sem("q_ready"), 2 * (n - Q0 - 1)))
            pe.wait_ge(sem("q_ready"), 8)
            pe.wait_ge(sem("v_ready"), 3)

            def score(h):
                c, b = h // 2, h % 2
                rows = slice(64 * b, 64 * b + 64)
                if h >= 2:
                    pe.wait_ge(sem("s_read"), h - 1)
                kv = KT[rows, c // 4, :]
                t_.matmul(ps[:, b, 0:W], QT[rows, c, 0:W], kv[:, 0:W], start=True, stop=True)
                t_.matmul(ps[:, b, W:3 * W], QT[rows, c, W:TP], kv[:, 0:2 * W], start=True, stop=True)\
                    .then_inc(sem("s_made"), 1)

            def turn(h):
                b = h % 2
                pe.wait_ge(sem("p_ready"), 2 * h + 2 if h < NH else 2 * NH + 1)
                if h >= 2:
                    pe.wait_ge(sem("pt_ready"), h - 1)
                for i in range(3 if h < NH else 1):
                    mm = t_.transpose(ps[:, 2 + b, i * P:(i + 1) * P], SC[:, b, i * P:(i + 1) * P], ident[:, :])
                mm.then_inc(sem("p_turned"), 1)

            def mix(h):
                c, b = h // 2, h % 2
                rows = slice(64 * b, 64 * b + 64)
                g = 2 * (c // 4) + b
                pe.wait_ge(sem("pt_ready"), h + 1)
                if c >= 2 and b == 0:
                    pe.wait_ge(sem("o_ready"), c - 1)
                out = ps[rows, 4 + c % 2, :]
                vg = lambda t: VT[:, t, g * HD:(g + 1) * HD]
                t_.matmul(out[:, 0:W], vg(0), PTT[:, b, 0:W], start=True, stop=True)
                t_.matmul(out[:, W:TP], vg(0), PTT[:, b, W:2 * W], start=True, stop=False)
                t_.matmul(out[:, W:TP], vg(1), PTT[:, b, 2 * W:3 * W], start=False, stop=True)\
                    .then_inc(sem("pv_made"), 1)

            for h in range(NH):
                score(h)
                if h:
                    turn(h - 1)
                if h >= 2:
                    mix(h - 2)
            pe.wait_ge(sem("kc_ready"), 1)
            pe.wait_ge(sem("cache_loaded"), 16 * (TS + 1))
            pe.wait_ge(sem("new_v_loaded"), 16)
            for b in range(TS):
                for g in range(NKV):
                    rows = slice(64 * (g % 2), 64 * (g % 2) + 64)
                    c0 = (2 * b + g // 2) * R
                    mm = t_.matmul(ps[:, 6 + g % 2, c0:c0 + R], KCT[rows, b, g // 2, :],
                                   QT[rows, 4 * (g // 2):4 * (g // 2) + 4, TP + b], start=True, stop=True)
            mm.then_inc(sem("st_made"), 1)
            turn(NH - 1)
            mix(NH - 2)
            pe.wait_ge(sem("st_ready"), 2)
            pe.wait_ge(sem("s_read"), NH - 1)
            t_.transpose(ps[:, 0, 0:P], STS[:, :], ident[:, :]).then_inc(sem("s_made"), 1)
            mix(NH - 1)
            turn(NH)
            pe.wait_ge(sem("pt_ready"), NH + 1)
            for b in range(TS):
                for g in range(NKV):
                    rows = slice(64 * (g % 2), 64 * (g % 2) + 64)
                    out = ps[rows, 6, 0:KC * TS].rearrange("p (c b) -> p c b", c=KC)
                    mm = t_.matmul(out[:, 4 * (g // 2):4 * (g // 2) + 4, b], VC[:, b, g * HD:(g + 1) * HD],
                                   PTT[:, 0, b * NH + g * R:b * NH + g * R + R], start=True, stop=True)
            mm.then_inc(sem("os_made"), 1)
            pe.wait_ge(sem("o_ready"), KC + 1)
            for n in range(O0, NDENSE):
                pair(dense(n), (OTH, OTL),
                     (sem("pt_ready"), NH + 1) if n < O0 + 2 else (sem("resid_o"), 2 * (n - O0 - 1)))
            norm(3)
            pe.wait_ge(sem("xn_ready"), 32)
            pe.wait_ge(sem("root_ready"), 4)
            pe.wait_ge(sem("router_loaded"), 16)
            for t in range(3):
                rows = tokens(t)
                for k in range(KC):
                    mm = t_.matmul(ps[0:rows, 3, t * E:(t + 1) * E], XN[:, k, t * P:t * P + rows], WR[:, k, :],
                                   start=(k == 0), stop=(k == KC - 1))
            mm.then_inc(sem("logits_made"), 1)
            for t in range(3):
                rows = tokens(t)
                for hf in range(2):
                    if t:
                        pe.wait_ge(sem("ht_ready"), 2 * t + hf - 1)
                    for k in range(4):
                        mm = t_.transpose(ps[0:rows, 1 + hf, k * P:(k + 1) * P],
                                          XN[:, 4 * hf + k, t * P:t * P + rows], ident[:, :])
                    mm.then_inc(sem("h_turned"), 1)
            pe.wait_ge(sem("sel_ready"), 1)
            for t in range(3):
                rows = tokens(t)
                out = ps[0:rows, 4, t * E:(t + 1) * E]
                for u in range(t):
                    t_.matmul(out, ones[:, 0:rows], SELM[:, u, :], start=(u == 0), stop=False)
                t_.matmul(out, tri[0:rows, 0:rows], SELM[0:rows, t, :], start=(t == 0), stop=True)
            for t in range(3):
                rows = tokens(t)
                mm = t_.matmul(ps[0:1, 4, 3 * E:4 * E], ones[0:rows, 0:1], SELM[0:rows, t, :],
                               start=(t == 0), stop=(t == 2))
            mm.then_inc(sem("pos_made"), 1)
            pe.wait_ge(sem("ht_ready"), 6)
            pe.wait_ge(sem("plan_ready"), 1)

            def gather(n):
                spread = pe.snap(n * 3)
                pe.wait_ge(sem("dispatched"), spread)
                for p_, part in enumerate((HTH, HTL)):
                    for c in range(KC):
                        for t in range(3):
                            rows = tokens(t)
                            mm = t_.matmul(ps[:, 2 * p_ + c // 4, (c % 4) * P:(c % 4 + 1) * P],
                                           part[0:rows, t, c * P:(c + 1) * P], DSP[0:rows, t, :],
                                           start=(t == 0), stop=(t == 2))
                mm.then_inc(sem("gathered"), 1)

            def turn(r, j):
                pe.wait_ge(sem("act_ready"), pe.snap(r * JE + (j + 1)))
                if j >= 2:
                    pe.wait_ge(sem("af_split"), pe.snap(r * JE + (j - 1)))
                elif j == 0:
                    pe.wait_ge(sem("x_added"), pe.snap(r * 2))
                for i in range(4):
                    mm = t_.transpose(ps[:, 6 + j % 2, i * P:(i + 1) * P], AC[:, j % 2, i * P:(i + 1) * P],
                                      ident[:, :])
                mm.then_inc(sem("act_turned"), 1)

            def scatter(r, i):
                if i == 0:
                    pe.wait_ge(sem("ye_split"), pe.snap(r + 1))
                    pe.wait_ge(sem("gs_split"), pe.snap(r + 1))
                else:
                    pe.wait_ge(sem("x_added"), pe.snap(r * 2 + 1))
                for c in range(4 * i, 4 * i + 4):
                    mm = passes(ps[:, 4 + c % 4, 0:NT], [y[:, c * P:(c + 1) * P] for y in (YEH, YEL)],
                                (GSH[:, :], GSL[:, :]), True, True)
                mm.then_inc(sem("scattered"), 1)

            def product(tile, stat, bank, first, last):
                w = arrived(tile)
                for k in range(2):
                    for i in range(2):
                        cols = slice((2 * k + i) * 512, (2 * k + i + 1) * 512)
                        mm = passes(ps[:, bank + i, :], stat[k], [x[:, cols] for x in w],
                                    first and k == 0, last and k == 1)
                mm.then_inc(used, 1)

            def expert_gate_up(r, j, prev=None):
                if j >= 2:
                    pe.wait_ge(sem("act_ready"), pe.snap(r * JE + (j - 1)))
                elif j == 0:
                    pe.wait_ge(sem("xeh_ready"), pe.snap(r + 1))
                    pe.wait_ge(sem("xel_ready"), pe.snap(r + 1))
                for kq in range(4):
                    product(expert_tile(r, 4 * j + kq), [[x[:, 2 * kq + k, :] for x in (XEH, XEL)] for k in range(2)],
                            2 * (j % 2), kq == 0, kq == 3)
                    if kq == 1 and j:
                        turn(r, j - 1)
                    if prev is not None and kq % 2:
                        scatter(prev, kq // 2)

            def expert_rest(r, more):
                for j in range(1, JE):
                    expert_gate_up(r, j)
                for d in range(NDE):
                    if d % 2 == 0:
                        pe.wait_ge(sem("af_split"), pe.snap(r * JE + (d // 2 + 1)))
                    product(expert_tile(r, NGU + d), [[x[:, 2 * d + k, :] for x in (AFH, AFL)] for k in range(2)],
                            4, d == 0, d == NDE - 1)
                    if d == 1:
                        turn(r, JE - 1)
                    if d == 3:
                        pe.wait_ge(sem("af_split"), pe.snap(r * JE + (JE - 1)))
                        pe.wait_ge(sem("gate_spread"), pe.snap(r * 3 + 3))
                        for t in range(3):
                            rows = tokens(t)
                            mm = t_.transpose(ps[:, 7, t * P:t * P + rows], DG[0:rows, t, :], ident[0:rows, 0:rows])
                        mm.then_inc(sem("gate_turned"), 1)
                    if d == 6 and more:
                        gather(pe.snap(r + 2))
                if more:
                    expert_gate_up(pe.snap(r + 1), 0, r)
                else:
                    scatter(r, 0)
                    scatter(r, 1)

            zero = pe.snap(0)
            gather(pe.snap(zero + 1))
            expert_gate_up(zero, 0)
            with pe.Fori(0, E - 1) as e:
                expert_rest(e, True)
            expert_rest(pe.snap(zero + (E - 1)), False)
            with pe.Fori(0, 2 * E) as i:
                more = pe.value_load(plan[0:1, bass.ds(i, 1)], min_val=0, max_val=1)
                with pe.If(more > 0):
                    r = pe.value_load(plan[0:1, bass.ds(i + 2 * E, 1)], min_val=E, max_val=E + 4)
                    gather(pe.snap(r + 1))
                    expert_gate_up(r, 0)
                    expert_rest(r, False)
            norm(4)
            pe.wait_ge(sem("root_ready"), 5)


def _tiles(w, pair):
    v = w.reshape(KC, P, -1)
    return [np.stack([v[:, :, a:a + P], v[:, :, b:b + P]], 2).transpose(1, 0, 2, 3).reshape(P, TILE)
            for a, b in pair]


def kernel(**inp):
    import concourse.bacc as bacc
    from concourse.bass_utils import run_bass_kernel_spmd

    a = {k: np.asarray(v) for k, v in inp.items()}
    c8 = lambda v: v.reshape(KC, P).T
    x = np.concatenate([a["x_prompt"].reshape(TP, D), a["x_sample"].reshape(TS, D)], 0)
    xT = x.T.reshape(KC, P, NT).transpose(1, 0, 2)
    vecs = np.stack([c8(v) for v in (a["g_mix"][0], a["g_mix"][1], a["g_ffn"][0], a["g_ffn"][1],
                                     a["g_kv"], a["g_final"], a["ssm_d"][0])], 1)
    cols = np.concatenate([np.arange(h * HD, (h + 1) * HD) for h in HEADS])
    wq, wo = a["w_q"][0][:, cols], a["w_o"][0][cols, :]
    wdn = a["w_ffn_down"][0].reshape(NF // 2, 2, P, D).transpose(0, 2, 1, 3).reshape(NF // 2, P, TILE)
    wkv = a["w_kv"]
    wv = wkv[:, 256:].reshape(KC, P, 256).transpose(1, 0, 2).reshape(P, TILE)
    wd = np.stack(
        _tiles(a["w_glu"][0], [(j * P, D + j * P) for j in range(KC)])
        + _tiles(a["w_ffn_gate_up"][0], [(j * P, DFF + j * P) for j in range(NF)])
        + list(wdn)
        + _tiles(wkv, [(0, P)]) + [wv]
        + _tiles(wq, [(2 * j * P, (2 * j + 1) * P) for j in range(4)])
        + _tiles(wo, [(2 * j * P, (2 * j + 1) * P) for j in range(4)]), 0)
    gu = a["w_exp_gate_up"][0].reshape(E, 4, 2, P, 2, JE, 512).transpose(0, 5, 1, 3, 2, 4, 6)
    dn = a["w_exp_down"][0].reshape(E, NDE, 2, P, D).transpose(0, 1, 3, 2, 4)
    we = np.concatenate([gu.reshape(E, NGU, P, TILE), dn.reshape(E, NDE, P, TILE)], 1).reshape(E * NE, P, TILE)
    wr = a["w_router"][0].reshape(KC, P, E).transpose(1, 0, 2)
    br, bi = (a[k][0].transpose(1, 0, 2) for k in ("ssm_b_re", "ssm_b_im"))
    cr, ci = (a[k][0].transpose(2, 0, 1) for k in ("ssm_c_re", "ssm_c_im"))
    hr, hi = (a[k][0].transpose(2, 1, 0) for k in ("state_ssm_re", "state_ssm_im"))
    dist = 255 - np.arange(384)
    large = 16 + (np.log(np.maximum(dist, 1).astype(np.float32) / 16) / math.log(8) * 16).astype(np.int32)
    bucket = np.where(dist < 16, dist, np.minimum(large, NBUCK - 1))
    bucket = np.where((dist >= 0) & (dist < W), bucket, NBUCK)
    onehot = (np.arange(NBUCK + 1)[:, None] == bucket[None]).astype(np.float32)
    ins = {
        "xT": xT, "vecs": vecs, "wd": wd, "we": we, "wr": wr,
        "a_re": a["ssm_a_re"][0].T, "a_im": a["ssm_a_im"][0].T, "log_dt": a["ssm_log_dt"],
        "bq": np.concatenate([br, bi], 0), "bx": np.concatenate([bi, br], 0),
        "cq": np.concatenate([cr, ci], 0), "cx": np.concatenate([ci, cr], 0),
        "h0q": np.concatenate([hr, hi], 0), "h0x": np.concatenate([hi, hr], 0),
        "kcT": a["cache_k_win"].reshape(TS, W, 2, P).transpose(0, 3, 2, 1),
        "vc": a["cache_v_win"].reshape(TS, W, 256).transpose(1, 0, 2),
        "sinks": a["attn_sinks"], "relb": a["rel_bias"], "onehot": onehot,
    }
    outs = {"yT": (P, KC, NT), "hp": (P, G), "hs": (P, G, TS), "kp": (P, 2, W), "vp": (P, 256),
            "ks": (P, TS, 2, W), "vs": (P, TS, 256)}
    nc = bacc.Bacc("TRN2", target_bir_lowering=False, num_devices=1)
    arrays, args = {}, []
    for name, v in ins.items():
        arrays["in_" + name] = np.ascontiguousarray(v)
        args.append(nc.dram_tensor("in_" + name, v.shape, F32, kind="ExternalInput").ap())
    for name, shape in outs.items():
        args.append(nc.dram_tensor("out_" + name, shape, F32, kind="ExternalOutput").ap())
    build(nc, *args)
    o = run_bass_kernel_spmd(nc, [arrays], core_ids=[0]).results[0]
    y = o["out_yT"].transpose(1, 0, 2).reshape(D, NT).T
    hp, hs = o["out_hp"], o["out_hs"]
    st = lambda v: v.transpose(2, 1, 0)[None]
    return (y[:TP].reshape(1, TP, D), y[TP:].reshape(TS, 1, D),
            hp[:S].T.reshape(1, 1, G, S), hp[S:].T.reshape(1, 1, G, S),
            o["out_kp"].transpose(2, 1, 0).reshape(1, W, NKV, HD), o["out_vp"].reshape(1, W, NKV, HD),
            st(hs[:S]), st(hs[S:]),
            o["out_ks"].transpose(1, 3, 2, 0).reshape(TS, W, NKV, HD),
            o["out_vs"].transpose(1, 0, 2).reshape(TS, W, NKV, HD))
```

```python
from contextlib import ExitStack
import math

import numpy as np
import concourse.bass as bass
from concourse import mybir

F32 = mybir.dt.float32
F32R = mybir.dt.float32r
I32 = mybir.dt.int32
ALU = mybir.AluOpType
ACT = mybir.ActivationFunctionType
AX_X = mybir.AxisListType.X

P = 128
D = 1024
KC = D // P
TP, TS = 256, 8
NT = TP + TS
G, H, S = 64, 16, 64
L = 8
NB = TP // L
UC = NB + TS
SMID = 4
GH = G // 2
G8 = P // H
NH, NKV, HD, R = 16, 4, 64, 4
W = 128
NBUCK = 32
SCALE = 1.0 / math.sqrt(HD)
NEG = -1e30
DFF = 2816
E, DFE = 8, 3584
EPS = 1e-6
TILE = 2048
NF = DFF // P
GLU0, GU0, DN0, KV0, Q0, O0, NDENSE = 0, 8, 30, 41, 43, 47, 51
JE, NGU, NDE = DFE // 512, 28, 14
NE = NGU + NDE
RING = 6
HT_BANK = (1, 2, 5, 6, 7, 0)
GATHER0, GATHER = (3, 0), (0, 2)
S_BANK = (0, 1, 6)
NORM_BANK = (0, 4, 0, 4, 0)
SPLIT = 3
BANK = 512
TWO_PI_HI = 6.28125
TWO_PI_LO = 2 * math.pi - TWO_PI_HI
MAGIC = 1.5 * 2.0 ** 23
PI_IN = 3.1415925
HEADS = [(2 * gp + b) * R + r for gp in range(2) for r in range(R) for b in range(2)]
G_MIX0, G_MIX1, G_FFN0, G_FFN1, G_KV, G_FIN, SSM_D = range(7)


def build(nc, xT, vecs, wd, we, wr, a_re, a_im, log_dt, bq, bx, cq, cx, h0q, h0x,
          kcT, vc, sinks, relb, onehot,
          yT, hp_out, hs_out, kp_out, vp_out, ks_out, vs_out):
    with ExitStack() as ctx:
        cur = [ctx]

        def sb(name, shape, dt=F32):
            return cur[0].enter_context(nc.sbuf_tensor(name, shape, dt))

        sems = {}

        def sem(name):
            if name not in sems:
                sems[name] = ctx.enter_context(nc.semaphore(name))
            return sems[name]

        ps = ctx.enter_context(nc.psum_tensor("ps", [P, 8, BANK], F32))
        bias_dram = nc.dram_tensor("bias_rows", (NH, P, 384), F32).ap()

        X = sb("X", [P, KC, NT])

        def in_one_place(stack, *tensors):
            for t in tensors:
                with ExitStack() as own:
                    cur[0] = own if t is not tensors[-1] else stack
                    made = [sb(*a) for a in t]
                yield made if len(made) > 1 else made[0]
            cur[0] = stack

        XN, (XEH, XEL), XNL = in_one_place(ctx,
            [("XN", [P, KC, NT])], [("XEH", [P, KC, P], F32R), ("XEL", [P, KC, P], F32R)],
            [("XNL", [P, KC, NT], F32R)])
        TMP, (YEH, YEL), XNH = in_one_place(ctx,
            [("TMP", [P, KC, NT])], [("YEH", [P, D], F32R), ("YEL", [P, D], F32R)],
            [("XNH", [P, KC, NT], F32R)])
        SQ = sb("SQ", [P, 2, NT])
        rstd = sb("rstd", [P, NT])
        root = sb("root", [P, NT])
        vec = sb("vec", [P, 7, KC])
        ones = sb("ones", [P, P])
        ident = sb("ident", [P, P])
        epsb = sb("epsb", [P, 1])
        halfpi = sb("halfpi", [P, 1])
        ahead = sb("ahead", [P, 1])

        ssm = ExitStack()
        cur[0] = ssm
        swp = sb("swp", [P, P])
        sel, sel_r = in_one_place(ssm, [("sel", [P, 8, 240])], [("sel_r", [P, 8, 240], F32R)])
        tmask = sb("tmask", [P, P])
        sgn = sb("sgn", [P, 1])
        nsgn = sb("nsgn", [P, 1])
        kramp = sb("kramp", [P, 9])
        jramp = sb("jramp", [P, NB])
        are, aim, dtt = sb("are", [P, G]), sb("aim", [P, G]), sb("dtt", [P, G])
        BQ, BX, CQ, CX = (sb(n, [P, GH, H]) for n in ("BQ", "BX", "CQ", "CX"))
        H0Q, H0X = sb("H0Q", [P, G, TS]), sb("H0X", [P, G, TS])
        q = [sb(f"q{i}", [P, G]) for i in range(14)]
        MT = sb("MT", [P, 9, G])
        T9 = [sb(f"t9{i}", [P, 9, G]) for i in range(2)]
        ER, EI = sb("ER", [P, 9, G]), sb("EI", [P, 9, G])
        TA, TB, TC = (sb(n, [P, GH, NB]) for n in ("TA", "TB", "TC"))
        COS, SS = sb("COS", [P, GH, NB]), sb("SS", [P, GH, NB])
        AM, TM = sb("AM", [P, GH, P]), sb("TM", [P, GH, P])
        CM = [sb(f"CM{i}", [P, GH, P]) for i in range(2)]
        YS = [sb(n, [P, G, UC], F32R) for n in ("YSH", "YSL")]
        PT = TC[:, 0:GH // 2, :].rearrange("p a (b h) -> p (a b) h", h=H)
        CT = sb("CT", [P, GH, H])
        AT = sb("AT", [P, 8, P])
        VB = sb("VB", [P, 2, 8 * UC])
        U = sb("U", [P, G, UC])
        WV = sb("WV", [P, 1 + GH * NB])
        R8 = sb("R8", [P, GH, NB])
        SV = sb("SV", [P, GH, NB])
        VS = MT[:, 0:4, :].rearrange("p a b -> p (a b)").rearrange("p (g n) -> p g n", n=TS)
        HM = sb("HM", [P, GH, UC])
        GL = sb("GL", [P, GH])
        HP = sb("HP", [P, G])
        HS = H0X
        ssm.close()

        cur[0] = ctx
        raw = [sb(f"raw{i}", [P, TILE]) for i in range(RING)]
        WH = [sb(f"WH{i}", [P, TILE], F32R) for i in range(SPLIT)]
        WL = [sb(f"WL{i}", [P, TILE], F32R) for i in range(SPLIT)]
        WR = sb("WR", [P, KC, E])
        tri = sb("tri", [P, P])
        slot = sb("slot", [P, 3, P])
        LG = sb("LG", [P, 3, E])
        dz = sb("dz", [P, 3, E])
        attn = ExitStack()
        inner = ExitStack()
        cur[0] = inner
        QT = sb("QT", [P, KC, NT])
        KCT = sb("KCT", [P, TS, 2, W])
        VC = sb("VC", [P, TS, NKV * HD])
        with ExitStack() as a1:
            cur[0] = a1
            XQ, XQH = sb("XQ", [P, KC, NT]), sb("XQH", [P, KC, NT], F32R)
        with ExitStack() as a1:
            cur[0] = a1
            XQL = sb("XQL", [P, KC, NT], F32R)
        cur[0] = inner
        OTH, OTL = sb("OTH", [P, KC, NT], F32R), sb("OTL", [P, KC, NT], F32R)
        inner.close()
        cur[0] = attn
        FAH = sb("FAH", [P, NF, NT], F32R)
        FAL = sb("FAL", [P, NF, NT], F32R)
        SG = sb("SG", [P, 2, NT])
        KT = sb("KT", [P, 2, NT])
        VT = sb("VT", [P, 3, NKV * HD])
        BIAS = sb("BIAS", [P, NH, 2 * W])
        BSM = sb("BSM", [P, W])
        relx = sb("relx", [NBUCK + 1, NH])
        SINK = sb("SINK", [P, NH])
        SINKC = sb("SINKC", [P, 1])
        SC = sb("SC", [P, 3, 384])
        mx = sb("mx", [P, 3, 2])
        nm = sb("nm", [P, 3, 2])
        sm = sb("sm", [P, 3, 2])
        es = sb("es", [P, 3, 2])
        rd = sb("rd", [P, 3, 2])
        PTT = sb("PTT", [P, 2, 384])
        brow, oneh = SC[0:NH, 0, :], SC[0:NBUCK + 1, 1, :]
        STS = SG[:, 0, 0:P]
        attn.close()
        cur[0] = ctx
        r1, r2, r3, r4 = (sb(f"r{i}", [P, 3, E]) for i in range(1, 5))
        top = sb("top", [P, 3, 8])
        v1 = sb("v1", [P, 3])
        SELM = sb("SELM", [P, 3, E])
        GATE = sb("GATE", [P, 3, E])
        POS = sb("POS", [P, 3, E])
        cnt = sb("cnt", [1, 2 * E])
        run = sb("run", [1, 2 * E + 1])
        plan = sb("plan", [1, 4 * E + 1], I32)
        HTH, HTL = sb("HTH", [P, 3, D], F32R), sb("HTL", [P, 3, D], F32R)
        DSP = sb("DSP", [P, 3, P], F32R)
        DG = sb("DG", [P, 3, P])
        GSH, GSL = sb("GSH", [P, NT], F32R), sb("GSL", [P, NT], F32R)
        SIL = sb("SIL", [P, 2, BANK])
        AC = sb("AC", [P, 2, BANK])
        AFH, AFL = sb("AFH", [P, DFE // P, P], F32R), sb("AFL", [P, DFE // P, P], F32R)

        block = ctx.enter_context(nc.Block())

        def at(eng, tile, step=0, per=1):
            r, stride, c = tile
            value = c + step
            return per * value if r is None else eng.snap(r * (stride * per) + per * value)

        def loads(eng, tile):
            r, stride, c = tile
            value = 16 * (c // RING + 1)
            return value if r is None else eng.snap(r * (16 * stride // RING) + value)

        def dense(n):
            return (None, 0, n)

        def expert_tile(r, m):
            return (r, NE, NDENSE + m)

        def after(tile, k):
            r, stride, c = tile
            return (r, stride, c + k)

        def tokens(t):
            return P if t < 2 else TS

        loaded = [sem(f"tile_loaded_{i}") for i in range(RING)]
        split = sem("tiles_split")
        used = sem("tiles_used")
        PAIRS = 6
        TURNS = NF // PAIRS

        @block.sync
        def _(sp):
            sp.dma_start(X[:, :, :], xT).then_inc(sem("x_loaded"), 16)
            sp.dma_start(vec[:, :, :], vecs).then_inc(sem("vec_loaded"), 16)
            for half in range(2):
                rows = slice(64 * half, 64 * half + 64)
                sp.dma_start(are[rows, :], a_re).then_inc(sem("lam_loaded"), 16)
                sp.dma_start(aim[rows, :], a_im).then_inc(sem("lam_loaded"), 16)
            sp.dma_start(dtt[:, :], log_dt.to_broadcast([P, G])).then_inc(sem("lam_loaded"), 16)
            sp.dma_start(H0Q[:, :, :], h0q).then_inc(sem("h0_loaded"), 16)
            sp.dma_start(H0X[:, :, :], h0x).then_inc(sem("h0_loaded"), 16)
            for hf in range(2):
                gs = slice(hf * GH, hf * GH + GH)
                if hf == 1:
                    sp.wait_ge(sem("a_built"), 1)
                sp.dma_start(BQ[:, :, :], bq[:, gs, :]).then_inc(sem("b_loaded"), 16)
                sp.dma_start(BX[:, :, :], bx[:, gs, :]).then_inc(sem("b_loaded"), 16)
                if hf == 1:
                    sp.wait_ge(sem("c_built"), 1)
                sp.dma_start(CQ[:, :, :], cq[:, gs, :]).then_inc(sem("c_loaded"), 16)
                sp.dma_start(CX[:, :, :], cx[:, gs, :]).then_inc(sem("c_loaded"), 16)
            sp.wait_ge(sem("states_done"), 2)
            sp.dma_start(hp_out, HP[:, :]).then_inc(sem("stored"), 16)
            sp.dma_start(hs_out, HS[:, :, :]).then_inc(sem("stored_ssm"), 16)
            sp.wait_ge(sem("stored"), 16)
            sp.wait_ge(sem("stored_ssm"), 16)
            sp.wait_ge(sem("y_mixed"), 8)
            for n in range(RING):
                sp.dma_start(raw[n][:, :], wd[n]).then_inc(loaded[n], 16)

            def load(tile, src):
                free = at(sp, tile, 1 - RING)
                sp.wait_ge(split, free)
                sp.dma_start(raw[tile[2] % RING][:, :], src).then_inc(loaded[tile[2] % RING], 16)

            turns = NDENSE // RING - 1
            with sp.Fori(0, turns) as r:
                for i in range(RING):
                    load((r, RING, RING + i), wd[bass.ds(r * RING + (RING + i), 1)].rearrange("a p n -> (a p) n"))
            for n in range((turns + 1) * RING, NDENSE):
                load(dense(n), wd[n])

            def expert_tiles(e, r):
                for m in range(NE):
                    load(expert_tile(r, m), we[bass.ds(e * NE + m, 1)].rearrange("a p n -> (a p) n"))

            with sp.Fori(0, E) as e:
                expert_tiles(e, e)
            sp.wait_ge(sem("plan_ready"), 1)
            any_more = sp.value_load(plan[0:1, 4 * E:4 * E + 1], min_val=E, max_val=E + 4)
            with sp.If(any_more > E):
                with sp.Fori(0, E) as e:
                    for k in range(2):
                        i = sp.snap(e * 2 + k)
                        more = sp.value_load(plan[0:1, bass.ds(i, 1)], min_val=0, max_val=1)
                        with sp.If(more > 0):
                            r = sp.value_load(plan[0:1, bass.ds(i + 2 * E, 1)], min_val=E, max_val=E + 4)
                            expert_tiles(e, r)
            for k in range(2):
                sp.wait_ge(sem("xn_ready"), 4 * KC + 4 * (k + 1))
                sp.dma_start(yT[:, 4 * k:4 * k + 4, :], XN[:, 4 * k:4 * k + 4, :]).then_inc(sem("y_stored"), 16)
            sp.wait_ge(sem("y_stored"), 32)

        @block.gpsimd
        def _(pool):
            g = nc.gpsimd
            g.memset(ones[:, :], 1.0).then_inc(sem("pool_step"), 1)
            g.memset(epsb[:, :], EPS).then_inc(sem("pool_step"), 1)
            g.memset(halfpi[:, :], math.pi / 2).then_inc(sem("pool_step"), 1)
            g.memset(sel[:, :, :], 0.0).then_inc(sem("pool_step"), 1)
            g.iota(kramp[:, :], pattern=[[1, 9]], base=-4, channel_multiplier=0,
                   allow_small_or_imprecise_dtypes=True).then_inc(sem("pool_step"), 1)
            g.iota(jramp[:, :], pattern=[[1, NB]], base=0, channel_multiplier=0,
                   allow_small_or_imprecise_dtypes=True).then_inc(sem("pool_step"), 1)
            pool.wait_ge(sem("pool_step"), 6)
            g.affine_select(out=ident[:, :], in_=ones[:, :], compare_op=ALU.is_equal, fill=0.0, base=0,
                            pattern=[[-1, P]], channel_multiplier=1).then_inc(sem("consts"), 1)
            g.affine_select(out=swp[:, 0:64], in_=ones[:, 0:64], compare_op=ALU.is_equal, fill=0.0, base=-64,
                            pattern=[[-1, 64]], channel_multiplier=1).then_inc(sem("consts"), 1)
            g.affine_select(out=swp[:, 64:128], in_=ones[:, 0:64], compare_op=ALU.is_equal, fill=0.0, base=0,
                            pattern=[[-1, 64]], channel_multiplier=1).then_inc(sem("consts"), 1)
            g.affine_select(out=sel[:, :, 112:128], in_=ones[:, :].rearrange("p (m x) -> p m x", m=8),
                            compare_op=ALU.is_equal, fill=0.0, base=0, pattern=[[-16, 8], [-1, 16]],
                            channel_multiplier=1).then_inc(sem("consts"), 1)
            g.affine_select(out=tmask[:, :], in_=ones[:, :], compare_op=ALU.is_ge, fill=0.0, base=15,
                            pattern=[[16, 8], [0, 16]], channel_multiplier=-1).then_inc(sem("consts"), 1)
            pool.wait_ge(sem("consts"), 5)
            pool.wait_ge(sem("pow_ready"), 1)
            n = 0
            for hf in range(2):
                gs = slice(hf * GH, hf * GH + GH)
                pool.wait_ge(sem("c_loaded"), 32 * (hf + 1))
                for s in range(L):
                    fr = T9[0][:, s, gs].unsqueeze(2).to_broadcast([P, GH, H])
                    fs = T9[1][:, s, gs].unsqueeze(2).to_broadcast([P, GH, H])
                    out = CM[hf][:, :, s * H:(s + 1) * H]
                    if n:
                        pool.wait_ge(sem("c_step"), n)
                    g.tensor_tensor(out, CQ[:, :, :], fr, ALU.mult).then_inc(sem("c_step"), 1)
                    g.tensor_tensor(CT[:, :, :], CX[:, :, :], fs, ALU.mult).then_inc(sem("c_step"), 1)
                    n += 2
                    pool.wait_ge(sem("c_step"), n)
                    ins = g.tensor_tensor(out, out, CT[:, :, :], ALU.add)
                    if s < L - 1:
                        ins.then_inc(sem("c_step"), 1)
                        n += 1
                    else:
                        ins.then_inc(sem("c_built"), 1)
                        pool.wait_ge(sem("c_built"), hf + 1)
            pool.wait_ge(sem("y_mixed"), 8)
            g.affine_select(out=tri[:, :], in_=ones[:, :], compare_op=ALU.is_gt, fill=0.0, base=0,
                            pattern=[[1, P]], channel_multiplier=-1).then_inc(sem("route_consts"), 1)
            g.iota(slot[:, :, :], pattern=[[P, 3], [1, P]], base=0, channel_multiplier=0,
                   allow_small_or_imprecise_dtypes=True).then_inc(sem("route_consts"), 1)
            g.memset(LG[:, :, :], 0.0).then_inc(sem("route_consts"), 1)
            g.memset(dz[:, :, :], 1.0).then_inc(sem("route_consts"), 1)
            pool.wait_ge(sem("route_consts"), 4)
            g.memset(dz[:, :, 0:1], 0.0).then_inc(sem("route_consts"), 1)
            pool.dma_start(relx[0:NBUCK, :], relb).then_inc(sem("rel_loaded"), 16)
            pool.dma_start(oneh[:, :], onehot).then_inc(sem("rel_loaded"), 16)
            pool.dma_start(SINK[:, :], sinks.to_broadcast([P, NH])).then_inc(sem("sink_loaded"), 16)
            for b in range(TS):
                pool.dma_start(SINKC[b * NH:(b + 1) * NH, :], sinks.rearrange("a h -> h a"))\
                    .then_inc(sem("sink_loaded"), 16)
            pool.dma_start(WR[:, :, :], wr).then_inc(sem("router_loaded"), 16)
            pool.wait_ge(sem("bias_rows_ready"), 1)
            pool.dma_start(bias_dram, brow[:, :].unsqueeze(1).to_broadcast([NH, P, 384]))\
                .then_inc(sem("bias_stored"), 16)
            pool.wait_ge(sem("bias_stored"), 16)
            for h in range(NH):
                src = bias_dram[h, :, 127:127 + 2 * W]
                src = bass.AP(src.tensor, src.offset, [[384 - 1, P], [1, 2 * W]])
                pool.dma_start(BIAS[:, h, :], src).then_inc(sem("bias_loaded"), 16)
            for b in range(TS):
                pool.dma_start(BSM[b * NH:(b + 1) * NH, :], bias_dram[:, 0, W:2 * W]).then_inc(sem("bias_loaded"), 16)

            pool.wait_ge(used, KV0)
            for b in range(TS):
                pool.dma_start(KCT[:, b, :, 0:W - 1], kcT[b][:, :, 1:W]).then_inc(sem("cache_loaded"), 16)
            pool.dma_start(VC[0:W - 1, :, :], vc[1:W]).then_inc(sem("cache_loaded"), 16)
            pool.wait_ge(sem("v_ready"), 3)
            pool.dma_start(VC[W - 1:W, :, :], VT[P - TS:P, 2, :]).then_inc(sem("new_v_loaded"), 16)
            pool.wait_ge(sem("cache_loaded"), 16 * (TS + 1))
            pool.wait_ge(sem("new_v_loaded"), 16)
            pool.wait_ge(sem("kc_ready"), 1)
            pool.dma_start(kp_out, KT[:, :, TP - W:TP]).then_inc(sem("kv_stored"), 16)
            pool.dma_start(vp_out, VT[:, 1, :]).then_inc(sem("kv_stored"), 16)
            pool.dma_start(ks_out, KCT[:, :, :, :]).then_inc(sem("kv_stored"), 16)
            pool.dma_start(vs_out, VC[:, :, :]).then_inc(sem("kv_stored"), 16)
            pool.wait_ge(sem("kv_stored"), 64)

        @block.scalar
        def _(act):
            a = nc.scalar

            def square(i, c, ready, n_ready):
                act.wait_ge(ready, n_ready)
                n = KC * i + c
                if n >= 2:
                    act.wait_ge(sem("sq_summed"), n - 1)
                a.activation(SQ[:, c % 2, :], X[:, c, :], ACT.Square).then_inc(sem("squared"), 1)

            def table_ahead(func):
                a.activation(ahead[:, :], epsb[:, :], func)

            def norm_root(i):
                act.wait_ge(sem("sq_summed"), KC * (i + 1))
                if i:
                    act.wait_ge(sem("rstd_ready"), i)
                else:
                    act.wait_ge(sem("consts"), 5)
                a.activation(root[:, :], ps[:, NORM_BANK[i], 0:NT], ACT.Sqrt, bias=epsb[:, :], scale=1.0 / D)\
                    .then_inc(sem("root_ready"), 1)

            def norm(i, ready, n_ready):
                for c in range(KC):
                    square(i, c, ready, n_ready(c))
                norm_root(i)

            act.wait_ge(sem("lam_loaded"), 80)
            a.activation(q[0][:, :], dtt[:, :], ACT.Tanh, scale=1.0 / 32).then_inc(sem("tanh_ready"), 1)
            norm(0, sem("x_loaded"), lambda c: 16)
            act.wait_ge(sem("decay_ready"), 1)
            a.activation(q[3][:, :], q[1][:, :], ACT.Tanh, scale=0.5).then_inc(sem("tanh_ready"), 1)
            act.wait_ge(sem("phase9_ready"), 1)
            a.activation(EI[:, :, :], T9[0][:, :, :], ACT.Sin).then_inc(sem("sin9_ready"), 1)
            a.activation(ER[:, :, :], T9[0][:, :, :], ACT.Abs).then_inc(sem("sin9_ready"), 1)
            a.activation(q[6][:, :], q[4][:, :], ACT.Sin, scale=0.5).then_inc(sem("sin9_ready"), 1)
            act.wait_ge(sem("sin9_ready"), 3)
            a.activation(ER[:, :, :], ER[:, :, :], ACT.Sin, scale=-1.0, bias=halfpi[:, :])\
                .then_inc(sem("sin9_ready"), 1)
            for k in range(G8):
                act.wait_ge(sem("u_moved"), k + 1)
                a.copy(U[:, :, :].rearrange("p (c k) n -> p k c n", k=G8)[:, k],
                       ps[:, k % 2, 0:KC * UC].rearrange("p (c n) -> p c n", c=KC)).then_inc(sem("u_ready"), 1)
            a.copy(sel_r[:, :, :], sel[:, :, :]).then_inc(sem("sel_r_ready"), 1)
            for hf in range(2):
                act.wait_ge(sem("phase_ready"), hf + 1)
                if hf:
                    act.wait_ge(sem("states_done"), 1)
                a.activation(SS[:, :, :], TA[:, :, :], ACT.Sin, scale=sgn[:, :]).then_inc(sem("turn_ready"), 1)
                a.activation(COS[:, :, :], TA[:, :, :], ACT.Abs).then_inc(sem("turn_ready"), 1)
                act.wait_ge(sem("turn_ready"), 3 * hf + 2)
                a.activation(COS[:, :, :], COS[:, :, :], ACT.Sin, scale=-1.0, bias=halfpi[:, :])\
                    .then_inc(sem("turn_ready"), 1)
                for b in range(GH // 4):
                    act.wait_ge(sem("a_turned"), 8 * hf + b + 1)
                    if 8 * hf + b >= 2:
                        act.wait_ge(sem("v_made"), (8 * hf + b) // 2)
                    dst = AT[:, 4 * (b % 2):4 * (b % 2) + 4, :]
                    src = ps[:, 4 + b % 2, :].rearrange("p (g n) -> p g n", g=4)
                    a.copy(dst, src).then_inc(sem("at_ready"), 1)
                    if b % 2:
                        j = b // 2
                        act.wait_ge(sem("v_made"), 4 * hf + j + 1)
                        if j >= 2:
                            act.wait_ge(sem("v_turned"), 4 * hf + j - 1)
                        a.copy(VB[:, j % 2, :], ps[:, 6 if j % 2 == 0 else 0, 0:8 * UC]).then_inc(sem("v_in_sbuf"), 1)
                for b in range(4):
                    act.wait_ge(sem("y_made"), 4 * hf + b + 1)
                    a.copy(YS[0][:, hf * GH + 8 * b:hf * GH + 8 * b + 8, :],
                           ps[:, 4 + b % 2, 0:8 * UC].rearrange("p (g n) -> p g n", g=8)).then_inc(sem("ysh_ready"), 1)
            table_ahead(ACT.Gelu_apprx_tanh)
            act.wait_ge(sem("y_mixed"), 8)

            def hi(tile):
                slot_ = tile[2] % RING
                act.wait_ge(loaded[slot_], loads(act, tile))
                if tile[0] is not None or tile[2] >= SPLIT:
                    act.wait_ge(used, at(act, tile, 1 - SPLIT))
                a.copy(WH[tile[2] % SPLIT][:, :], raw[slot_][:, :]).then_inc(sem("hi_made"), 1)

            def xn_hi(dst, src, ready, base):
                for k in range(4):
                    act.wait_ge(ready, base + 2 * k + 2)
                    c2 = slice(2 * k, 2 * k + 2)
                    a.copy(dst[:, c2, :], src[:, c2, :]).then_inc(sem("xn_hi_made"), 1)

            for k in range(5):
                if k < 4:
                    c2 = slice(2 * k, 2 * k + 2)
                    a.activation(XN[:, c2, :], TMP[:, c2, :], ACT.Gelu_apprx_tanh).then_inc(sem("z_ready"), 1)
                if k:
                    c2 = slice(2 * k - 2, 2 * k)
                    act.wait_ge(sem("z_ready"), k)
                    a.copy(XNH[:, c2, :], XN[:, c2, :]).then_inc(sem("xn_hi_made"), 1)
            for n in range(SPLIT):
                hi(dense(n))

            def gate(tile, func, first):
                b = tile[2] % 2
                act.wait_ge(used, at(act, tile, 1))
                if tile[0] is not None or tile[2] >= 2:
                    act.wait_ge(sem("pair_done"), at(act, tile, -1))
                a.activation(SG[:, b, :], ps[:, 2 * b + first, 0:NT], func).then_inc(sem("gated"), 1)

            for n in range(GU0):
                gate(dense(n), ACT.Sigmoid, 1)
                if n == GU0 - 1:
                    table_ahead(ACT.Sqrt)
                if n:
                    square(1, n - 1, sem("pair_done"), n)
                if n < GU0 - 1:
                    hi(dense(n + SPLIT))
            square(1, KC - 1, sem("pair_done"), KC)
            act.wait_ge(sem("bias_made"), 1)
            a.copy(brow[:, :], ps[0:NH, 7, 0:384]).then_inc(sem("bias_rows_ready"), 1)
            norm_root(1)
            hi(dense(GU0 - 1 + SPLIT))
            xn_hi(XNH, XN, sem("xn_ready"), KC)
            with act.Fori(0, TURNS) as r:
                for i in range(PAIRS):
                    gate((r, PAIRS, GU0 + i), ACT.Silu, 0)
                    hi((r, PAIRS, GU0 + i + SPLIT))
            for n in range(GU0 + TURNS * PAIRS, DN0):
                gate(dense(n), ACT.Silu, 0)
                hi(dense(n + SPLIT))
            for n in range(DN0, KV0 - 1):
                hi(dense(n + SPLIT))
            table_ahead(ACT.Sqrt)
            for c in range(KC):
                square(2, c, sem("resid_ffn"), c + 1)
            norm_root(2)
            hi(dense(KV0 - 1 + SPLIT))
            xn_hi(XNH, XN, sem("xn_ready"), 2 * KC)
            xn_hi(XQH, XQ, sem("xq_ready"), 0)
            act.wait_ge(used, KV0 + 1)
            for i in range(2):
                a.copy(KT[:, i, :], ps[:, 2 * (KV0 % 2) + i, 0:NT]).then_inc(sem("k_ready"), 1)
            hi(dense(KV0 + SPLIT))
            act.wait_ge(used, KV0 + 2)
            for t in range(3):
                rows = slice(0, P) if t < 2 else slice(96, P)
                a.copy(VT[rows, t, :], ps[rows, 4 + t, 0:NKV * HD]).then_inc(sem("v_ready"), 1)
            hi(dense(KV0 + 1 + SPLIT))
            for n in range(Q0, O0):
                act.wait_ge(used, n + 1)
                for i in range(2):
                    a.copy(QT[:, 2 * (n - Q0) + i, :], ps[:, 2 * (n % 2) + i, 0:NT]).then_inc(sem("q_ready"), 1)
                hi(dense(n + SPLIT))
            act.wait_ge(sem("k_ready"), 2)
            act.wait_ge(sem("cache_loaded"), 16 * (TS + 1))
            a.copy(KCT[:, :, :, W - 1].rearrange("p b k -> p k b"), KT[:, :, TP:NT]).then_inc(sem("kc_ready"), 1)
            def exps(h):
                b = h % 3
                act.wait_ge(sem("shift_ready"), h + 1)
                a.activation(SC[:, b, 0:W], SC[:, b, 0:W], ACT.Exp, bias=nm[:, b, 0:1],
                             accum_out=sm[:, b, 0:1]).then_inc(sem("exp_ready"), 1)
                if h < NH:
                    a.activation(SC[:, b, W:3 * W], SC[:, b, W:3 * W], ACT.Exp, bias=nm[:, b, 1:2],
                                 accum_out=sm[:, b, 1:2]).then_inc(sem("exp_ready"), 1)
                    a.activation(es[:, b, :], nm[:, b, :], ACT.Exp, bias=SINK[:, HEADS[h]:HEADS[h] + 1])\
                        .then_inc(sem("exp_ready"), 1)
                else:
                    a.activation(es[:, b, 0:1], nm[:, b, 0:1], ACT.Exp, bias=SINKC[:, :])\
                        .then_inc(sem("exp_ready"), 1)

            def second_block(h):
                act.wait_ge(sem("rd_ready"), h + 1)
                a.activation(SC[:, h % 3, W:3 * W], SC[:, h % 3, W:3 * W], ACT.Copy, scale=rd[:, h % 3, 1:2])\
                    .then_inc(sem("p2_ready"), 1)

            def turned_out(h):
                act.wait_ge(sem("p_turned"), h + 1)
                if h >= 2:
                    act.wait_ge(sem("pv_made"), h - 1)
                n = 3 * W if h < NH else W
                a.copy(PTT[:, h % 2, 0:n], ps[:, 2 + h % 2, 0:n]).then_inc(sem("pt_ready"), 1)

            for h in range(NH):
                exps(h)
                if h >= 1:
                    second_block(h - 1)
                if h >= 2:
                    turned_out(h - 2)
            second_block(NH - 1)
            turned_out(NH - 2)
            exps(NH)
            turned_out(NH - 1)
            turned_out(NH)
            table_ahead(ACT.Sqrt)
            for n in range(O0, NDENSE):
                for c in range(2 * (n - O0), 2 * (n - O0) + 2):
                    square(3, c, sem("resid_o"), c + 1)
                if n == NDENSE - 1:
                    norm_root(3)
                hi(dense(n + SPLIT))
            act.wait_ge(sem("kv_stored"), 64)
            for t in range(3):
                rows = tokens(t)
                for hf in range(2):
                    act.wait_ge(sem("h_turned"), 2 * t + hf + 1)
                    if t == 2 and hf == 0:
                        act.wait_ge(sem("gap_ready"), 1)
                        a.activation(r4[:, :, :], r3[:, :, :], ACT.Exp).then_inc(sem("gexp_ready"), 1)
                    a.copy(HTH[0:rows, t, hf * 512:hf * 512 + 512], ps[0:rows, HT_BANK[2 * t + hf], :]).then_inc(sem("hth_ready"), 1)
            def expert_gate_up(r, j):
                for kq in range(4):
                    m = 4 * j + kq
                    if kq == 1 and j:
                        hidden_hi(r, j - 1)
                    if kq == 3:
                        act.wait_ge(used, at(act, expert_tile(r, m), 1))
                        if j >= 2:
                            act.wait_ge(sem("act_ready"), act.snap(JE * r + (j - 1)))
                        a.activation(SIL[:, j % 2, :], ps[:, 2 * (j % 2), :], ACT.Silu).then_inc(sem("silu_ready"), 1)
                    hi(expert_tile(r, m + SPLIT))

            def hidden_hi(r, j):
                act.wait_ge(sem("act_turned"), act.snap(JE * r + (j + 1)))
                a.copy(AFH[:, 4 * j:4 * j + 4, :], ps[:, 6 + j % 2, :].rearrange("p (c n) -> p c n", c=4))\
                    .then_inc(sem("afh_ready"), 1)

            def tokens_hi(n, bank=GATHER[0]):
                act.wait_ge(sem("gathered_hi"), n)
                a.copy(XEH[:, :, :].rearrange("p c n -> p (c n)"), ps[:, bank:bank + 2, :].rearrange("p b n -> p (b n)"))\
                    .then_inc(sem("xeh_ready"), 1)

            def expert_rest(r, more):
                for j in range(1, JE):
                    expert_gate_up(r, j)
                for d in range(NDE):
                    if d == 1:
                        hidden_hi(r, JE - 1)
                    if d == 3:
                        act.wait_ge(sem("gate_turned"), act.snap(r + 1))
                        a.copy(GSH[:, :], ps[:, 7, 0:NT]).then_inc(sem("gsh_ready"), 1)
                    if d == 6 and more:
                        tokens_hi(act.snap(r + 2))
                    if d == NDE - 1:
                        act.wait_ge(used, at(act, expert_tile(r, NE)))
                        a.copy(YEH[:, :], ps[:, 4:6, :].rearrange("p b n -> p (b n)")).then_inc(sem("yeh_ready"), 1)
                    if more or NGU + d + SPLIT < NE:
                        hi(expert_tile(r, NGU + d + SPLIT))
                if more:
                    expert_gate_up(act.snap(r + 1), 0)

            zero = act.snap(0)
            tokens_hi(1, GATHER0[0])
            expert_gate_up(zero, 0)
            with act.Fori(0, E - 1) as e:
                expert_rest(e, True)
            last = act.snap(zero + (E - 1))
            expert_rest(last, False)
            act.wait_ge(sem("plan_ready"), 1)
            any_more = act.value_load(plan[0:1, 4 * E:4 * E + 1], min_val=E, max_val=E + 4)
            with act.If(any_more > E):
                with act.Fori(0, 2 * E) as i:
                    more = act.value_load(plan[0:1, bass.ds(i, 1)], min_val=0, max_val=1)
                    with act.If(more > 0):
                        r = act.value_load(plan[0:1, bass.ds(i + 2 * E, 1)], min_val=E, max_val=E + 4)
                        for m in range(SPLIT):
                            hi(expert_tile(r, m))
                        tokens_hi(act.snap(r + 1))
                        expert_gate_up(r, 0)
                        expert_rest(r, False)
            table_ahead(ACT.Sqrt)
            norm(4, sem("moe_done"), lambda c: 1)

        @block.vector
        def _(dve):
            v = nc.vector
            steps = [0]

            def link(ins):
                steps[0] += 1
                ins.then_inc(sem("dve_step"), 1)
                dve.wait_ge(sem("dve_step"), steps[0])

            def reduce_phase(x, t, last=None):
                link(v.tensor_scalar(t, x, 1.0 / (2 * math.pi), MAGIC, ALU.mult, ALU.add))
                link(v.tensor_scalar(t, t, MAGIC, None, ALU.subtract))
                link(v.scalar_tensor_tensor(out=x, in0=t, scalar=-TWO_PI_HI, in1=x, op0=ALU.mult, op1=ALU.add))
                link(v.scalar_tensor_tensor(out=x, in0=t, scalar=-TWO_PI_LO, in1=x, op0=ALU.mult, op1=ALU.add))
                ins = v.tensor_scalar(x, x, PI_IN, -PI_IN, ALU.min, ALU.max)
                if last is None:
                    link(ins)
                else:
                    ins.then_inc(last, 1)

            def norm(i, gidx, done, lo_part=None):
                dve.wait_ge(sem("root_ready"), i + 1)
                v.reciprocal(rstd[:, :], root[:, :]).then_inc(sem("rstd_ready"), 1)
                dve.wait_ge(sem("rstd_ready"), i + 1)
                if lo_part is None:
                    scale(XN, gidx, done, range(KC))
                else:
                    scale_and_split(XN, gidx, done, *lo_part)

            def scale_and_split(out, gidx, done, n_hi, lo_, hi_):
                for k in range(5):
                    if k < 4:
                        scale(out, gidx, done, (2 * k, 2 * k + 1))
                    if k:
                        xn_lo(n_hi + k, k - 1, lo_, out, hi_)

            def xn_lo(n_hi, k, lo_, src, hi_):
                c2 = slice(2 * k, 2 * k + 2)
                dve.wait_ge(sem("xn_hi_made"), n_hi)
                v.tensor_tensor(lo_[:, c2, :], src[:, c2, :], hi_[:, c2, :].bitcast(F32), ALU.subtract)\
                    .then_inc(sem("xn_split"), 1)

            def scale(out, gidx, done, chunks):
                for c in chunks:
                    v.scalar_tensor_tensor(out=out[:, c, :], in0=X[:, c, :], scalar=vec[:, gidx, c:c + 1],
                                           in1=rstd[:, :], op0=ALU.mult, op1=ALU.mult).then_inc(done, 1)

            for rows, x in ((slice(0, 64), 1.0), (slice(64, 128), -1.0)):
                link(v.memset(sgn[rows, :], x))
                link(v.memset(nsgn[rows, :], -x))
            dve.wait_ge(sem("lam_loaded"), 80)
            dve.wait_ge(sem("tanh_ready"), 1)
            link(v.tensor_scalar(q[1][:, :], q[0][:, :], -1.0, 1.0, ALU.mult, ALU.add))
            link(v.reciprocal(q[1][:, :], q[1][:, :]))
            link(v.scalar_tensor_tensor(out=dtt[:, :], in0=q[0][:, :], scalar=1.0, in1=q[1][:, :],
                                        op0=ALU.add, op1=ALU.mult))
            for _ in range(4):
                link(v.tensor_tensor(dtt[:, :], dtt[:, :], dtt[:, :], ALU.mult))
            v.tensor_tensor(q[1][:, :], are[:, :], dtt[:, :], ALU.mult).then_inc(sem("decay_ready"), 1)
            link(v.tensor_tensor(q[4][:, :], aim[:, :], dtt[:, :], ALU.mult))
            reduce_phase(q[4][:, :], q[5][:, :])
            dve.wait_ge(sem("consts"), 5)
            dve.wait_ge(sem("vec_loaded"), 16)
            link(v.tensor_tensor(T9[0][:, :, :], q[4][:, :].unsqueeze(1).to_broadcast([P, 9, G]),
                                 kramp[:, :].unsqueeze(2).to_broadcast([P, 9, G]), ALU.mult))
            reduce_phase(T9[0][:, :, :], T9[1][:, :, :], sem("phase9_ready"))
            link(v.tensor_scalar(q[7][:, :], q[4][:, :], float(L), None, ALU.mult))
            reduce_phase(q[7][:, :], q[5][:, :])
            dve.wait_ge(sem("tanh_ready"), 2)
            t2 = q[3][:, :]
            link(v.tensor_scalar(q[8][:, :], t2, 1.0, None, ALU.add))
            link(v.tensor_scalar(q[9][:, :], t2, -1.0, 1.0, ALU.mult, ALU.add))
            link(v.reciprocal(q[10][:, :], q[8][:, :]))
            link(v.reciprocal(q[11][:, :], q[9][:, :]))
            link(v.memset(MT[:, 4, :], 1.0))
            link(v.tensor_tensor(MT[:, 5, :], q[8][:, :], q[11][:, :], ALU.mult))
            link(v.tensor_tensor(MT[:, 3, :], q[9][:, :], q[10][:, :], ALU.mult))
            for sgn_, one in ((1, 5), (-1, 3)):
                for k in range(2, 5):
                    link(v.tensor_tensor(MT[:, 4 + sgn_ * k, :], MT[:, 4 + sgn_ * (k - 1), :], MT[:, one, :], ALU.mult))
            norm(0, G_MIX0, sem("xn_ready"))
            dve.wait_ge(sem("sin9_ready"), 4)
            link(v.tensor_tensor(q[8][:, :], are[:, :], are[:, :], ALU.mult))
            link(v.tensor_tensor(q[9][:, :], aim[:, :], aim[:, :], ALU.mult))
            link(v.tensor_tensor(q[8][:, :], q[8][:, :], q[9][:, :], ALU.add))
            link(v.reciprocal(q[8][:, :], q[8][:, :]))
            link(v.scalar_tensor_tensor(out=q[9][:, :], in0=t2, scalar=2.0, in1=q[11][:, :],
                                        op0=ALU.mult, op1=ALU.mult))
            link(v.tensor_tensor(q[9][:, :], q[9][:, :], ER[:, 5, :], ALU.mult))
            link(v.tensor_tensor(q[6][:, :], q[6][:, :], q[6][:, :], ALU.mult))
            link(v.scalar_tensor_tensor(out=q[9][:, :], in0=q[6][:, :], scalar=-2.0, in1=q[9][:, :],
                                        op0=ALU.mult, op1=ALU.add))
            link(v.tensor_tensor(q[10][:, :], MT[:, 5, :], EI[:, 5, :], ALU.mult))
            link(v.tensor_tensor(q[12][:, :], q[9][:, :], are[:, :], ALU.mult))
            link(v.tensor_tensor(q[11][:, :], q[10][:, :], aim[:, :], ALU.mult))
            link(v.tensor_tensor(q[12][:, :], q[12][:, :], q[11][:, :], ALU.add))
            link(v.tensor_tensor(q[12][:, :], q[12][:, :], q[8][:, :], ALU.mult))
            link(v.tensor_tensor(q[13][:, :], q[10][:, :], are[:, :], ALU.mult))
            link(v.tensor_tensor(q[11][:, :], q[9][:, :], aim[:, :], ALU.mult))
            link(v.tensor_tensor(q[13][:, :], q[13][:, :], q[11][:, :], ALU.subtract))
            link(v.tensor_tensor(q[13][:, :], q[13][:, :], q[8][:, :], ALU.mult))
            link(v.tensor_tensor(ER[:, :, :], ER[:, :, :], MT[:, :, :], ALU.mult))
            link(v.tensor_tensor(EI[:, :, :], EI[:, :, :], MT[:, :, :], ALU.mult))
            link(v.tensor_scalar(T9[0][:, :, :], ER[:, :, :], sgn[:, :], None, ALU.mult))
            v.tensor_scalar(T9[1][:, :, :], EI[:, :, :], -1.0, None, ALU.mult).then_inc(sem("pow_ready"), 1)
            link(v.tensor_copy(q[0][:, :], ER[:, 5, :]))
            link(v.tensor_scalar(q[1][:, :], EI[:, 5, :], nsgn[:, :], None, ALU.mult))
            link(v.tensor_copy(q[2][:, :], ER[:, 7, :]))
            link(v.tensor_copy(q[3][:, :], EI[:, 7, :]))
            link(v.tensor_tensor(q[4][:, :], MT[:, 8, :], MT[:, 8, :], ALU.mult))
            cr = q[12][:, :].unsqueeze(1).to_broadcast([P, 9, G])
            ci = q[13][:, :].unsqueeze(1).to_broadcast([P, 9, G])
            link(v.tensor_tensor(MT[:, :, :], EI[:, :, :], ci, ALU.mult))
            link(v.tensor_tensor(EI[:, :, :], EI[:, :, :], cr, ALU.mult))
            X9 = TC[:, :, :].rearrange("p a b -> p (a b)")[:, 0:9 * G].rearrange("p (a b) -> p a b", a=9)
            link(v.tensor_tensor(X9, ER[:, :, :], ci, ALU.mult))
            link(v.tensor_tensor(ER[:, :, :], ER[:, :, :], cr, ALU.mult))
            link(v.tensor_tensor(ER[:, :, :], ER[:, :, :], MT[:, :, :], ALU.subtract))
            link(v.tensor_tensor(EI[:, :, :], EI[:, :, :], X9, ALU.add))
            link(v.tensor_scalar(EI[:, :, :], EI[:, :, :], nsgn[:, :], None, ALU.mult))

            def y_lo(hf, b):
                g8 = slice(hf * GH + 8 * b, hf * GH + 8 * b + 8)
                dve.wait_ge(sem("ysh_ready"), 4 * hf + b + 1)
                v.tensor_tensor(YS[1][:, g8, :], ps[:, 4 + b % 2, 0:8 * UC].rearrange("p (g n) -> p g n", g=8),
                                YS[0][:, g8, :].bitcast(F32), ALU.subtract).then_inc(sem("y_split"), 1)

            for hf in range(2):
                gs = slice(hf * GH, hf * GH + GH)
                link(v.tensor_tensor(TA[:, :, :], q[7][:, gs].unsqueeze(2).to_broadcast([P, GH, NB]),
                                     jramp[:, :].unsqueeze(1).to_broadcast([P, GH, NB]), ALU.mult))
                reduce_phase(TA[:, :, :], TB[:, :, :], sem("phase_ready"))
                dve.wait_ge(sem("b_loaded"), 32 * (hf + 1))
                if hf:
                    dve.wait_ge(sem("toep_made"), 8)
                for s in range(L):
                    if hf and s in (2, 4, 7):
                        y_lo(0, (2, 4, 7).index(s))
                    er = ER[:, 8 - s, gs].unsqueeze(2).to_broadcast([P, GH, H])
                    ei = EI[:, 8 - s, gs].unsqueeze(2).to_broadcast([P, GH, H])
                    out = AM[:, :, s * H:(s + 1) * H]
                    v.tensor_tensor(out, BQ[:, :, :], er, ALU.mult).then_inc(sem("dve_step"), 1)
                    steps[0] += 1
                    link(v.tensor_tensor(PT[:, :, :], BX[:, :, :], ei, ALU.mult))
                    ins = v.tensor_tensor(out, out, PT[:, :, :], ALU.add)
                    if s < L - 1:
                        link(ins)
                    else:
                        ins.then_inc(sem("a_built"), 1)
                if hf:
                    y_lo(0, 3)
                if hf == 0:
                    dve.wait_ge(sem("h0_loaded"), 32)
                    wide = lambda x: x.unsqueeze(2).to_broadcast([P, G, TS])
                    link(v.tensor_tensor(H0Q[:, :, :], H0Q[:, :, :], wide(q[0][:, :]), ALU.mult))
                    link(v.tensor_tensor(H0X[:, :, :], H0X[:, :, :], wide(q[1][:, :]), ALU.mult))
                    link(v.tensor_tensor(H0Q[:, :, :], H0Q[:, :, :], H0X[:, :, :], ALU.add))
                link(v.tensor_copy(R8[:, :, :], q[4][:, gs].unsqueeze(2).to_broadcast([P, GH, NB])))
                link(v.memset(R8[:, :, 0:1], 0.0))
                link(v.memset(WV[:, 0:1], 0.0))
                dve.wait_ge(sem("turn_ready"), 3 * hf + 3)
                wv = WV[:, 1:].rearrange("p (g j) -> p g j", g=GH)

                def turn_back(b):
                    dve.wait_ge(sem("v_swapped"), 4 * hf + b + 1)
                    bk = 6 if b % 2 == 0 else 0
                    g8 = slice(8 * b, 8 * b + 8)
                    V = VB[:, b % 2, :].rearrange("p (g n) -> p g n", g=8)
                    VX = ps[:, bk + 1, 0:8 * UC].rearrange("p (g n) -> p g n", g=8)
                    v.tensor_tensor(TB[:, g8, :], V[:, :, 0:NB], COS[:, g8, :], ALU.mult).then_inc(sem("dve_step"), 1)
                    v.tensor_copy(VS[:, g8, :], V[:, :, NB:UC]).then_inc(sem("dve_step"), 1)
                    steps[0] += 2
                    v.tensor_tensor(TC[:, g8, :], VX[:, :, 0:NB], SS[:, g8, :], ALU.mult).then_inc(sem("v_turned"), 1)
                    dve.wait_ge(sem("dve_step"), steps[0])
                    dve.wait_ge(sem("v_turned"), 4 * hf + b + 1)
                    link(v.tensor_tensor(wv[:, g8, :], TB[:, g8, :], TC[:, g8, :], ALU.add))

                for b in range(8):
                    dve.wait_ge(sem("toep_made"), 8 * hf + b + 1)
                    v.tensor_tensor(TM[:, 4 * b:4 * b + 4, :], ps[:, 2 + b % 2, :].rearrange("p (g n) -> p g n", g=4),
                                    tmask[:, :].unsqueeze(1).to_broadcast([P, 4, P]), ALU.mult)\
                        .then_inc(sem("toep_ready"), 1)
                    if b % 2 and b > 1:
                        turn_back(b // 2 - 1)
                turn_back(3)
                sv = SV[:, :, :].rearrange("p g j -> p (g j)")
                v.tensor_tensor_scan(sv, WV[:, 0:GH * NB], R8[:, :, :].rearrange("p g j -> p (g j)"), 0.0,
                                     ALU.add, ALU.mult).then_inc(sem("scanned"), 1)
                dve.wait_ge(sem("scanned"), hf + 1)
                v.tensor_tensor(GL[:, :], SV[:, :, NB - 1], wv[:, :, NB - 1], ALU.add).then_inc(sem("last_ready"), 1)
                link(v.tensor_tensor(TB[:, :, :], SV[:, :, :], COS[:, :, :], ALU.mult))
                for i in range(2):
                    dve.wait_ge(sem("swapped"), 3 * hf + i + 1)
                    g16 = slice(16 * i, 16 * i + 16)
                    link(v.tensor_tensor(TC[:, g16, :], ps[:, 2 + i, :].rearrange("p (g j) -> p g j", g=16),
                                         SS[:, g16, :], ALU.mult))
                if hf:
                    dve.wait_ge(sem("y_made"), 4)
                link(v.tensor_tensor(HM[:, :, 0:NB], TB[:, :, :], TC[:, :, :], ALU.subtract))
                v.tensor_copy(HM[:, :, NB:UC], H0Q[:, gs, :]).then_inc(sem("h_ready"), 1)
                c31, s31 = COS[:, :, NB - 1], SS[:, :, NB - 1]
                link(v.tensor_scalar(q[8][:, 0:GH], s31, sgn[:, :], None, ALU.mult))
                link(v.tensor_tensor(q[9][:, 0:GH], q[2][:, gs], c31, ALU.mult))
                link(v.tensor_tensor(q[10][:, 0:GH], q[3][:, gs], q[8][:, 0:GH], ALU.mult))
                link(v.tensor_tensor(q[9][:, 0:GH], q[9][:, 0:GH], q[10][:, 0:GH], ALU.subtract))
                link(v.tensor_tensor(q[8][:, 0:GH], q[8][:, 0:GH], q[2][:, gs], ALU.mult))
                link(v.tensor_tensor(q[10][:, 0:GH], q[3][:, gs], c31, ALU.mult))
                link(v.tensor_tensor(q[8][:, 0:GH], q[8][:, 0:GH], q[10][:, 0:GH], ALU.add))
                link(v.tensor_scalar(q[8][:, 0:GH], q[8][:, 0:GH], nsgn[:, :], None, ALU.mult))
                link(v.tensor_tensor(q[9][:, 0:GH], q[9][:, 0:GH], GL[:, :], ALU.mult))
                dve.wait_ge(sem("swapped"), 3 * hf + 3)
                link(v.tensor_tensor(q[8][:, 0:GH], ps[:, 7, 0:GH], q[8][:, 0:GH], ALU.mult))
                link(v.tensor_tensor(HP[:, gs], q[9][:, 0:GH], q[8][:, 0:GH], ALU.add))
                v.tensor_tensor(HS[:, gs, :], H0Q[:, gs, :], VS[:, :, :], ALU.add).then_inc(sem("states_done"), 1)
            for c in range(KC):
                v.tensor_scalar(TMP[:, c, :], XN[:, c, :], vec[:, SSM_D, c:c + 1], None, ALU.mult)\
                    .then_inc(sem("du_ready"), 1)
            for b in range(4):
                y_lo(1, b)
            dve.wait_ge(sem("du_ready"), 8)
            for s in range(L):
                dve.wait_ge(sem("y_moved"), s + 1)
                y_t = TMP[:, :, s:TP:L]
                wide_cols = UC if s == SMID else NB
                src = ps[:, s % 2, 0:KC * wide_cols].rearrange("p (c n) -> p c n", c=KC)
                if s == SMID:
                    link(v.tensor_tensor(TMP[:, :, TP:NT], src[:, :, NB:UC], TMP[:, :, TP:NT], ALU.add))
                v.tensor_tensor(y_t, src[:, :, 0:NB], y_t, ALU.add).then_inc(sem("y_mixed"), 1)

            dve.wait_ge(sem("y_mixed"), 8)
            v.memset(relx[NBUCK:NBUCK + 1, :], NEG).then_inc(sem("outside_ready"), 1)

            def lo(tile):
                hi_ = WH[tile[2] % SPLIT][:, :].bitcast(F32)
                dve.wait_ge(sem("hi_made"), at(dve, tile, 1))
                v.tensor_tensor(WL[tile[2] % SPLIT][:, :], raw[tile[2] % RING][:, :], hi_, ALU.subtract)\
                    .then_inc(split, 1)

            for k in range(4):
                xn_lo(k + 1, k, XNL, XN, XNH)
            for n in range(SPLIT):
                lo(dense(n))
            for n in range(GU0):
                dve.wait_ge(sem("gated"), n + 1)
                link(v.tensor_tensor(SG[:, n % 2, :], ps[:, 2 * (n % 2), 0:NT], SG[:, n % 2, :], ALU.mult))
                v.tensor_tensor(X[:, n, :], X[:, n, :], SG[:, n % 2, :], ALU.add).then_inc(sem("pair_done"), 1)
                if n < GU0 - 1:
                    lo(dense(n + SPLIT))
            norm(1, G_FFN0, sem("xn_ready"), (4, XNL, XNH))
            lo(dense(GU0 - 1 + SPLIT))

            def gate_up(tile):
                b = tile[2] % 2
                r, stride, c = tile
                out = c - GU0 if r is None else bass.ds(r * stride + (c - GU0), 1)
                fah, fal = (f[:, out, :] if r is None else f[:, out, :].rearrange("p a n -> p (a n)")
                            for f in (FAH, FAL))
                dve.wait_ge(sem("gated"), at(dve, tile, 1))
                v.tensor_tensor(SG[:, b, :], ps[:, 2 * b + 1, 0:NT], SG[:, b, :], ALU.mult).then_inc(sem("fa_made"), 1)
                dve.wait_ge(sem("fa_made"), at(dve, tile, 1 - GU0))
                v.tensor_copy(fah, SG[:, b, :]).then_inc(sem("fah_made"), 1)
                dve.wait_ge(sem("fah_made"), at(dve, tile, 1 - GU0))
                v.tensor_tensor(fal, SG[:, b, :], fah.bitcast(F32), ALU.subtract).then_inc(sem("pair_done"), 1)
                lo(after(tile, SPLIT))

            with dve.Fori(0, TURNS) as r:
                for i in range(PAIRS):
                    gate_up((r, PAIRS, GU0 + i))
            for n in range(GU0 + TURNS * PAIRS, DN0):
                gate_up(dense(n))
            for n in range(DN0, KV0 - 1):
                lo(dense(n + SPLIT))
            dve.wait_ge(used, KV0)
            for c in range(KC):
                v.tensor_tensor(X[:, c, :], ps[:, c, 0:NT], X[:, c, :], ALU.add).then_inc(sem("resid_ffn"), 1)
            norm(2, G_KV, sem("xn_ready"), (8, XNL, XNH))
            lo(dense(KV0 - 1 + SPLIT))
            scale_and_split(XQ, G_MIX1, sem("xq_ready"), 12, XQL, XQH)
            for n in range(KV0, O0):
                lo(dense(n + SPLIT))
            dve.wait_ge(sem("sink_loaded"), 16 * (TS + 1))
            dve.wait_ge(sem("bias_loaded"), 16 * (NH + TS))

            def scores(h):
                b = h % 3
                bank = S_BANK[b]
                dve.wait_ge(sem("s_made"), h + 1)
                if h >= 3:
                    dve.wait_ge(sem("p_turned"), h - 2)
                if h < NH:
                    v.scalar_tensor_tensor(out=SC[:, b, 0:W], in0=ps[:, bank, 0:W], scalar=SCALE,
                                           in1=BIAS[:, HEADS[h], W:2 * W], op0=ALU.mult, op1=ALU.add)\
                        .then_inc(sem("dve_step"), 1)
                    v.scalar_tensor_tensor(out=SC[:, b, W:3 * W], in0=ps[:, bank, W:3 * W], scalar=SCALE,
                                           in1=BIAS[:, HEADS[h], :], op0=ALU.mult, op1=ALU.add).then_inc(sem("s_read"), 1)
                    steps[0] += 1
                    dve.wait_ge(sem("dve_step"), steps[0])
                    link(v.reduce_max(mx[:, b, 0:1], SC[:, b, 0:W], AX_X))
                    dve.wait_ge(sem("s_read"), h + 1)
                    link(v.reduce_max(mx[:, b, 1:2], SC[:, b, W:3 * W], AX_X))
                    v.tensor_scalar(nm[:, b, :], mx[:, b, :], SINK[:, HEADS[h]:HEADS[h] + 1], -1.0, ALU.max, ALU.mult)\
                        .then_inc(sem("shift_ready"), 1)
                else:
                    v.scalar_tensor_tensor(out=SC[:, b, 0:W], in0=ps[:, bank, 0:W], scalar=SCALE,
                                           in1=BSM[:, :], op0=ALU.mult, op1=ALU.add).then_inc(sem("s_read"), 1)
                    dve.wait_ge(sem("s_read"), h + 1)
                    link(v.reduce_max(mx[:, b, 0:1], SC[:, b, 0:W], AX_X))
                    v.tensor_scalar(nm[:, b, 0:1], mx[:, b, 0:1], SINKC[:, :], -1.0, ALU.max, ALU.mult)\
                        .then_inc(sem("shift_ready"), 1)

            def probs(h):
                b = h % 3
                k = 2 if h < NH else 1
                dve.wait_ge(sem("exp_ready"), 3 * h + 3 if h < NH else 3 * NH + 2)
                link(v.tensor_tensor(rd[:, b, 0:k], sm[:, b, 0:k], es[:, b, 0:k], ALU.add))
                v.reciprocal(rd[:, b, 0:k], rd[:, b, 0:k]).then_inc(sem("rd_ready"), 1)
                dve.wait_ge(sem("rd_ready"), h + 1)
                v.tensor_scalar(SC[:, b, 0:W], SC[:, b, 0:W], rd[:, b, 0:1], None, ALU.mult)\
                    .then_inc(sem("p_ready"), 1)

            def heads_out(h):
                c = h // 2
                dve.wait_ge(sem("pv_made"), h + 1)
                link(v.tensor_copy(OTH[:, c, 0:TP], ps[:, 4 + c % 2, 0:TP]))
                v.tensor_tensor(OTL[:, c, 0:TP], ps[:, 4 + c % 2, 0:TP], OTH[:, c, 0:TP].bitcast(F32), ALU.subtract)\
                    .then_inc(sem("o_ready"), 1)

            for h in range(NH):
                scores(h)
                if h:
                    probs(h - 1)
                if h >= 5 and h % 2:
                    heads_out(h - 4)
            dve.wait_ge(sem("st_made"), NH)
            for i in range(2):
                v.tensor_copy(STS[:, :].rearrange("p (x g r) -> p x g r", g=2, r=R)[:, :, i],
                              ps[:, 7, 64 * i:64 * i + 64].rearrange("p (x r) -> p x r", r=R))\
                    .then_inc(sem("st_ready"), 1)
            probs(NH - 1)
            heads_out(NH - 3)
            scores(NH)
            heads_out(NH - 1)
            probs(NH)
            dve.wait_ge(sem("os_made"), 1)
            o_new = ps[:, 6, 0:KC * TS].rearrange("p (c b) -> p c b", c=KC)
            link(v.tensor_copy(OTH[:, :, TP:NT], o_new))
            v.tensor_tensor(OTL[:, :, TP:NT], o_new, OTH[:, :, TP:NT].bitcast(F32), ALU.subtract)\
                .then_inc(sem("o_ready"), 1)
            for n in range(O0, NDENSE):
                dve.wait_ge(used, n + 1)
                for i in range(2):
                    c = 2 * (n - O0) + i
                    v.tensor_tensor(X[:, c, :], ps[:, 2 * (n % 2) + i, 0:NT], X[:, c, :], ALU.add)\
                        .then_inc(sem("resid_o"), 1)
                if n < NDENSE - 1:
                    lo(dense(n + SPLIT))
            norm(3, G_FFN1, sem("xn_ready"))
            lo(dense(NDENSE - 1 + SPLIT))

            dve.wait_ge(sem("kv_stored"), 64)
            dve.wait_ge(sem("logits_made"), 1)
            dve.wait_ge(sem("route_consts"), 5)
            link(v.tensor_copy(LG[:, 0:2, :], ps[:, 3, 0:2 * E].rearrange("p (t e) -> p t e", t=2)))
            link(v.tensor_copy(LG[0:TS, 2, :], ps[0:TS, 3, 2 * E:3 * E]))
            for t in range(3):
                link(v.max(top[:, t, :], LG[:, t, :]))
            first = top[:, :, 0:1].to_broadcast([P, 3, E])
            second = top[:, :, 1:2].to_broadcast([P, 3, E])
            link(v.tensor_tensor(r1[:, :, :], LG[:, :, :], second, ALU.is_gt))
            link(v.tensor_tensor(r2[:, :, :], LG[:, :, :], second, ALU.is_equal))
            flat = lambda x: x[:, :, :].rearrange("p t e -> p (t e)")
            link(v.tensor_tensor_scan(flat(r3), flat(dz), flat(r2), 0.0, ALU.mult, ALU.add))
            link(v.tensor_reduce(v1[:, :], r1[:, :, :], AX_X, ALU.add))
            link(v.tensor_tensor(r3[:, :, :], r3[:, :, :], v1[:, :].unsqueeze(2).to_broadcast([P, 3, E]), ALU.add))
            link(v.tensor_scalar(r3[:, :, :], r3[:, :, :], 2.0, None, ALU.is_le))
            link(v.tensor_tensor(r2[:, :, :], r2[:, :, :], r3[:, :, :], ALU.mult))
            v.tensor_tensor(SELM[:, :, :], r1[:, :, :], r2[:, :, :], ALU.add).then_inc(sem("sel_ready"), 1)
            dve.wait_ge(sem("sel_ready"), 1)
            v.tensor_tensor(r3[:, :, :], LG[:, :, :], first, ALU.subtract).then_inc(sem("gap_ready"), 1)
            dve.wait_ge(sem("gexp_ready"), 1)
            link(v.tensor_tensor(GATE[:, :, :], r4[:, :, :], SELM[:, :, :], ALU.mult))
            link(v.tensor_reduce(v1[:, :], GATE[:, :, :], AX_X, ALU.add))
            link(v.reciprocal(v1[:, :], v1[:, :]))
            link(v.tensor_tensor(GATE[:, :, :], GATE[:, :, :], v1[:, :].unsqueeze(2).to_broadcast([P, 3, E]), ALU.mult))
            dve.wait_ge(sem("pos_made"), 1)
            link(v.memset(POS[:, :, :], 0.0))
            link(v.tensor_copy(POS[:, 0:2, :], ps[:, 4, 0:2 * E].rearrange("p (t e) -> p t e", t=2)))
            link(v.tensor_copy(POS[0:TS, 2, :], ps[0:TS, 4, 2 * E:3 * E]))
            link(v.scalar_tensor_tensor(out=POS[:, :, :], in0=POS[:, :, :], scalar=1.0, in1=SELM[:, :, :],
                                        op0=ALU.add, op1=ALU.mult))
            link(v.tensor_scalar(POS[:, :, :], POS[:, :, :], -1.0, None, ALU.add))
            need = cnt[:, :].rearrange("p (e k) -> p e k", k=2)
            total = ps[0:1, 4, 3 * E:4 * E]
            link(v.tensor_scalar(need[:, :, 0], total, float(P) + 0.5, None, ALU.is_gt))
            link(v.tensor_scalar(need[:, :, 1], total, 2.0 * P + 0.5, None, ALU.is_gt))

            def dispatch(e, k):
                for t in range(3):
                    rows = tokens(t)
                    pos, gate_ = POS[0:rows, t, bass.ds(e, 1)], GATE[0:rows, t, bass.ds(e, 1)]
                    v.tensor_scalar(DSP[0:rows, t, :], slot[0:rows, k, :], pos, None, ALU.is_equal)\
                        .then_inc(sem("dispatched"), 1)
                    v.tensor_scalar(DG[0:rows, t, :], slot[0:rows, k, :], pos, gate_, ALU.is_equal, ALU.mult)\
                        .then_inc(sem("gate_spread"), 1)

            def expert_gate_up(r, j, prev=None):
                for kq in range(4):
                    m = 4 * j + kq
                    if kq == 1 and j:
                        hidden_lo(r, j - 1)
                    if kq == 3:
                        dve.wait_ge(sem("silu_ready"), dve.snap(JE * r + (j + 1)))
                        if j >= 2:
                            dve.wait_ge(sem("act_turned"), dve.snap(JE * r + (j - 1)))
                        v.tensor_tensor(AC[:, j % 2, :], ps[:, 2 * (j % 2) + 1, :], SIL[:, j % 2, :], ALU.mult)\
                            .then_inc(sem("act_ready"), 1)
                    lo(expert_tile(r, m + SPLIT))
                    if prev is not None and kq % 2:
                        add(prev, kq // 2)

            def hidden_lo(r, j):
                dve.wait_ge(sem("afh_ready"), dve.snap(JE * r + (j + 1)))
                v.tensor_tensor(AFL[:, 4 * j:4 * j + 4, :], ps[:, 6 + j % 2, :].rearrange("p (c n) -> p c n", c=4),
                                AFH[:, 4 * j:4 * j + 4, :].bitcast(F32), ALU.subtract).then_inc(sem("af_split"), 1)

            def tokens_lo(n, bank=GATHER[1]):
                dve.wait_ge(sem("gathered"), n)
                v.tensor_copy(XEL[:, :, :].rearrange("p c n -> p (c n)"), ps[:, bank:bank + 2, :].rearrange("p b n -> p (b n)"))\
                    .then_inc(sem("xel_ready"), 1)

            def add(r, i):
                dve.wait_ge(sem("scattered"), dve.snap(2 * r + (i + 1)))
                c4 = slice(4 * i, 4 * i + 4)
                v.tensor_tensor(X[:, c4, :], ps[:, 4:8, 0:NT], X[:, c4, :], ALU.add).then_inc(sem("x_added"), 1)

            def expert_rest(r, more):
                for j in range(1, JE):
                    expert_gate_up(r, j)
                for d in range(NDE):
                    if d == 1:
                        hidden_lo(r, JE - 1)
                    if d == 3:
                        dve.wait_ge(sem("gsh_ready"), dve.snap(r + 1))
                        v.tensor_tensor(GSL[:, :], ps[:, 7, 0:NT], GSH[:, :].bitcast(F32), ALU.subtract)\
                            .then_inc(sem("gs_split"), 1)
                        if more:
                            dispatch(dve.snap(r + 1), 0)
                    if d == 6 and more:
                        tokens_lo(dve.snap(r + 2))
                    if d == NDE - 1:
                        dve.wait_ge(sem("yeh_ready"), dve.snap(r + 1))
                        v.tensor_tensor(YEL[:, :], ps[:, 4:6, :].rearrange("p b n -> p (b n)"),
                                        YEH[:, :].bitcast(F32), ALU.subtract).then_inc(sem("ye_split"), 1)
                    if more or NGU + d + SPLIT < NE:
                        lo(expert_tile(r, NGU + d + SPLIT))
                if more:
                    expert_gate_up(dve.snap(r + 1), 0, r)
                else:
                    add(r, 0)
                    add(r, 1)

            zero = dve.snap(0)
            dispatch(zero, 0)
            for t in range(3):
                rows = tokens(t)
                for hf in range(2):
                    half_ = slice(hf * 512, hf * 512 + 512)
                    dve.wait_ge(sem("hth_ready"), 2 * t + hf + 1)
                    v.tensor_tensor(HTL[0:rows, t, half_], ps[0:rows, HT_BANK[2 * t + hf], :], HTH[0:rows, t, half_].bitcast(F32),
                                    ALU.subtract).then_inc(sem("ht_ready"), 1)
            link(v.memset(run[:, :], 1.0))
            link(v.memset(run[:, 0:1], float(E)))
            link(v.tensor_tensor_scan(run[:, 1:2 * E + 1], run[:, 1:2 * E + 1], cnt[:, :], float(E), ALU.mult, ALU.add))
            link(v.tensor_copy(plan[:, 0:2 * E], cnt[:, :]))
            v.tensor_copy(plan[:, 2 * E:4 * E + 1], run[:, :]).then_inc(sem("plan_ready"), 1)
            dve.wait_ge(sem("plan_ready"), 1)
            dve.sem_inc(sem("x_added"), 1)
            tokens_lo(1, GATHER0[1])
            expert_gate_up(zero, 0)
            with dve.Fori(0, E - 1) as e:
                expert_rest(e, True)
            expert_rest(dve.snap(zero + (E - 1)), False)
            any_more = dve.value_load(plan[0:1, 4 * E:4 * E + 1], min_val=E, max_val=E + 4)
            with dve.If(any_more > E):
                with dve.Fori(0, E) as e:
                    for k in range(2):
                        i = dve.snap(e * 2 + k)
                        more = dve.value_load(plan[0:1, bass.ds(i, 1)], min_val=0, max_val=1)
                        with dve.If(more > 0):
                            r = dve.value_load(plan[0:1, bass.ds(i + 2 * E, 1)], min_val=E, max_val=E + 4)
                            for m in range(SPLIT):
                                lo(expert_tile(r, m))
                            dispatch(e, k + 1)
                            tokens_lo(dve.snap(r + 1))
                            expert_gate_up(r, 0)
                            expert_rest(r, False)
            dve.drain()
            v.memset(cnt[:, 0:1], 0.0).then_inc(sem("moe_done"), 1)
            norm(4, G_FIN, sem("xn_ready"))

        @block.tensor
        def _(pe):
            t_ = nc.tensor

            def norm_part(i, c):
                pe.wait_ge(sem("squared"), KC * i + c + 1)
                t_.matmul(ps[:, NORM_BANK[i], 0:NT], ones[:, :], SQ[:, c % 2, :], start=(c == 0), stop=(c == KC - 1))\
                    .then_inc(sem("sq_summed"), 1)

            def norm(i):
                for c in range(KC):
                    norm_part(i, c)

            pe.wait_ge(sem("consts"), 5)
            norm(0)
            pe.wait_ge(sem("xn_ready"), 8)
            pe.wait_ge(sem("root_ready"), 1)
            for k in range(G8):
                if k >= 2:
                    pe.wait_ge(sem("u_ready"), k - 1)
                out = ps[:, k % 2, 0:KC * UC].rearrange("p (c n) -> p c n", c=KC)
                for s in range(L):
                    w0 = 112 - 16 * s
                    mm = t_.matmul(out[:, :, 0:NB], sel[:, k, w0:w0 + P], XN[:, :, s:TP:L],
                                   start=(s == 0), stop=(s == L - 1), skip_group_check=True)
                    if s == SMID:
                        mm = t_.matmul(out[:, :, NB:UC], sel[:, k, w0:w0 + P], XN[:, :, TP:NT],
                                       start=False, stop=True, skip_group_check=True)
                mm.then_inc(sem("u_moved"), 1)
            for hf in range(2):
                g0 = hf * GH
                pe.wait_ge(sem("a_built"), hf + 1)

                def project(b):
                    bk = 6 if b % 2 == 0 else 0
                    if b == 0:
                        pe.wait_ge(sem("u_ready"), 8)
                        if hf:
                            pe.wait_ge(sem("states_done"), 1)
                    elif b >= 2:
                        pe.wait_ge(sem("v_turned"), 4 * hf + b - 1)
                    pe.wait_ge(sem("at_ready"), 8 * hf + 2 * b + 2)
                    for g in range(8):
                        mm = t_.matmul(ps[:, bk, g * UC:(g + 1) * UC], AT[:, g, :], U[:, g0 + 8 * b + g, :],
                                       start=True, stop=True)
                    mm.then_inc(sem("v_made"), 1)

                def swap(b):
                    pe.wait_ge(sem("v_in_sbuf"), 4 * hf + b + 1)
                    t_.matmul(ps[:, 7 if b % 2 == 0 else 1, 0:8 * UC], swp[:, :], VB[:, b % 2, :],
                              start=True, stop=True).then_inc(sem("v_swapped"), 1)

                for b in range(8):
                    if b >= 2:
                        pe.wait_ge(sem("at_ready"), 8 * hf + b - 1)
                    elif hf:
                        pe.wait_ge(sem("y_split"), 4)
                    for g in range(4):
                        mm = t_.transpose(ps[:, 4 + b % 2, g * P:(g + 1) * P], AM[:, 4 * b + g, :], ident[:, :])
                    mm.then_inc(sem("a_turned"), 1)
                    if b == 0:
                        pe.wait_ge(sem("c_built"), hf + 1)
                    if b >= 2:
                        pe.wait_ge(sem("toep_ready"), 8 * hf + b - 1)
                    elif hf:
                        pe.wait_ge(sem("h_ready"), 1)
                    for g in range(4):
                        mm = t_.matmul(ps[:, 2 + b % 2, g * P:(g + 1) * P], AM[:, 4 * b + g, :], CM[hf][:, 4 * b + g, :],
                                       start=True, stop=True)
                    mm.then_inc(sem("toep_made"), 1)
                    if b % 2:
                        project(b // 2)
                    elif b:
                        swap(b // 2 - 1)
                swap(3)
                pe.wait_ge(sem("scanned"), hf + 1)
                pe.wait_ge(sem("toep_ready"), 8 * hf + 8)
                for i in range(2):
                    t_.matmul(ps[:, 2 + i, :], swp[:, :], SV[:, 16 * i:16 * i + 16, :].rearrange("p g j -> p (g j)"),
                              start=True, stop=True).then_inc(sem("swapped"), 1)
                pe.wait_ge(sem("last_ready"), hf + 1)
                pe.wait_ge(sem("v_turned"), 4 * hf + 4)
                t_.matmul(ps[:, 7, 0:GH], swp[:, :], GL[:, :], start=True, stop=True).then_inc(sem("swapped"), 1)
                pe.wait_ge(sem("h_ready"), hf + 1)
                pe.wait_ge(sem("at_ready"), 8 * hf + 8)
                for b in range(4):
                    if b >= 2:
                        pe.wait_ge(sem("y_split"), 4 * hf + b - 1)
                    for g in range(8):
                        out = ps[:, 4 + b % 2, g * UC:(g + 1) * UC]
                        t_.matmul(out, TM[:, 8 * b + g, :], U[:, g0 + 8 * b + g, :], start=True, stop=False)
                        mm = t_.matmul(out, CM[hf][:, 8 * b + g, :], HM[:, 8 * b + g, :], start=False, stop=True)
                    mm.then_inc(sem("y_made"), 1)
            pe.wait_ge(sem("y_split"), 8)
            pe.wait_ge(sem("sel_r_ready"), 1)
            for s in range(L):
                if s >= 2:
                    pe.wait_ge(sem("y_mixed"), s - 1)
                cols = UC if s == SMID else NB
                out = ps[:, s % 2, 0:KC * cols].rearrange("p (c n) -> p c n", c=KC)
                for k in range(G8):
                    w0 = 112 - 16 * k
                    for i, part in enumerate(YS):
                        mm = t_.matmul(out, sel_r[:, s, w0:w0 + P],
                                       part[:, :, :].rearrange("p (c k) n -> p k c n", k=G8)[:, k, :, 0:cols],
                                       start=(k == 0 and i == 0), stop=(k == G8 - 1 and i == 1))
                mm.then_inc(sem("y_moved"), 1)

            def passes(out, stat, mov, first, last):
                (sh, sl), (mh, ml) = stat, mov
                t_.matmul(out, sh, mh, start=first, stop=False)
                t_.matmul(out, sh, ml, start=False, stop=False)
                return t_.matmul(out, sl, mh, start=False, stop=last)

            def arrived(tile):
                pe.wait_ge(split, at(pe, tile, 1))
                return WH[tile[2] % SPLIT], WL[tile[2] % SPLIT]

            def pair(tile, rhs, wait=None, n_split=None):
                w = arrived(tile)
                if wait:
                    pe.wait_ge(*wait)
                for i in range(2):
                    for k in range(KC):
                        if n_split is not None and i == 0 and k % 2 == 0:
                            pe.wait_ge(sem("xn_split"), n_split + k // 2 + 1)
                        cols = slice((2 * k + i) * P, (2 * k + i + 1) * P)
                        mm = passes(ps[:, 2 * (tile[2] % 2) + i, 0:NT], [x[:, cols] for x in w],
                                    [x[:, k, :] for x in rhs], k == 0, k == KC - 1)
                mm.then_inc(used, 1)

            XNS = (XNH, XNL)
            for n in range(GU0):
                pair(dense(n), XNS, (sem("pair_done"), n - 1) if n >= 2 else None, n_split=0 if n == 0 else None)
                if n >= 2:
                    norm_part(1, n - 2)
            pe.wait_ge(sem("rel_loaded"), 32)
            pe.wait_ge(sem("outside_ready"), 1)
            t_.matmul(ps[0:NH, 7, 0:384], relx[:, :], oneh[:, :], start=True, stop=True).then_inc(sem("bias_made"), 1)
            for c in range(KC - 2, KC):
                norm_part(1, c)
            pe.wait_ge(sem("root_ready"), 2)
            with pe.Fori(0, TURNS) as r:
                for i in range(PAIRS):
                    tile = (r, PAIRS, GU0 + i)
                    pair(tile, XNS, (sem("pair_done"), at(pe, tile, -1)), n_split=4 if i == 0 else None)
            for n in range(GU0 + TURNS * PAIRS, DN0):
                pair(dense(n), XNS, (sem("pair_done"), n - 1))
            pe.wait_ge(sem("pair_done"), DN0)
            for j in range(NF // 2):
                w = arrived(dense(DN0 + j))
                for k in range(2):
                    for c in range(KC):
                        cols = slice((k * KC + c) * P, (k * KC + c + 1) * P)
                        mm = passes(ps[:, c, 0:NT], [x[:, cols] for x in w], [f[:, 2 * j + k, :] for f in (FAH, FAL)],
                                    j == 0 and k == 0, j == NF // 2 - 1 and k == 1)
                mm.then_inc(used, 1)
            pe.wait_ge(sem("resid_ffn"), 8)
            norm(2)
            pe.wait_ge(sem("root_ready"), 3)
            pair(dense(KV0), XNS, n_split=8)
            w = arrived(dense(KV0 + 1))
            for t in range(3):
                tok = slice(t * P, (t + 1) * P) if t < 2 else slice(NT - P, NT)
                for k in range(KC):
                    mm = passes(ps[:, 4 + t, 0:256], [x[:, k, tok] for x in XNS],
                                [x[:, k * 256:(k + 1) * 256] for x in w], k == 0, k == KC - 1)
            mm.then_inc(used, 1)
            for n in range(Q0, O0):
                pair(dense(n), (XQH, XQL), (sem("k_ready"), 2) if n < Q0 + 2 else (sem("q_ready"), 2 * (n - Q0 - 1)),
                     n_split=12 if n == Q0 else None)
            pe.wait_ge(sem("q_ready"), 8)
            pe.wait_ge(sem("v_ready"), 3)

            def score(h):
                c, b, bank = h // 2, h % 2, S_BANK[h % 3]
                rows = slice(64 * b, 64 * b + 64)
                if h >= 3:
                    pe.wait_ge(sem("s_read"), h - 2)
                kv = KT[rows, c // 4, :]
                t_.matmul(ps[:, bank, 0:W], QT[rows, c, 0:W], kv[:, 0:W], start=True, stop=True)
                t_.matmul(ps[:, bank, W:3 * W], QT[rows, c, W:TP], kv[:, 0:2 * W], start=True, stop=True)\
                    .then_inc(sem("s_made"), 1)

            def turn(h):
                b = h % 2
                pe.wait_ge(sem("p_ready"), h + 1)
                if h < NH:
                    pe.wait_ge(sem("p2_ready"), h + 1)
                if h >= 2:
                    pe.wait_ge(sem("pt_ready"), h - 1)
                for i in range(3 if h < NH else 1):
                    mm = t_.transpose(ps[:, 2 + b, i * P:(i + 1) * P], SC[:, h % 3, i * P:(i + 1) * P], ident[:, :])
                mm.then_inc(sem("p_turned"), 1)

            def mix(h):
                c, b = h // 2, h % 2
                rows = slice(64 * b, 64 * b + 64)
                g = 2 * (c // 4) + b
                pe.wait_ge(sem("pt_ready"), h + 1)
                if c >= 2 and b == 0:
                    pe.wait_ge(sem("o_ready"), c - 1)
                out = ps[rows, 4 + c % 2, :]
                vg = lambda t: VT[:, t, g * HD:(g + 1) * HD]
                t_.matmul(out[:, 0:W], vg(0), PTT[:, b, 0:W], start=True, stop=True)
                t_.matmul(out[:, W:TP], vg(0), PTT[:, b, W:2 * W], start=True, stop=False)
                t_.matmul(out[:, W:TP], vg(1), PTT[:, b, 2 * W:3 * W], start=False, stop=True)\
                    .then_inc(sem("pv_made"), 1)

            def score_decoded(n):
                b, half_ = n // 2, n % 2
                rows = slice(64 * half_, 64 * half_ + 64)
                if n:
                    pe.wait_ge(sem("st_made"), n)
                for g2 in range(2):
                    c0 = 64 * half_ + (2 * b + g2) * R
                    mm = t_.matmul(ps[:, 7, c0:c0 + R], KCT[rows, b, g2, :],
                                   QT[rows, 4 * g2:4 * g2 + 4, TP + b], start=True, stop=True)
                mm.then_inc(sem("st_made"), 1)

            pe.wait_ge(sem("kc_ready"), 1)
            for h in range(NH):
                score(h)
                if h >= 3:
                    mix(h - 3)
                if h:
                    score_decoded(h - 1)
                if h >= 2:
                    turn(h - 2)
            mix(NH - 3)
            turn(NH - 2)
            score_decoded(NH - 1)
            turn(NH - 1)
            mix(NH - 2)
            pe.wait_ge(sem("st_ready"), 2)
            t_.transpose(ps[:, S_BANK[NH % 3], 0:P], STS[:, :], ident[:, :]).then_inc(sem("s_made"), 1)
            mix(NH - 1)
            turn(NH)
            pe.wait_ge(sem("pt_ready"), NH + 1)
            pe.wait_ge(sem("cache_loaded"), 16 * (TS + 1))
            pe.wait_ge(sem("new_v_loaded"), 16)
            for b in range(TS):
                for g in range(NKV):
                    rows = slice(64 * (g % 2), 64 * (g % 2) + 64)
                    out = ps[rows, 6, 0:KC * TS].rearrange("p (c b) -> p c b", c=KC)
                    mm = t_.matmul(out[:, 4 * (g // 2):4 * (g // 2) + 4, b], VC[:, b, g * HD:(g + 1) * HD],
                                   PTT[:, 0, b * NH + g * R:b * NH + g * R + R], start=True, stop=True)
            mm.then_inc(sem("os_made"), 1)
            pe.wait_ge(sem("o_ready"), KC + 1)
            for n in range(O0, NDENSE):
                pair(dense(n), (OTH, OTL),
                     (sem("pt_ready"), NH + 1) if n < O0 + 2 else (sem("resid_o"), 2 * (n - O0 - 1)))
                if n > O0:
                    for c in range(2 * (n - O0) - 2, 2 * (n - O0)):
                        norm_part(3, c)
            for c in range(KC - 2, KC):
                norm_part(3, c)
            pe.wait_ge(sem("root_ready"), 4)
            pe.wait_ge(sem("router_loaded"), 16)
            for k in range(KC):
                pe.wait_ge(sem("xn_ready"), 3 * KC + k + 1)
                for t in range(3):
                    rows = tokens(t)
                    mm = t_.matmul(ps[0:rows, 3, t * E:(t + 1) * E], XN[:, k, t * P:t * P + rows], WR[:, k, :],
                                   start=(k == 0 and t == 0), stop=(k == KC - 1), skip_group_check=True)
            mm.then_inc(sem("logits_made"), 1)
            for t in range(3):
                rows = tokens(t)
                for hf in range(2):
                    for k in range(4):
                        mm = t_.transpose(ps[0:rows, HT_BANK[2 * t + hf], k * P:(k + 1) * P],
                                          XN[:, 4 * hf + k, t * P:t * P + rows], ident[:, :])
                    mm.then_inc(sem("h_turned"), 1)
            pe.wait_ge(sem("sel_ready"), 1)
            for t in range(3):
                rows = tokens(t)
                out = ps[0:rows, 4, t * E:(t + 1) * E]
                for u in range(t):
                    t_.matmul(out, ones[:, 0:rows], SELM[:, u, :], start=(u == 0), stop=False)
                t_.matmul(out, tri[0:rows, 0:rows], SELM[0:rows, t, :], start=(t == 0), stop=True)
            for t in range(3):
                rows = tokens(t)
                mm = t_.matmul(ps[0:1, 4, 3 * E:4 * E], ones[0:rows, 0:1], SELM[0:rows, t, :],
                               start=(t == 0), stop=(t == 2))
            mm.then_inc(sem("pos_made"), 1)
            pe.wait_ge(sem("hth_ready"), 6)

            def gather(n, banks=GATHER, lo_wait=None):
                spread = pe.snap(n * 3)
                pe.wait_ge(sem("dispatched"), spread)
                for part, bank, done in ((HTH, banks[0], sem("gathered_hi")), (HTL, banks[1], sem("gathered"))):
                    if part is HTL and lo_wait:
                        pe.wait_ge(*lo_wait)
                    for c in range(KC):
                        for t in range(3):
                            rows = tokens(t)
                            mm = t_.matmul(ps[:, bank + c // 4, (c % 4) * P:(c % 4 + 1) * P],
                                           part[0:rows, t, c * P:(c + 1) * P], DSP[0:rows, t, :],
                                           start=(t == 0), stop=(t == 2))
                    mm.then_inc(done, 1)

            def turn(r, j):
                pe.wait_ge(sem("act_ready"), pe.snap(r * JE + (j + 1)))
                if j >= 2:
                    pe.wait_ge(sem("af_split"), pe.snap(r * JE + (j - 1)))
                elif j == 0:
                    pe.wait_ge(sem("x_added"), pe.snap(r * 2 + 1))
                for i in range(4):
                    mm = t_.transpose(ps[:, 6 + j % 2, i * P:(i + 1) * P], AC[:, j % 2, i * P:(i + 1) * P],
                                      ident[:, :])
                mm.then_inc(sem("act_turned"), 1)

            def scatter(r, i):
                if i == 0:
                    pe.wait_ge(sem("ye_split"), pe.snap(r + 1))
                    pe.wait_ge(sem("gs_split"), pe.snap(r + 1))
                else:
                    pe.wait_ge(sem("x_added"), pe.snap(r * 2 + 2))
                for c in range(4 * i, 4 * i + 4):
                    mm = passes(ps[:, 4 + c % 4, 0:NT], [y[:, c * P:(c + 1) * P] for y in (YEH, YEL)],
                                (GSH[:, :], GSL[:, :]), True, True)
                mm.then_inc(sem("scattered"), 1)

            def product(tile, stat, bank, first, last):
                w = arrived(tile)
                for k in range(2):
                    for i in range(2):
                        cols = slice((2 * k + i) * 512, (2 * k + i + 1) * 512)
                        mm = passes(ps[:, bank + i, :], stat[k], [x[:, cols] for x in w],
                                    first and k == 0, last and k == 1)
                mm.then_inc(used, 1)

            def expert_gate_up(r, j, prev=None):
                if j >= 2:
                    pe.wait_ge(sem("act_ready"), pe.snap(r * JE + (j - 1)))
                elif j == 0:
                    pe.wait_ge(sem("xeh_ready"), pe.snap(r + 1))
                    pe.wait_ge(sem("xel_ready"), pe.snap(r + 1))
                for kq in range(4):
                    product(expert_tile(r, 4 * j + kq), [[x[:, 2 * kq + k, :] for x in (XEH, XEL)] for k in range(2)],
                            2 * (j % 2), kq == 0, kq == 3)
                    if kq == 1 and j:
                        turn(r, j - 1)
                    if prev is not None and kq % 2:
                        scatter(prev, kq // 2)

            def expert_rest(r, more):
                for j in range(1, JE):
                    expert_gate_up(r, j)
                for d in range(NDE):
                    if d % 2 == 0:
                        pe.wait_ge(sem("af_split"), pe.snap(r * JE + (d // 2 + 1)))
                    product(expert_tile(r, NGU + d), [[x[:, 2 * d + k, :] for x in (AFH, AFL)] for k in range(2)],
                            4, d == 0, d == NDE - 1)
                    if d == 1:
                        turn(r, JE - 1)
                    if d == 3:
                        pe.wait_ge(sem("af_split"), pe.snap(r * JE + (JE - 1)))
                        pe.wait_ge(sem("gate_spread"), pe.snap(r * 3 + 3))
                        for t in range(3):
                            rows = tokens(t)
                            mm = t_.transpose(ps[:, 7, t * P:t * P + rows], DG[0:rows, t, :], ident[0:rows, 0:rows])
                        mm.then_inc(sem("gate_turned"), 1)
                    if d == 6 and more:
                        gather(pe.snap(r + 2))
                if more:
                    expert_gate_up(pe.snap(r + 1), 0, r)
                else:
                    scatter(r, 0)
                    scatter(r, 1)

            zero = pe.snap(0)
            gather(pe.snap(zero + 1), GATHER0, (sem("ht_ready"), 6))
            expert_gate_up(zero, 0)
            with pe.Fori(0, E - 1) as e:
                expert_rest(e, True)
            expert_rest(pe.snap(zero + (E - 1)), False)
            pe.wait_ge(sem("plan_ready"), 1)
            any_more = pe.value_load(plan[0:1, 4 * E:4 * E + 1], min_val=E, max_val=E + 4)
            with pe.If(any_more > E):
                with pe.Fori(0, 2 * E) as i:
                    more = pe.value_load(plan[0:1, bass.ds(i, 1)], min_val=0, max_val=1)
                    with pe.If(more > 0):
                        r = pe.value_load(plan[0:1, bass.ds(i + 2 * E, 1)], min_val=E, max_val=E + 4)
                        gather(pe.snap(r + 1))
                        expert_gate_up(r, 0)
                        expert_rest(r, False)
            norm(4)
            pe.wait_ge(sem("root_ready"), 5)


def _tiles(w, pair):
    v = w.reshape(KC, P, -1)
    return [np.stack([v[:, :, a:a + P], v[:, :, b:b + P]], 2).transpose(1, 0, 2, 3).reshape(P, TILE)
            for a, b in pair]


def kernel(**inp):
    import concourse.bacc as bacc
    from concourse.bass_utils import run_bass_kernel_spmd

    a = {k: np.asarray(v) for k, v in inp.items()}
    c8 = lambda v: v.reshape(KC, P).T
    x = np.concatenate([a["x_prompt"].reshape(TP, D), a["x_sample"].reshape(TS, D)], 0)
    xT = x.T.reshape(KC, P, NT).transpose(1, 0, 2)
    vecs = np.stack([c8(v) for v in (a["g_mix"][0], a["g_mix"][1], a["g_ffn"][0], a["g_ffn"][1],
                                     a["g_kv"], a["g_final"], a["ssm_d"][0])], 1)
    cols = np.concatenate([np.arange(h * HD, (h + 1) * HD) for h in HEADS])
    wq, wo = a["w_q"][0][:, cols], a["w_o"][0][cols, :]
    wdn = a["w_ffn_down"][0].reshape(NF // 2, 2, P, D).transpose(0, 2, 1, 3).reshape(NF // 2, P, TILE)
    wkv = a["w_kv"]
    wv = wkv[:, 256:].reshape(KC, P, 256).transpose(1, 0, 2).reshape(P, TILE)
    wd = np.stack(
        _tiles(a["w_glu"][0], [(j * P, D + j * P) for j in range(KC)])
        + _tiles(a["w_ffn_gate_up"][0], [(j * P, DFF + j * P) for j in range(NF)])
        + list(wdn)
        + _tiles(wkv, [(0, P)]) + [wv]
        + _tiles(wq, [(2 * j * P, (2 * j + 1) * P) for j in range(4)])
        + _tiles(wo, [(2 * j * P, (2 * j + 1) * P) for j in range(4)]), 0)
    gu = a["w_exp_gate_up"][0].reshape(E, 4, 2, P, 2, JE, 512).transpose(0, 5, 1, 3, 2, 4, 6)
    dn = a["w_exp_down"][0].reshape(E, NDE, 2, P, D).transpose(0, 1, 3, 2, 4)
    we = np.concatenate([gu.reshape(E, NGU, P, TILE), dn.reshape(E, NDE, P, TILE)], 1).reshape(E * NE, P, TILE)
    wr = a["w_router"][0].reshape(KC, P, E).transpose(1, 0, 2)
    br, bi = (a[k][0].transpose(1, 0, 2) for k in ("ssm_b_re", "ssm_b_im"))
    cr, ci = (a[k][0].transpose(2, 0, 1) for k in ("ssm_c_re", "ssm_c_im"))
    hr, hi = (a[k][0].transpose(2, 1, 0) for k in ("state_ssm_re", "state_ssm_im"))
    dist = 255 - np.arange(384)
    large = 16 + (np.log(np.maximum(dist, 1).astype(np.float32) / 16) / math.log(8) * 16).astype(np.int32)
    bucket = np.where(dist < 16, dist, np.minimum(large, NBUCK - 1))
    bucket = np.where((dist >= 0) & (dist < W), bucket, NBUCK)
    onehot = (np.arange(NBUCK + 1)[:, None] == bucket[None]).astype(np.float32)
    ins = {
        "xT": xT, "vecs": vecs, "wd": wd, "we": we, "wr": wr,
        "a_re": a["ssm_a_re"][0].T, "a_im": a["ssm_a_im"][0].T, "log_dt": a["ssm_log_dt"],
        "bq": np.concatenate([br, bi], 0), "bx": np.concatenate([bi, br], 0),
        "cq": np.concatenate([cr, ci], 0), "cx": np.concatenate([ci, cr], 0),
        "h0q": np.concatenate([hr, hi], 0), "h0x": np.concatenate([hi, hr], 0),
        "kcT": a["cache_k_win"].reshape(TS, W, 2, P).transpose(0, 3, 2, 1),
        "vc": a["cache_v_win"].reshape(TS, W, 256).transpose(1, 0, 2),
        "sinks": a["attn_sinks"], "relb": a["rel_bias"], "onehot": onehot,
    }
    outs = {"yT": (P, KC, NT), "hp": (P, G), "hs": (P, G, TS), "kp": (P, 2, W), "vp": (P, 256),
            "ks": (P, TS, 2, W), "vs": (P, TS, 256)}
    nc = bacc.Bacc("TRN2", target_bir_lowering=False, num_devices=1)
    arrays, args = {}, []
    for name, v in ins.items():
        arrays["in_" + name] = np.ascontiguousarray(v)
        args.append(nc.dram_tensor("in_" + name, v.shape, F32, kind="ExternalInput").ap())
    for name, shape in outs.items():
        args.append(nc.dram_tensor("out_" + name, shape, F32, kind="ExternalOutput").ap())
    build(nc, *args)
    o = run_bass_kernel_spmd(nc, [arrays], core_ids=[0]).results[0]
    y = o["out_yT"].transpose(1, 0, 2).reshape(D, NT).T
    hp, hs = o["out_hp"], o["out_hs"]
    st = lambda v: v.transpose(2, 1, 0)[None]
    return (y[:TP].reshape(1, TP, D), y[TP:].reshape(TS, 1, D),
            hp[:S].T.reshape(1, 1, G, S), hp[S:].T.reshape(1, 1, G, S),
            o["out_kp"].transpose(2, 1, 0).reshape(1, W, NKV, HD), o["out_vp"].reshape(1, W, NKV, HD),
            st(hs[:S]), st(hs[S:]),
            o["out_ks"].transpose(1, 3, 2, 0).reshape(TS, W, NKV, HD),
            o["out_vs"].transpose(1, 0, 2).reshape(TS, W, NKV, HD))
```
